# Optimizing a Trainium2 kernel written in Bass

```python
import jax, jax.numpy as jnp
from jax import lax
import numpy as np

D_MODEL = 1024
BATCH = 1
SEQ = 512
DEPTH = 1

GRID_W = 64
CTX_LEN = 256
RET_HEADS = 8
RET_QK_DIM = 64
RET_V_DIM = 128
RET_QK_WIDTH = RET_HEADS * RET_QK_DIM
RET_V_WIDTH = RET_HEADS * RET_V_DIM
CHUNK = 128
ROPE_BASE = 10000.0
FOURIER_GROUPS = 4
FOURIER_GROUP_DIM = 128
FOURIER_WIDTH = FOURIER_GROUPS * FOURIER_GROUP_DIM
Q_OFF = 0
K_OFF = Q_OFF + RET_QK_WIDTH
V_OFF = K_OFF + RET_QK_WIDTH
G_OFF = V_OFF + RET_V_WIDTH
F_OFF = G_OFF + RET_V_WIDTH
IN_COLS = F_OFF + FOURIER_WIDTH
N_BRANCHES = 2
FFN_DIM = 2816
CONV_W = 3
N_MOD = 6
EPS = 1e-6


def rms_norm(x, w):
    x32 = x.astype(jnp.float32)
    y = x32 * lax.rsqrt(jnp.mean(x32 * x32, axis=-1, keepdims=True) + EPS)
    return (y * w.astype(jnp.float32)).astype(x.dtype)

def modulate(h, shift, scale):
    return h * (1 + scale) + shift

def split_heads(t, n_heads):
    b, l, w = t.shape
    return t.reshape(b, l, n_heads, w // n_heads).transpose(0, 2, 1, 3)

def rope_2d(t, row, col):
    n_freq = RET_QK_DIM // 4
    inv = ROPE_BASE ** (-jnp.arange(n_freq, dtype=jnp.float32) / n_freq)
    ang = jnp.concatenate([row[:, None] * inv, col[:, None] * inv], axis=-1)
    cos, sin = jnp.cos(ang), jnp.sin(ang)
    half = RET_QK_DIM // 2
    t1, t2 = t[..., :half], t[..., half:]
    return jnp.concatenate([t1 * cos - t2 * sin, t1 * sin + t2 * cos], axis=-1).astype(t.dtype)

def log_gamma(a):
    return -jnp.exp(a.astype(jnp.float32))

def chunk_retention(q, k, v, a, s0):
    b, h, l, dk = q.shape
    dv = v.shape[-1]
    n = l // CHUNK
    lg = log_gamma(a)
    qc = q.reshape(b, h, n, CHUNK, dk)
    kc = k.reshape(b, h, n, CHUNK, dk)
    vc = v.reshape(b, h, n, CHUNK, dv)
    pos = jnp.arange(CHUNK, dtype=jnp.float32)
    diff = pos[:, None] - pos[None, :]
    intra_decay = jnp.where(diff >= 0, jnp.exp(lg[:, None, None] * jnp.maximum(diff, 0.0)), 0.0)
    scores = jnp.einsum('bhncd,bhnsd->bhncs', qc, kc) * intra_decay[None, :, None]
    intra = jnp.einsum('bhncs,bhnse->bhnce', scores, vc)
    k_dec = kc * jnp.exp(lg[:, None] * (CHUNK - 1 - pos))[None, :, None, :, None]
    kv = jnp.einsum('bhnsd,bhnse->nbhde', k_dec, vc)
    chunk_decay = jnp.exp(lg * CHUNK)[None, :, None, None]

    def step(s, kv_n):
        return chunk_decay * s + kv_n, s

    s_final, s_prev = lax.scan(step, s0.astype(jnp.float32), kv)
    q_dec = qc * jnp.exp(lg[:, None] * (pos + 1))[None, :, None, :, None]
    inter = jnp.einsum('bhncd,nbhde->bhnce', q_dec, s_prev)
    return (intra + inter).reshape(b, h, l, dv), s_final

def retention_state(k, v, a):
    l = k.shape[2]
    lg = log_gamma(a)
    w = jnp.exp(lg[:, None] * (l - 1 - jnp.arange(l, dtype=jnp.float32)))
    return jnp.einsum('bhld,bhle,hl->bhde', k, v, w)

def bidir_retention(q, k, v, a_f, a_b, s_f0, s_b0):
    o_f, s_f = chunk_retention(q, k, v, a_f, s_f0)
    o_b, s_b = chunk_retention(jnp.flip(q, 2), jnp.flip(k, 2), jnp.flip(v, 2), a_b, s_b0)
    return o_f + jnp.flip(o_b, 2), s_f, s_b

def ret_readout(o, g, w_o):
    mu = jnp.mean(o, axis=-1, keepdims=True)
    var = jnp.mean(jnp.square(o - mu), axis=-1, keepdims=True)
    o = (o - mu) * lax.rsqrt(var + EPS)
    b, h, l, dv = o.shape
    o = o.transpose(0, 2, 1, 3).reshape(b, l, h * dv).astype(g.dtype)
    return (o * jax.nn.silu(g)) @ w_o

def fourier_mix(f, w_f):
    b, l, _ = f.shape
    fg = f.reshape(b, l, FOURIER_GROUPS, FOURIER_GROUP_DIM).astype(jnp.float32)
    z = jnp.fft.fft2(fg, axes=(1, 3), norm='ortho').real
    return z.reshape(b, l, FOURIER_WIDTH).astype(f.dtype) @ w_f

def merge_branches(h, ret_d, four_d, w_bg, b_bg, w_out):
    gates = jax.nn.sigmoid(h @ w_bg + b_bg)
    g_r, g_f = jnp.split(gates, N_BRANCHES, axis=-1)
    return (g_r * ret_d + g_f * four_d) @ w_out

def depthwise_conv3(u, w, b):
    up = jnp.pad(u, ((0, 0), (1, 1), (0, 0)))
    return up[:, :-2] * w[0] + up[:, 1:-1] * w[1] + up[:, 2:] * w[2] + b

def conv_ffn(h, w_up, conv_w, conv_b, w_down):
    u = depthwise_conv3(h @ w_up, conv_w, conv_b)
    a, val = jnp.split(u, 2, axis=-1)
    return (jax.nn.gelu(a) * val) @ w_down

def split_proj(p):
    return (p[..., Q_OFF:K_OFF], p[..., K_OFF:V_OFF], p[..., V_OFF:G_OFF],
            p[..., G_OFF:F_OFF], p[..., F_OFF:IN_COLS])

def first_inputs(seed: int = 0) -> dict:
    key = jax.random.key(seed)
    ks = jax.random.split(key, 24)

    def nrm(k, shape, scale):
        return jax.random.normal(k, shape, jnp.float32) * scale

    d = D_MODEL
    base_decay = jnp.log(-jnp.log1p(-(2.0 ** (-5.0 - jnp.arange(RET_HEADS, dtype=jnp.float32)))))
    return {
        "x": nrm(ks[0], (BATCH, SEQ, d), 1.0),
        "c": nrm(ks[1], (BATCH, d), 1.0),
        "ctx": nrm(ks[2], (BATCH, CTX_LEN, d), 1.0),
        "c_ctx": nrm(ks[3], (d,), 1.0),
        "w_mod": nrm(ks[4], (DEPTH, d, N_MOD * d), 0.5 * d ** -0.5),
        "b_mod": nrm(ks[5], (DEPTH, N_MOD * d), 0.01),
        "norm1_w": 1.0 + nrm(ks[6], (DEPTH, d), 0.05),
        "w_in": nrm(ks[7], (DEPTH, d, IN_COLS), d ** -0.5),
        "ret_decay_f": base_decay[None] + nrm(ks[8], (DEPTH, RET_HEADS), 0.1),
        "ret_decay_b": base_decay[None] + nrm(ks[9], (DEPTH, RET_HEADS), 0.1),
        "w_ret_out": nrm(ks[10], (DEPTH, RET_V_WIDTH, d), RET_V_WIDTH ** -0.5),
        "w_four_out": nrm(ks[11], (DEPTH, FOURIER_WIDTH, d), FOURIER_WIDTH ** -0.5),
        "w_branch_gate": nrm(ks[12], (DEPTH, d, N_BRANCHES * d), d ** -0.5),
        "b_branch_gate": nrm(ks[13], (DEPTH, N_BRANCHES * d), 0.01),
        "w_out": nrm(ks[14], (DEPTH, d, d), d ** -0.5),
        "norm2_w": 1.0 + nrm(ks[15], (DEPTH, d), 0.05),
        "w_up": nrm(ks[16], (DEPTH, d, 2 * FFN_DIM), d ** -0.5),
        "conv_w": nrm(ks[17], (DEPTH, CONV_W, 2 * FFN_DIM), CONV_W ** -0.5),
        "conv_b": nrm(ks[18], (DEPTH, 2 * FFN_DIM), 0.01),
        "w_down": nrm(ks[19], (DEPTH, FFN_DIM, d), FFN_DIM ** -0.5),
        "final_norm_w": 1.0 + nrm(ks[20], (d,), 0.05),
    }

def first_block(x, c, ctx, c_ctx, w_mod, b_mod, norm1_w, w_in, ret_decay_f, ret_decay_b,
              w_ret_out, w_four_out, w_branch_gate, b_branch_gate, w_out, norm2_w,
              w_up, conv_w, conv_b, w_down, final_norm_w):
    b, l, _ = x.shape
    rows = l // GRID_W
    row = jnp.repeat(jnp.arange(rows, dtype=jnp.float32), GRID_W)
    col = jnp.tile(jnp.arange(GRID_W, dtype=jnp.float32), rows)
    q_scale = RET_QK_DIM ** -0.5
    silu_c = jax.nn.silu(c)
    silu_cc = jax.nn.silu(c_ctx)
    xc = ctx
    for layer in range(DEPTH):
        last = layer == DEPTH - 1
        wi = w_in[layer]
        a_f, a_b = ret_decay_f[layer], ret_decay_b[layer]
        mod = silu_c @ w_mod[layer] + b_mod[layer]
        sh1, sc1, g1, sh2, sc2, g2 = [m[:, None, :] for m in jnp.split(mod, N_MOD, axis=-1)]
        mc = jnp.split(silu_cc @ w_mod[layer] + b_mod[layer], N_MOD)

        h = modulate(rms_norm(x, norm1_w[layer]), sh1, sc1)
        hc = modulate(rms_norm(xc, norm1_w[layer]), mc[0], mc[1])

        if last:
            kc = split_heads(hc @ wi[:, K_OFF:V_OFF], RET_HEADS)
            vc = split_heads(hc @ wi[:, V_OFF:G_OFF], RET_HEADS)
            s_f = retention_state(kc, vc, a_f)
            s_b = retention_state(jnp.flip(kc, 2), jnp.flip(vc, 2), a_b)
        else:
            qc, kc, vc, gc, fc = split_proj(hc @ wi)
            qc = split_heads(qc, RET_HEADS) * q_scale
            kc = split_heads(kc, RET_HEADS)
            vc = split_heads(vc, RET_HEADS)
            zeros = jnp.zeros((b, RET_HEADS, RET_QK_DIM, RET_V_DIM), jnp.float32)
            oc, s_f, s_b = bidir_retention(qc, kc, vc, a_f, a_b, zeros, zeros)
            yc = merge_branches(hc, ret_readout(oc, gc, w_ret_out[layer]),
                                fourier_mix(fc, w_four_out[layer]),
                                w_branch_gate[layer], b_branch_gate[layer], w_out[layer])
            xc = xc + mc[2] * yc
            hc2 = modulate(rms_norm(xc, norm2_w[layer]), mc[3], mc[4])
            xc = xc + mc[5] * conv_ffn(hc2, w_up[layer], conv_w[layer], conv_b[layer], w_down[layer])

        q, k, v, g, f = split_proj(h @ wi)
        q = rope_2d(split_heads(q, RET_HEADS), row, col) * q_scale
        k = rope_2d(split_heads(k, RET_HEADS), row, col)
        v = split_heads(v, RET_HEADS)
        o, _, _ = bidir_retention(q, k, v, a_f, a_b, s_f, s_b)
        y = merge_branches(h, ret_readout(o, g, w_ret_out[layer]),
                           fourier_mix(f, w_four_out[layer]),
                           w_branch_gate[layer], b_branch_gate[layer], w_out[layer])
        x = x + g1 * y
        h2 = modulate(rms_norm(x, norm2_w[layer]), sh2, sc2)
        x = x + g2 * conv_ffn(h2, w_up[layer], conv_w[layer], conv_b[layer], w_down[layer])
    return rms_norm(x, final_norm_w)


A_GROUPS = 8
A_WIDTH = 1024
A_GROUP_DIM = A_WIDTH // A_GROUPS
N_HEADS = 16
N_KV_HEADS = 4
HEAD_DIM = 64
B_WIDTH = N_HEADS * HEAD_DIM
KV_WIDTH = N_KV_HEADS * HEAD_DIM
WINDOW = 128
BLOCK = 128
N_EXPERTS = 16
CAPACITY_FACTOR = 2
D_EXPERT = 2048
OFF_U = 0
OFF_VA = OFF_U + A_WIDTH
OFF_Q = OFF_VA + A_WIDTH
OFF_K = OFF_Q + B_WIDTH
OFF_VB = OFF_K + KV_WIDTH
OFF_GATE = OFF_VB + KV_WIDTH
IN_COLS_2 = OFF_GATE + 2 * D_MODEL


def rmsnorm(x, g):
    xf = x.astype(jnp.float32)
    y = xf * lax.rsqrt(jnp.mean(xf * xf, axis=-1, keepdims=True) + EPS)
    return (y * g.astype(jnp.float32)).astype(x.dtype)

def layernorm(x, g, b):
    xf = x.astype(jnp.float32)
    mu = jnp.mean(xf, axis=-1, keepdims=True)
    var = jnp.mean(jnp.square(xf - mu), axis=-1, keepdims=True)
    y = (xf - mu) * lax.rsqrt(var + EPS)
    return (y * g.astype(jnp.float32) + b.astype(jnp.float32)).astype(x.dtype)

def modulate_2(h, shift, scale):
    return h * (1 + scale) + shift

def _axis_angles(pos, dim):
    freqs = ROPE_BASE ** (-jnp.arange(0, dim, 2, dtype=jnp.float32) / dim)
    return pos.astype(jnp.float32)[:, None] * freqs[None, :]

def _rotate(x, ang):
    x1, x2 = jnp.split(x.astype(jnp.float32), 2, axis=-1)
    cos = jnp.cos(ang)[None, :, None, :]
    sin = jnp.sin(ang)[None, :, None, :]
    return jnp.concatenate([x1 * cos - x2 * sin, x1 * sin + x2 * cos], axis=-1)

def rope_2d_2(x, row, col):
    half = x.shape[-1] // 2
    xr, xc = x[..., :half], x[..., half:]
    out = jnp.concatenate([_rotate(xr, _axis_angles(row, half)),
                           _rotate(xc, _axis_angles(col, half))], axis=-1)
    return out.astype(x.dtype)

def chunk_gmlp(u, v, ln_g, ln_b, w_s, b_s):
    Bn, L, _ = v.shape
    v = layernorm(v, ln_g, ln_b)
    vc = v.reshape(Bn, L // CHUNK, CHUNK, A_GROUPS, A_GROUP_DIM)
    mixed = jnp.einsum('gpq,bnqgd->bnpgd', w_s, vc) + b_s.T[None, None, :, :, None]
    return u * mixed.reshape(Bn, L, A_WIDTH)

def window_gqa(q, k, v, k_ctx, v_ctx, sink):
    Bn, L, H, Dh = q.shape
    nb = L // BLOCK
    rep = H // N_KV_HEADS
    scale = HEAD_DIM ** -0.5
    qb = q.reshape(Bn, nb, BLOCK, N_KV_HEADS, rep, Dh)

    def band(t):
        tb = t.reshape(Bn, nb, BLOCK, N_KV_HEADS, Dh)
        tp = jnp.pad(tb, ((0, 0), (1, 1), (0, 0), (0, 0), (0, 0)))
        return jnp.concatenate([tp[:, :-2], tp[:, 1:-1], tp[:, 2:]], axis=2)

    kb, vb = band(k), band(v)
    a_idx = jnp.arange(BLOCK)[:, None]
    s_idx = jnp.arange(3 * BLOCK)[None, :]
    rel = s_idx - BLOCK - a_idx
    sink_l = sink.astype(jnp.float32).reshape(N_KV_HEADS, rep)[None, :, :, None, None]
    vals_ctx = v_ctx.astype(jnp.float32)

    def one_block(args):
        n, qn, kn, vn = args
        key_pos = (n - 1) * BLOCK + s_idx
        mask = (jnp.abs(rel) <= WINDOW) & (key_pos >= 0) & (key_pos < L)
        s_loc = jnp.einsum('bqkrd,bskd->bkrqs', qn, kn, preferred_element_type=jnp.float32) * scale
        s_loc = jnp.where(mask, s_loc, jnp.float32(-1e30))
        s_ctx = jnp.einsum('bqkrd,bskd->bkrqs', qn, k_ctx, preferred_element_type=jnp.float32) * scale
        logits = jnp.concatenate([s_loc, s_ctx], axis=-1)
        m = jnp.maximum(jnp.max(logits, axis=-1, keepdims=True), sink_l)
        p = jnp.exp(logits - m)
        denom = jnp.sum(p, axis=-1, keepdims=True) + jnp.exp(sink_l - m)
        vals = jnp.concatenate([vn.astype(jnp.float32), vals_ctx], axis=1)
        out = jnp.einsum('bkrqs,bskd->bqkrd', p / denom, vals)
        return out.astype(q.dtype)

    xs = (jnp.arange(nb), jnp.moveaxis(qb, 1, 0), jnp.moveaxis(kb, 1, 0), jnp.moveaxis(vb, 1, 0))
    out = lax.map(one_block, xs)
    return jnp.moveaxis(out, 0, 1).reshape(Bn, L, H * Dh)

def expert_choice_ffn(h, w_router, w_gate, w_up, w_down):
    Bn, N, D = h.shape
    cap = max(1, CAPACITY_FACTOR * N // N_EXPERTS)
    logits = jnp.einsum('bnd,de->bne', h, w_router, preferred_element_type=jnp.float32)
    aff = jax.nn.softmax(logits, axis=-1)
    top_w, top_idx = lax.top_k(jnp.swapaxes(aff, 1, 2), cap)
    xe = jax.vmap(lambda hb, ib: hb[ib])(h, top_idx)
    g = jnp.einsum('becd,edf->becf', xe, w_gate)
    u = jnp.einsum('becd,edf->becf', xe, w_up)
    y = jnp.einsum('becf,efd->becd', jax.nn.silu(g) * u, w_down)
    y = y * top_w[..., None].astype(y.dtype)
    return jax.vmap(lambda ib, yb: jnp.zeros((N, D), yb.dtype).at[ib.reshape(-1)].add(yb.reshape(-1, D)))(top_idx, y)

def second_inputs(seed: int = 0) -> dict:
    key = jax.random.key(seed)
    ks = jax.random.split(key, 24)
    f32 = jnp.float32
    D = D_MODEL

    def nrm(k, shape, s):
        return jax.random.normal(k, shape, f32) * s

    return {
        "x": nrm(ks[0], (BATCH, SEQ, D), 1.0),
        "c": nrm(ks[1], (BATCH, D), 1.0),
        "ctx": nrm(ks[2], (BATCH, CTX_LEN, D), 1.0),
        "c_ctx": nrm(ks[3], (D,), 1.0),
        "w_ada": nrm(ks[4], (DEPTH, D, 6 * D), 0.3 * D ** -0.5),
        "b_ada": nrm(ks[5], (DEPTH, 6 * D), 0.02),
        "norm1_g": 1.0 + nrm(ks[6], (DEPTH, D), 0.05),
        "w_in": nrm(ks[7], (DEPTH, D, IN_COLS_2), D ** -0.5),
        "b_merge_gate": nrm(ks[8], (DEPTH, 2 * D), 0.02),
        "gmlp_ln_g": 1.0 + nrm(ks[9], (DEPTH, A_WIDTH), 0.05),
        "gmlp_ln_b": nrm(ks[10], (DEPTH, A_WIDTH), 0.02),
        "w_spatial": nrm(ks[11], (DEPTH, A_GROUPS, CHUNK, CHUNK), CHUNK ** -0.5),
        "b_spatial": nrm(ks[12], (DEPTH, A_GROUPS, CHUNK), 0.02),
        "attn_sink": nrm(ks[13], (DEPTH, N_HEADS), 0.5),
        "w_proj_a": nrm(ks[14], (DEPTH, A_WIDTH, D), A_WIDTH ** -0.5),
        "w_proj_b": nrm(ks[15], (DEPTH, B_WIDTH, D), B_WIDTH ** -0.5),
        "w_out": nrm(ks[16], (DEPTH, D, D), D ** -0.5),
        "norm2_g": 1.0 + nrm(ks[17], (DEPTH, D), 0.05),
        "w_router": nrm(ks[18], (DEPTH, D, N_EXPERTS), D ** -0.5),
        "w_exp_gate": nrm(ks[19], (DEPTH, N_EXPERTS, D, D_EXPERT), D ** -0.5),
        "w_exp_up": nrm(ks[20], (DEPTH, N_EXPERTS, D, D_EXPERT), D ** -0.5),
        "w_exp_down": nrm(ks[21], (DEPTH, N_EXPERTS, D_EXPERT, D), D_EXPERT ** -0.5),
        "final_g": 1.0 + nrm(ks[22], (D,), 0.05),
    }

def second_block(x, c, ctx, c_ctx, w_ada, b_ada, norm1_g, w_in, b_merge_gate, gmlp_ln_g, gmlp_ln_b,
              w_spatial, b_spatial, attn_sink, w_proj_a, w_proj_b, w_out, norm2_g, w_router,
              w_exp_gate, w_exp_up, w_exp_down, final_g):
    Bn, L, D = x.shape
    rows = L // GRID_W
    row = jnp.repeat(jnp.arange(rows), GRID_W)
    col = jnp.tile(jnp.arange(GRID_W), rows)

    for l in range(DEPTH):
        mod = jax.nn.silu(c) @ w_ada[l] + b_ada[l]
        sh1, sc1, g1, sh2, sc2, g2 = jnp.split(mod[:, None, :], 6, axis=-1)
        mod_ctx = jax.nn.silu(c_ctx) @ w_ada[l] + b_ada[l]
        csh1, csc1 = mod_ctx[:D], mod_ctx[D:2 * D]

        h = modulate_2(rmsnorm(x, norm1_g[l]), sh1, sc1)
        proj = h @ w_in[l]
        u_a, v_a, q, k, v, gates = jnp.split(proj, [OFF_VA, OFF_Q, OFF_K, OFF_VB, OFF_GATE], axis=-1)

        hc = modulate_2(rmsnorm(ctx, norm1_g[l]), csh1, csc1)
        kv_ctx = hc @ w_in[l][:, OFF_K:OFF_GATE]
        k_ctx, v_ctx = jnp.split(kv_ctx.reshape(Bn, -1, 2 * N_KV_HEADS, HEAD_DIM), 2, axis=2)

        y_a = chunk_gmlp(jax.nn.gelu(u_a), jax.nn.gelu(v_a), gmlp_ln_g[l], gmlp_ln_b[l],
                         w_spatial[l], b_spatial[l])

        qh = rope_2d_2(q.reshape(Bn, L, N_HEADS, HEAD_DIM), row, col)
        kh = rope_2d_2(k.reshape(Bn, L, N_KV_HEADS, HEAD_DIM), row, col)
        vh = v.reshape(Bn, L, N_KV_HEADS, HEAD_DIM)
        y_b = window_gqa(qh, kh, vh, k_ctx, v_ctx, attn_sink[l])

        g_a, g_b = jnp.split(jax.nn.sigmoid(gates + b_merge_gate[l]), 2, axis=-1)
        merged = g_a * (y_a @ w_proj_a[l]) + g_b * (y_b @ w_proj_b[l])
        x = x + g1 * (merged @ w_out[l])

        h2 = modulate_2(rmsnorm(x, norm2_g[l]), sh2, sc2)
        x = x + g2 * expert_choice_ffn(h2, w_router[l], w_exp_gate[l], w_exp_up[l], w_exp_down[l])

    return rmsnorm(x, final_g)


def setup_inputs(seed=0):
    out = dict(first_inputs(seed))
    for name, value in second_inputs(seed + 1).items():
        if name != "x":
            out[name + "_2"] = value
    return out


def reference(
    x, c, ctx, c_ctx, w_mod, b_mod, norm1_w, w_in, ret_decay_f, ret_decay_b, w_ret_out,
    w_four_out, w_branch_gate, b_branch_gate, w_out, norm2_w, w_up, conv_w, conv_b, w_down,
    final_norm_w, c_2, ctx_2, c_ctx_2, w_ada_2, b_ada_2, norm1_g_2, w_in_2, b_merge_gate_2,
    gmlp_ln_g_2, gmlp_ln_b_2, w_spatial_2, b_spatial_2, attn_sink_2, w_proj_a_2, w_proj_b_2,
    w_out_2, norm2_g_2, w_router_2, w_exp_gate_2, w_exp_up_2, w_exp_down_2, final_g_2,
):
    x = first_block(
        x, c, ctx, c_ctx, w_mod, b_mod, norm1_w, w_in, ret_decay_f, ret_decay_b, w_ret_out,
        w_four_out, w_branch_gate, b_branch_gate, w_out, norm2_w, w_up, conv_w, conv_b, w_down,
        final_norm_w,
    )
    return second_block(
        x, c_2, ctx_2, c_ctx_2, w_ada_2, b_ada_2, norm1_g_2, w_in_2, b_merge_gate_2,
        gmlp_ln_g_2, gmlp_ln_b_2, w_spatial_2, b_spatial_2, attn_sink_2, w_proj_a_2, w_proj_b_2,
        w_out_2, norm2_g_2, w_router_2, w_exp_gate_2, w_exp_up_2, w_exp_down_2, final_g_2,
    )


_drawn_inputs = setup_inputs


def setup_inputs(seed=0):
    import zlib

    import numpy as np

    out = dict(_drawn_inputs(seed))
    spreads = {}
    factors = {'b_mod': 4.787,
     'norm1_w': 4.223,
     'b_branch_gate': 8.0,
     'norm2_w': 3.28,
     'conv_b': 8.0,
     'ctx_2': 8.0,
     'c_ctx_2': 6.144,
     'b_ada_2': 5.752,
     'norm1_g_2': 8.0,
     'b_merge_gate_2': 8.0,
     'gmlp_ln_g_2': 8.0,
     'gmlp_ln_b_2': 8.0,
     'b_spatial_2': 8.0,
     'attn_sink_2': 8.0,
     'w_proj_b_2': 3.289,
     'norm2_g_2': 8.0}
    for name, (base, spread) in spreads.items():
        noise = np.random.default_rng([zlib.crc32(name.encode()), seed]).standard_normal(out[name].shape)
        drawn = base * np.exp(spread * noise) if base else spread * noise
        out[name] = __import__('jax').numpy.asarray(drawn.astype(out[name].dtype))
    for name, factor in factors.items():
        out[name] = (out[name] * factor).astype(out[name].dtype)
    return out
```

```python
from contextlib import ExitStack

import numpy as np

import concourse.bass as bass
from concourse import mybir

F32 = mybir.dt.float32
ALU = mybir.AluOpType
ACT = mybir.ActivationFunctionType
AX = mybir.AxisListType

P = 128
D = 1024
KT = D // P
L = 512
TT = L // P
LC = 256
CT = LC // P
SLOTS = 6
SLOT = 4096
EPS = 1e-6

H1, DK, DV = 8, 64, 128
FFN = 2816
FT = FFN // P
UPN = FFN // 256
FG = 4

NH, NKV, HD = 16, 4, 64
NG = 8
NE, DE, CAP = 16, 2048, 64
PAIRS = NE // 2
FQ = DE // 512
PAIR_CHUNKS = 6 * FQ

V1 = dict(c=0, c_ctx=8, norm1=16, norm2=24, final=32, b_gate=40, b_mod=56)
V2 = dict(w0=0, w1=44)
V3 = dict(w2=0, b=44)
V4 = V1

CONST = {}
_n = 0
for _name, _w in (("ident", 128), ("swap1", 128), ("swap2", 128), ("mask", 256), ("iota", 64),
                  ("age", 4), ("modsel", 2)):
    CONST[_name] = (_n, _n + _w)
    _n += _w
NCONST = _n


class Banks:

    def __init__(self):
        self.tiles, self.where, self.units = [], {}, []

    def add(self, name, by, width=1):
        if width == 2 and len(self.units) % 2:
            self.units.append(None)
        i = len(self.tiles)
        assert name not in self.where, name
        nth = sum(1 for t in self.tiles if t[1] == by) + 1
        self.tiles.append((name, by, len(self.units), nth, width))
        self.where[name] = i
        self.units += [i] * width

    def bank(self, name):
        return self.tiles[self.where[name]][2] % 8

    def before(self, name):
        _, _, u, _, w = self.tiles[self.where[name]]
        need = {}
        for v in range(u, u + w):
            for back in range(v - 8, -1, -8):
                if self.units[back] is not None:
                    _, by, _, nth, _ = self.tiles[self.units[back]]
                    need[by] = max(need.get(by, 0), nth)
                    break
        return sorted(need.items())


def plan_banks():
    b = Banks()
    b.add("vecs", "D")
    for k in range(KT):
        b.add(("xT", k), "AD"[k % 2])
    for k in range(KT // 2):
        b.add(("cT", k), "AD"[k % 2])

    def mods(tag):
        for c in range(12):
            b.add((tag, c), "A")
            if c:
                b.add((tag, "T", c - 1), "D")
        b.add((tag, "T", 11), "D")

    def merge(tag):
        for nq in range(2):
            for part in "ab":
                for n in range(4):
                    b.add((tag, "gate", part, nq, n), "A")
                for n in range(4):
                    b.add((tag, "proj", part, nq, n), "D")

    def rope(tag, n):
        for i in range(n + 1):
            if i < n:
                b.add((tag, i), "A")
            if i:
                b.add((tag, "swap", i - 1), "D")

    mods("mod1")
    b.add("n1", "A")
    b.add("nc", "A")
    rope("qk1", 4)
    for t in range(CT):
        b.add(("kc", t), "A")
    for i in range(5):
        if i < 4:
            b.add(("qk1", 4 + i), "A")
        if i:
            b.add(("qk1", "swap", 3 + i), "D")
    for hh in range(2):
        for t in range(CT):
            b.add(("vc", hh, t), "D")
        for t in range(TT):
            b.add(("v", hh, t), "D")
    b.add("S", "D", 2)
    for h in range(H1 + 1):
        if h:
            b.add(("o", h - 1), "A")
        if h < H1:
            for i in range(TT):
                b.add(("s", h, i), "D")
        if h:
            b.add(("var", h - 1), "A")
    for n in range(KT):
        b.add(("g", n), "A")
    for t in range(TT):
        b.add(("f", t), "A")
    for g in range(FG):
        for m in range(2):
            b.add(("fa", g, m), "A")
    for g in range(FG):
        b.add(("z", g), "D")
    merge("m1")
    for n in range(KT):
        b.add(("out1", n), "D")
    b.add("n2", "A")
    for j in range(UPN):
        for n in range(4):
            b.add(("up", j, n), "D")
    for n in range(KT):
        b.add(("down", n), "D")
    for k in range(KT // 2):
        b.add(("cT2", k), "AD"[k % 2])
    b.add("nf1", "A")
    mods("mod2")
    b.add("n3", "A")
    b.add("nc2", "A")
    for n in range(KT):
        b.add(("u", n), "A")
    for hh in range(2):
        for t in range(TT):
            b.add(("va", hh, t), "A")
    b.add(("ws", 0), "A")
    b.add(("ws", 1), "A")
    for g in range(NG):
        b.add(("mix", g), "D")
    rope("q2", 8)
    for i in range(3):
        if i < 2:
            b.add(("k2", i), "A")
        if i:
            b.add(("k2", "swap", i - 1), "D")
    for t in range(TT):
        b.add(("vb", t), "A")
    for i in range(2):
        b.add(("kc2", i), "D")
    for t in range(CT):
        b.add(("vc2", t), "A")
    for i in range(NH * TT + 1):
        if i < NH * TT:
            b.add(("as", i), "A", 2)
        if i and i % 4 == 1 and i > 1:
            b.add(("pv", i // 4 - 1), "D")
        if i:
            b.add(("at", i - 1), "A", 2)
    b.add(("pv", NH * TT // 4 - 1), "D")
    merge("m2")
    for n in range(KT):
        b.add(("out2", n), "D")
    b.add("n4", "A")
    for t in range(TT):
        for hh in range(2):
            b.add(("ht", t, hh), "AD"[hh])
    b.add("router", "D")
    b.add("affT", "D")
    b.add("slotT", "D")
    for q in range(PAIRS):
        b.add(("wt", q), "AD"[q % 2])
    b.add("nf2", "A")
    for t in range(TT):
        for hh in range(2):
            b.add(("ot", t, hh), "AD"[hh])
    return b


def build_two_blocks(nc, x, c, ctx, c_ctx, w_mod, b_mod, norm1_w, w_in, ret_decay_f, ret_decay_b,
                     w_ret_out, w_four_out, w_branch_gate, b_branch_gate, w_out, norm2_w, w_up,
                     conv_w, conv_b, w_down, final_norm_w, c_2, ctx_2, c_ctx_2, w_ada_2, b_ada_2,
                     norm1_g_2, w_in_2, b_merge_gate_2, gmlp_ln_g_2, gmlp_ln_b_2, w_spatial_2,
                     b_spatial_2, attn_sink_2, w_proj_a_2, w_proj_b_2, w_out_2, norm2_g_2,
                     w_router_2, w_exp_gate_2, w_exp_up_2, w_exp_down_2, final_g_2,
                     consts, rope1, rope2, dft_len, dft_dim, dist, out):
    banks = plan_banks()
    es = ExitStack()
    with es:
        def sb(name, *shape):
            return es.enter_context(nc.sbuf_tensor(name, [P, *shape], F32))

        ring = sb("weight_ring", SLOTS, SLOT)
        xT = sb("xT", KT, L)
        hT = sb("hT", KT, L)
        cst = sb("cst", NCONST)
        mean_ones = sb("mean_ones", 2, P)
        cols = sb("cols", 4, P)
        mod_cols = sb("mod_cols", 48, 2)
        scale_a = sb("scale_a", 3, KT)
        sc_pad = sb("sc_pad", KT, 32)
        small = sb("small", 160)
        AW = 18100
        w_route = sb("w_route", KT, NE)
        arena = sb("arena", AW)
        ps = es.enter_context(nc.psum_tensor("ps", [P, 8 * 512], F32))

        def const(name):
            a, b = CONST[name]
            return cst[:, a:b]

        ident = const("ident")
        eps_col = small[:, 0:1]

        def at(off, *dims):
            n = int(np.prod(dims))
            assert off + n <= AW, (off, n)
            v = arena[:, off:off + n]
            if len(dims) == 2:
                v = v.rearrange("p (a b) -> p a b", a=dims[0])
            if len(dims) == 3:
                v = v.rearrange("p (a b c) -> p a b c", a=dims[0], b=dims[1])
            if len(dims) == 4:
                v = v.rearrange("p (a b c d) -> p a b c d", a=dims[0], b=dims[1], c=dims[2])
            return v

        def slot(i, k):
            return ring[:, i % SLOTS, :].rearrange("p (k n) -> p k n", k=k)

        names = """landed0 landed1 landed2 landed3 landed4 landed5 chunk_free tile_full freed_a freed_d
            consts_in vecs_in bcast_in dve_chain act_chain pool_chain ones_ready silu_ready m1_sb mods_ready
            sq_ready root_ready recip_ready scaled h_ready raw_done rope_cos rope_sin rope_in q_ready
            kw_ready vc_ready decay_ready qdec_ready dist_in table_in table_arg table_exp table_ready table_used
            o_square o_sq_used o_root p_ready g_silu g_ready gate_sig merged_ready conv_mid conv_done gelu_ready act_ready
            ln_ready ln_stats ln_root lnrow_in mix_add ya_ready row_max exp_done p_scaled sink_exp pt_ready kdup_ready
            h2t_ready router_in aff_ready rank_ready sel_ready wsel_ready
            xe_full xe_ready g_full silu_done hm_ready hmt_full hmt_ready y_full y_ready sc_full x_added
            out_full out_ready stored x_final decay_exp stage2_in""".split()
        S = {n: es.enter_context(nc.semaphore(n)) for n in names}
        FREED = {"A": S["freed_a"], "D": S["freed_d"]}

        def tile(name, width=None):
            w = banks.tiles[banks.where[name]][4]
            k = banks.bank(name)
            return ps[:, k * 512:k * 512 + 512 * w]

        filled = []

        def claim(pe, name):
            for by, count in banks.before(name):
                pe.wait_ge(FREED[by], count)
            return tile(name)

        def fill(name, last):
            assert banks.where[name] == len(filled), name
            filled.append(name)
            last.then_inc(S["tile_full"], 1)

        def wait_full(eng, name):
            eng.wait_ge(S["tile_full"], banks.where[name] + 1)
            return tile(name)

        evacuated = {"A": 0, "D": 0}

        def free(name, by, last):
            _, b, _, nth, _ = banks.tiles[banks.where[name]]
            evacuated[by] += 1
            assert b == by and nth == evacuated[by], name
            last.then_inc(FREED[by], 1)

        def wait_freed(eng, name):
            _, by, _, nth, _ = banks.tiles[banks.where[name]]
            eng.wait_ge(FREED[by], nth)

        def kmaj(w, n0, n1):
            return w[:, n0:n1].rearrange("(k p) n -> p k n", p=P)

        chunks = []
        chunk_at = {}

        def chunk(name, *parts):
            chunk_at[name] = len(chunks)
            chunks.append(parts)

        chunk("x", x[0].rearrange("(t p) d -> p t d", p=P))
        chunk("ctx", ctx[0].rearrange("(t p) d -> p t d", p=P))
        for i in range(12):
            chunk(("mod1", i), kmaj(w_mod[0], 512 * i, 512 * i + 512))
        for i in range(7):
            chunk(("in1", i), kmaj(w_in[0], 512 * i, 512 * i + 512))
        chunk("dft", dft_len)
        for nq in range(2):
            o = 512 * nq
            chunk(("m1", "gate", "a", nq), kmaj(w_branch_gate[0], D + o, D + o + 512))
            chunk(("m1", "proj", "a", nq), kmaj(w_four_out[0], o, o + 512))
            chunk(("m1", "gate", "b", nq), kmaj(w_branch_gate[0], o, o + 512))
            chunk(("m1", "proj", "b", nq), kmaj(w_ret_out[0], o, o + 512))
        for nq in range(2):
            chunk(("out1", nq), kmaj(w_out[0], 512 * nq, 512 * nq + 512))
        for j in range(UPN):
            chunk(("up", j), kmaj(w_up[0], 256 * j, 256 * j + 256),
                  kmaj(w_up[0], FFN + 256 * j, FFN + 256 * j + 256))
        for j in range(6):
            part = w_down[0][512 * j:min(512 * j + 512, FFN), :].rearrange("(k p) n -> p k n", p=P)
            if j < 5:
                chunk(("down", j), part)
            else:
                chunk(("down", j), part, ctx_2[0].rearrange("(t p) d -> p t d", p=P))
        for i in range(12):
            chunk(("mod2", i), kmaj(w_ada_2[0], 512 * i, 512 * i + 512))
        for i in range(7):
            chunk(("in2", i), kmaj(w_in_2[0], 512 * i, 512 * i + 512))
        for nq in range(2):
            o = 512 * nq
            chunk(("m2", "gate", "a", nq), kmaj(w_in_2[0], 3584 + o, 3584 + o + 512))
            chunk(("m2", "proj", "a", nq), kmaj(w_proj_a_2[0], o, o + 512))
            chunk(("m2", "gate", "b", nq), kmaj(w_in_2[0], 3584 + D + o, 3584 + D + o + 512))
            chunk(("m2", "proj", "b", nq), kmaj(w_proj_b_2[0], o, o + 512))
        for nq in range(2):
            chunk(("out2", nq), kmaj(w_out_2[0], 512 * nq, 512 * nq + 512))
        NCH = len(chunks)
        assert NCH % SLOTS == 0

        def landed(eng, name):
            n = chunk_at[name]
            loads = sum(len(chunks[m]) for m in range(n % SLOTS, n + 1, SLOTS))
            eng.wait_ge(S[f"landed{n % SLOTS}"], 16 * loads)
            return n % SLOTS

        last_tile = {"x": ("xT", 7), "ctx": ("cT", 3), "dft": ("fa", 3, 1), ("down", 5): ("cT2", 3),
                     ("in1", 0): ("qk1", 3), ("in1", 1): ("qk1", 7), ("in1", 2): ("v", 0, 3),
                     ("in1", 3): ("v", 1, 3), ("in1", 4): ("g", 3), ("in1", 5): ("g", 7), ("in1", 6): ("f", 3),
                     ("in2", 0): ("u", 3), ("in2", 1): ("u", 7), ("in2", 2): ("va", 0, 3),
                     ("in2", 3): ("va", 1, 3), ("in2", 4): ("q2", 3), ("in2", 5): ("q2", 7),
                     ("in2", 6): ("vc2", 1)}
        for i in range(12):
            last_tile["mod1", i], last_tile["mod2", i] = ("mod1", i), ("mod2", i)
        for nq in range(2):
            for tag in ("m1", "m2"):
                for part in "ab":
                    for kind in ("gate", "proj"):
                        last_tile[tag, kind, part, nq] = (tag, kind, part, nq, 3)
            last_tile["out1", nq], last_tile["out2", nq] = ("out1", 4 * nq + 3), ("out2", 4 * nq + 3)
        for j in range(UPN):
            last_tile["up", j] = ("up", j, 3)
        order = {n: name for name, n in chunk_at.items()}

        def wait_spent(sp, n):
            if order[n] in last_tile:
                sp.wait_ge(S["tile_full"], banks.where[last_tile[order[n]]] + 1)
            else:
                sp.wait_ge(S["chunk_free"], order[n][1] + 1)

        LOOP_FREE = 6

        merge_views = {"m1": (at(5120, KT, L), at(13696, 2, 4, L)),
                       "m2": (at(8192, KT, L), at(12288, 2, 4, L))}
        sq8 = at(0, KT, L)
        root = at(4096, L)
        recip = at(4608, L)
        rows_v = at(5120, 4, P)
        m_sb = at(5632, 2, L)
        hc = at(10240, KT, LC)
        obuf = at(0, 10, L)
        v1 = at(5120, TT, D)
        rope_cs = at(5120, 2, L)
        raw = at(6144, 2, L)
        rcos = at(7168, 2, L)
        rsin = at(8192, 2, L)
        kc = at(12288, CT, 512)
        kw = at(13312, 2, CT, 512)
        vc = at(15360, CT, D)
        state = at(9216, 2, 4, P)
        dist_sb = at(10240, 896)
        tpos = at(11136, L)
        probs = at(11648, 4, L)
        table = at(13696, 2, 896)
        qdec = at(15488, 2, L)
        osq = at(16512, L)
        band = at(17600, P)
        rinv = at(17024, L)
        f_tok = at(5120, TT, 512)
        fa = at(7168, FG, 2, L)
        z = at(11264, FG, L)
        dftd = at(13312, 2, P)
        act = at(0, FT, L)
        conv = at(11264, 4, L)
        gelu_a = at(13312, 2, L)
        hc2 = at(14336, KT, LC)
        ug = at(0, KT, L)
        va = at(4096, TT, D)
        ln_rows = at(8192, 2, D)
        bs_rows = at(10240, NG, P)
        ws_t = at(11264, NG, P)
        ws_raw = at(12288, NG, P)
        mixed = at(13312, 2, L)
        stats = at(16384, TT, 16)
        q2 = at(4096, KT, L)
        kdup = at(8192, NKV, L)
        krot = at(10240, 2, L)
        rope_cs2 = at(11264, 2, L)
        raw2 = at(12288, 2, L)
        rcos2 = at(13312, 2, L)
        rsin2 = at(16384, 2, L)
        vb = at(11264, TT, NKV * HD)
        kcdup = at(12288, NKV, LC)
        vcx = at(10240, CT, NKV * HD)
        NPB = 3
        prob2 = at(13312, NPB, 640)
        prob_t = at(15232, 5, 4, P)
        h2_tok = at(0, TT, D)
        sel = at(4096, TT, D)
        wsel_t = at(8192, PAIRS, L)
        xe = at(12288, KT, P)
        y_sb = at(13312, D)
        sg = at(14336, 2, 512)
        rt_work = at(15360, L)
        aff_t = at(15872, L)
        rank = at(16384, L)
        chosen = at(16896, L)
        aff = at(17408, TT, NE)
        rt_small = at(17472, 64)
        slot_of = at(17536, TT, NE)
        top8 = at(17600, 8)
        wsel = hT[:, :, :].rearrange("p a b -> p (a b)").rearrange("p (t n) -> p t n", t=TT)
        hmid = hT[:, 0:4, :].rearrange("p a b -> p (a b)")
        hmid_t = hT[:, 4:8, :].rearrange("p a b -> p (a b)").rearrange("p (k n) -> p k n", k=16)
        out_sb = at(0, TT, D)
        decay = small[:, 8:24]
        sink = small[:, 24:40]
        ea = small[:, 64:80]
        lg = small[:, 80:96]
        qcol = small[:, 96:108].rearrange("p (a b) -> p a b", a=3)
        ctxw = small[:, 112:144].rearrange("p (d t h) -> p d t h", d=2, t=CT)
        neg_m = small[:, 144:148]
        den = small[:, 148:152]
        sink_e = small[:, 152:156]
        negmean = at(17536, 8)
        row_top = at(17792, 4)

        block = es.enter_context(nc.Block())

        @block.sync
        def _(sp):
            sp.dma_start(cst[:, :], consts).then_inc(S["consts_in"], 16)
            rows = [
                (0, V1["c"], c), (0, V1["c_ctx"], c_ctx), (0, V1["norm1"], norm1_w), (0, V1["norm2"], norm2_w),
                (0, V1["final"], final_norm_w), (0, V1["b_gate"], b_branch_gate), (0, V1["b_mod"], b_mod),
                (3, V4["c"], c_2), (3, V4["c_ctx"], c_ctx_2), (3, V4["norm1"], norm1_g_2),
                (3, V4["norm2"], norm2_g_2), (3, V4["final"], final_g_2), (3, V4["b_gate"], b_merge_gate_2),
                (3, V4["b_mod"], b_ada_2), (2, V3["b"], conv_b)]
            for i, r, v in rows:
                flat = v if len(v.shape) == 1 else v.rearrange("a n -> (a n)")
                n = flat.shape[0] // P
                sp.dma_start(rows_v[r:r + n, i, :], flat.rearrange("(r p) -> r p", p=P)).then_inc(S["vecs_in"], 16)
            for i, r, t in ((1, V2["w0"], 0), (1, V2["w1"], 1), (2, V3["w2"], 2)):
                sp.dma_start(rows_v[r:r + 44, i, :],
                             conv_w[0, t].rearrange("(r p) -> r p", p=P)).then_inc(S["vecs_in"], 16)
            for k, v in enumerate((ret_decay_f[0], ret_decay_b[0])):
                sp.dma_start(small[:, 8 + 8 * k:16 + 8 * k], v.partition_broadcast(P)).then_inc(S["bcast_in"], 16)
            sp.dma_start(small[:, 24:40], attn_sink_2[0].partition_broadcast(P)).then_inc(S["bcast_in"], 16)
            for n in range(NCH):
                if n >= SLOTS:
                    wait_spent(sp, n - SLOTS)
                sl = n % SLOTS
                src = chunks[n]
                if len(src) == 1 or src[0].shape[2] == D:
                    o = 0
                    for part in src:
                        k, w = part.shape[1], part.shape[2]
                        sp.dma_start(ring[:, sl, o:o + k * w].rearrange("p (k n) -> p k n", k=k),
                                     part).then_inc(S[f"landed{sl}"], 16)
                        o += k * w
                else:
                    v = slot(sl, 8)
                    sp.dma_start(v[:, :, 0:256], src[0]).then_inc(S[f"landed{sl}"], 16)
                    sp.dma_start(v[:, :, 256:512], src[1]).then_inc(S[f"landed{sl}"], 16)
            def gate_up(w, e, fq):
                return w[0, bass.ds(e, 1), :, 512 * fq:512 * fq + 512].rearrange("a (k p) n -> p (a k) n", p=P)

            def down(e, kq):
                return w_exp_down_2[0, bass.ds(e, 1), 512 * kq:512 * kq + 512, :].rearrange(
                    "a (k p) n -> p (a k) n", p=P)

            wait_spent(sp, NCH - 1)
            sp.sem_inc(S["chunk_free"], 1)
            with sp.Fori(0, PAIRS) as it:
                m = 0
                for fq in range(FQ):
                    for w in (w_exp_gate_2, w_exp_up_2):
                        for e in range(2):
                            sp.wait_ge(S["chunk_free"], it * PAIR_CHUNKS + LOOP_FREE + m - SLOTS + 1)
                            sp.dma_start(slot(m, 8), gate_up(w, it * 2 + e, fq)).then_inc(
                                S[f"landed{m % SLOTS}"], 16)
                            m += 1
                for kq in range(FQ):
                    for e in range(2):
                        sp.wait_ge(S["chunk_free"], it * PAIR_CHUNKS + LOOP_FREE + m - SLOTS + 1)
                        sp.dma_start(slot(m, 4), down(it * 2 + e, kq)).then_inc(
                            S[f"landed{m % SLOTS}"], 16)
                        m += 1
            for t in range(TT):
                for hh in range(2):
                    wait_freed(sp, ("ot", t, hh))
                sp.dma_start(out[0, t * P:(t + 1) * P, :], out_sb[:, t, :]).then_inc(S["stored"], 16)
            sp.wait_ge(S["stored"], 16 * TT)

        @block.tensor
        def _(pe):
            def feature_tiles(cname, tnames, src, kt=KT, width=512, c0=0):
                w = ring[:, landed(pe, cname), 0:kt * 512].rearrange("p (k n) -> p k n", k=kt)
                for n, tn in enumerate(tnames):
                    t = claim(pe, tn)[:, 0:width]
                    for k in range(kt):
                        last = pe.matmul(t, w[:, k, c0 + n * P:c0 + (n + 1) * P], src[:, k, 0:width],
                                         start=(k == 0), stop=(k == kt - 1))
                    fill(tn, last)

            def token_tiles(cname, tnames, src, c0=0, width=512):
                w = slot(landed(pe, cname), KT)
                for t, tn in enumerate(tnames):
                    o = claim(pe, tn)[:, 0:width]
                    for k in range(KT):
                        last = pe.matmul(o, src[:, k, t * P:(t + 1) * P], w[:, k, c0:c0 + width],
                                         start=(k == 0), stop=(k == KT - 1))
                    fill(tn, last)

            def turn(name, parts):
                t = claim(pe, name)
                for o, src in parts:
                    rows = src.shape[0]
                    last = pe.transpose(t[:, o:o + rows], src, ident[0:rows, 0:rows])
                fill(name, last)

            def norm(m, tag, width):
                t = claim(pe, tag)[:, 0:width]
                for k in range(KT):
                    pe.wait_ge(S["sq_ready"], KT * m + k + 1)
                    last = pe.matmul(t, mean_ones[:, 0, :], sq8[:, k, 0:width], start=(k == 0), stop=(k == KT - 1))
                fill(tag, last)

            def modulation(tag, nth):
                def turn_rows(c):
                    wait_freed(pe, (tag, c))
                    t = claim(pe, (tag, "T", c))
                    for j in range(4):
                        last = pe.matmul(t[:, 2 * j:2 * j + 2], m_sb[:, c % 2, j * P:(j + 1) * P],
                                         const("modsel"), start=True, stop=True)
                    fill((tag, "T", c), last)

                pe.wait_ge(S["silu_ready"], 2 * (nth + 1))
                for c in range(12):
                    w = slot(landed(pe, (tag, c)), KT)
                    t = claim(pe, (tag, c))
                    for k in range(KT):
                        g = 32 * (k % 4)
                        last = pe.matmul(t[g:g + 32, :], sc_pad[:, k, :], w[:, k, :],
                                         start=(k < 4), stop=(k >= 4), tile_position=(0, g))
                    fill((tag, c), last)
                    if c:
                        turn_rows(c - 1)
                turn_rows(11)

            def swap(tag, i, matrix, rawbuf):
                wait_freed(pe, (tag, i))
                t = claim(pe, (tag, "swap", i))
                fill((tag, "swap", i), pe.matmul(t, const(matrix), rawbuf[:, i % 2, :], start=True, stop=True))

            def roped(tag, cname, i0, n, matrix, rawbuf, first=None):
                for i in range(i0, i0 + n):
                    feature_tiles(cname, [(tag, i)], hT, c0=(i - i0) * P)
                    if i > i0 or first is not None:
                        if i > i0:
                            swap(tag, i - 1, matrix, rawbuf)
                        else:
                            first()

            def merge(tag, src_a, kt_a, src_b, kt_b):
                for nq in range(2):
                    for part, src, kt in (("a", src_a, kt_a), ("b", src_b, kt_b)):
                        feature_tiles((tag, "gate", part, nq), [(tag, "gate", part, nq, n) for n in range(4)], hT)
                        feature_tiles((tag, "proj", part, nq), [(tag, "proj", part, nq, n) for n in range(4)],
                                      src, kt=kt)

            def out_proj(tag, mtag):
                pe.wait_ge(S["merged_ready"], 8 * (1 if mtag == "m1" else 2))
                for nq in range(2):
                    feature_tiles((tag, nq), [(tag, 4 * nq + n) for n in range(4)], merge_views[mtag][0])

            pe.wait_ge(S["consts_in"], 16)
            pe.wait_ge(S["vecs_in"], 16 * 18)
            turn("vecs", [(i * P, rows_v[0:r, i, :]) for i, r in enumerate((104, 88, 88, 104))])
            w = slot(landed(pe, "x"), TT)
            for k in range(KT):
                turn(("xT", k), [(t * P, w[:, t, k * P:(k + 1) * P]) for t in range(TT)])
            w = slot(landed(pe, "ctx"), TT)
            for k in range(KT // 2):
                turn(("cT", k), [(j * LC + t * P, w[:, t, (2 * k + j) * P:(2 * k + j + 1) * P])
                                 for j in range(2) for t in range(CT)])
            modulation("mod1", 0)
            pe.wait_ge(S["ones_ready"], 4)
            norm(0, "n1", L)
            norm(1, "nc", LC)
            pe.wait_ge(S["h_ready"], 8)
            roped("qk1", ("in1", 0), 0, 4, "swap1", raw)
            swap("qk1", 3, "swap1", raw)
            pe.wait_ge(S["h_ready"], 16)
            token_tiles(("in1", 1), [("kc", t) for t in range(CT)], hc)
            roped("qk1", ("in1", 1), 4, 4, "swap1", raw)
            swap("qk1", 7, "swap1", raw)
            for hh in range(2):
                token_tiles(("in1", 2 + hh), [("vc", hh, t) for t in range(CT)], hc)
                token_tiles(("in1", 2 + hh), [("v", hh, t) for t in range(TT)], hT)
            pe.wait_ge(S["kw_ready"], 4)
            wait_freed(pe, ("vc", 1, CT - 1))
            t = claim(pe, "S").rearrange("p (d j e) -> p d j e", d=2, j=4)
            for d in range(2):
                for h in range(H1):
                    o = 64 * (h % 2)
                    for tt in range(CT):
                        last = pe.matmul(t[o:o + 64, d, h // 2, :], kw[:, d, tt, h * DK:(h + 1) * DK],
                                         vc[:, tt, h * DV:(h + 1) * DV], start=(tt == 0), stop=(tt == CT - 1))
            fill("S", last)
            def scores(h):
                o = 64 * (h % 2)
                for i in range(TT):
                    t = claim(pe, ("s", h, i))
                    fill(("s", h, i), pe.matmul(t, obuf[o:o + 64, 3 + 2 * (h // 2), i * P:(i + 1) * P],
                                                obuf[o:o + 64, 2 + 2 * (h // 2), :], start=True, stop=True))

            def outputs(h):
                o = 64 * (h % 2)
                t = claim(pe, ("o", h))
                for i in range(TT):
                    wait_freed(pe, ("s", h, i))
                    pe.matmul(t, v1[:, i, h * DV:(h + 1) * DV], probs[:, i, :], start=(i == 0), stop=False)
                pe.wait_ge(S["qdec_ready"], 2 * (h // 2) + 2)
                for d in range(2):
                    last = pe.matmul(t, state[o:o + 64, d, h // 2, :], qdec[o:o + 64, d, :],
                                     start=False, stop=(d == 1))
                fill(("o", h), last)

            pe.wait_ge(S["q_ready"], 8)
            wait_freed(pe, ("v", 1, TT - 1))
            wait_freed(pe, "S")
            for h in range(H1 + 1):
                if h:
                    outputs(h - 1)
                if h < H1:
                    scores(h)
                if h:
                    wait_freed(pe, ("o", h - 1))
                    t = claim(pe, ("var", h - 1))
                    fill(("var", h - 1), pe.matmul(t, mean_ones[:, 1, :], osq, start=True, stop=True))
            for n in range(2):
                feature_tiles(("in1", 4 + n), [("g", 4 * n + i) for i in range(4)], hT)
            token_tiles(("in1", 6), [("f", t) for t in range(TT)], hT)
            wl = ring[:, landed(pe, "dft"), :].rearrange("p (m k n) -> p m k n", m=2, k=TT)
            for g in range(FG):
                for m in range(2):
                    t = claim(pe, ("fa", g, m))
                    wait_freed(pe, ("f", TT - 1))
                    for k in range(TT):
                        last = pe.matmul(t, f_tok[:, k, g * P:(g + 1) * P], wl[:, m, k, :],
                                         start=(k == 0), stop=(k == TT - 1))
                    fill(("fa", g, m), last)
            pe.wait_ge(S["dist_in"], 48)
            for g in range(FG):
                t = claim(pe, ("z", g))
                wait_freed(pe, ("fa", g, 1))
                pe.matmul(t, dftd[:, 0, :], fa[:, g, 0, :], start=True, stop=False)
                fill(("z", g), pe.matmul(t, dftd[:, 1, :], fa[:, g, 1, :], start=False, stop=True))
            wait_freed(pe, ("z", FG - 1))
            pe.wait_ge(S["g_ready"], 8)
            merge("m1", z, 4, obuf, KT)
            out_proj("out1", "m1")
            norm(2, "n2", L)
            pe.wait_ge(S["h_ready"], 24)
            for j in range(UPN):
                feature_tiles(("up", j), [("up", j, n) for n in range(4)], hT)
            for n in range(KT):
                claim(pe, ("down", n))
            for j in range(6):
                kt = 4 if j < 5 else 2
                w = slot(landed(pe, ("down", j)), 4)
                for n in range(KT):
                    t = tile(("down", n))
                    for k in range(kt):
                        if n == 0:
                            pe.wait_ge(S["act_ready"], 4 * j + k + 1)
                        last = pe.matmul(t, w[:, k, n * P:(n + 1) * P], act[:, 4 * j + k, :],
                                         start=(j == 0 and k == 0), stop=(j == 5 and k == 1))
                    if j == 5:
                        fill(("down", n), last)
                if j < 5:
                    last.then_inc(S["chunk_free"], 1)
            w = slot(chunk_at["down", 5], 4)
            for k in range(KT // 2):
                turn(("cT2", k), [(j * LC + t * P, w[:, 2 + t, (2 * k + j) * P:(2 * k + j + 1) * P])
                                  for j in range(2) for t in range(CT)])
            norm(3, "nf1", L)
            modulation("mod2", 1)
            norm(4, "n3", L)
            norm(5, "nc2", LC)
            pe.wait_ge(S["h_ready"], 32)
            for n in range(2):
                feature_tiles(("in2", n), [("u", 4 * n + i) for i in range(4)], hT)
            for hh in range(2):
                token_tiles(("in2", 2 + hh), [("va", hh, t) for t in range(TT)], hT)
            pe.wait_ge(S["stage2_in"], 16 * 4)
            for i in range(2):
                turn(("ws", i), [(j * P, ws_raw[:, 4 * i + j, :]) for j in range(4)])
            wait_freed(pe, ("ws", 1))
            pe.wait_ge(S["ln_ready"], TT)
            for g in range(NG):
                t = claim(pe, ("mix", g))
                for cc in range(TT):
                    last = pe.matmul(t[:, cc * P:(cc + 1) * P], va[:, cc, g * P:(g + 1) * P], ws_t[:, g, :],
                                     start=True, stop=True)
                fill(("mix", g), last)
            roped("q2", ("in2", 4), 0, 4, "swap2", raw2)
            roped("q2", ("in2", 5), 4, 4, "swap2", raw2, first=lambda: swap("q2", 3, "swap2", raw2))
            swap("q2", 7, "swap2", raw2)
            roped("k2", ("in2", 6), 0, 2, "swap2", raw2)
            swap("k2", 1, "swap2", raw2)
            token_tiles(("in2", 6), [("vb", t) for t in range(TT)], hT, c0=256, width=256)
            pe.wait_ge(S["h_ready"], 40)
            feature_tiles(("in2", 6), [("kc2", i) for i in range(2)], hc2, width=LC)
            token_tiles(("in2", 6), [("vc2", t) for t in range(CT)], hc2, c0=256, width=256)
            def item(i):
                kv, n, r = i // 16, (i // 4) % 4, i % 4
                return kv, n, r, max(n - 1, 0), min(n + 2, TT)

            def att_scores(i):
                kv, n, r, b0, b1 = item(i)
                h = 4 * kv + r
                o = 64 * (h % 2)
                t = claim(pe, ("as", i))
                lq = q2[o:o + 64, h // 2, n * P:(n + 1) * P]
                pe.matmul(t[:, 512 - (b1 - b0) * P:512], lq, kdup[o:o + 64, kv, b0 * P:b1 * P],
                          start=True, stop=True)
                fill(("as", i), pe.matmul(t[:, 512:512 + LC], lq, kcdup[o:o + 64, kv, :],
                                          start=True, stop=True))

            def att_turn(i):
                _, _, _, b0, b1 = item(i)
                pe.wait_ge(S["p_scaled"], i + 1)
                t = claim(pe, ("at", i))
                nb = b1 - b0 + CT
                o = (3 - (b1 - b0)) * P
                for b in range(nb):
                    last = pe.transpose(t[:, b * P:(b + 1) * P],
                                        prob2[:, i % NPB, o + b * P:o + (b + 1) * P], ident)
                fill(("at", i), last)

            def att_values(g):
                kv, n, _, b0, b1 = item(4 * g)
                wait_freed(pe, ("at", 4 * g + 3))
                t = claim(pe, ("pv", g))
                nb = b1 - b0 + CT
                for b in range(nb):
                    vals = (vb[:, b0 + b, :] if b < b1 - b0 else vcx[:, b - (b1 - b0), :])
                    for par in range(2):
                        last = pe.matmul(t[64 * par:64 * par + 64, 0:256].rearrange("p (a q) -> p a q", a=2),
                                         vals[:, kv * HD:(kv + 1) * HD], prob_t[:, b, par:4:2, :],
                                         start=(b == 0), stop=(b == nb - 1))
                fill(("pv", g), last)

            pe.wait_ge(S["kdup_ready"], 1)
            wait_freed(pe, ("kc2", 1))
            wait_freed(pe, ("vc2", CT - 1))
            for i in range(NH * TT + 1):
                if i < NH * TT:
                    att_scores(i)
                if i % 4 == 1 and i > 1:
                    att_values(i // 4 - 1)
                if i:
                    att_turn(i - 1)
            att_values(NH * TT // 4 - 1)
            pe.wait_ge(S["ya_ready"], NG)
            wait_freed(pe, ("pv", NH * TT // 4 - 1))
            merge("m2", ug, KT, q2, KT)
            out_proj("out2", "m2")
            norm(6, "n4", L)
            pe.wait_ge(S["h_ready"], 48)
            for t in range(TT):
                for hh in range(2):
                    turn(("ht", t, hh), [(k * P, hT[:, 4 * hh + k, t * P:(t + 1) * P]) for k in range(4)])
            pe.wait_ge(S["router_in"], 16)
            r = claim(pe, "router")
            for t in range(TT):
                for k in range(KT):
                    last = pe.matmul(r[:, t * NE:(t + 1) * NE], hT[:, k, t * P:(t + 1) * P], w_route[:, k, :],
                                     start=(k == 0), stop=(k == KT - 1))
            fill("router", last)
            pe.wait_ge(S["aff_ready"], 1)
            a = claim(pe, "affT")
            for t in range(TT):
                last = pe.transpose(a[0:NE, t * P:(t + 1) * P], aff[:, t, :], ident)
            fill("affT", last)
            pe.wait_ge(S["rank_ready"], 1)
            a = claim(pe, "slotT")
            for t in range(TT):
                last = pe.transpose(a[:, t * NE:(t + 1) * NE], rank[0:NE, t * P:(t + 1) * P], ident[0:NE, 0:NE])
            fill("slotT", last)
            pe.wait_ge(S["wsel_ready"], TT)
            for q in range(PAIRS):
                turn(("wt", q), [(t * P, wsel[:, t, q * P:(q + 1) * P]) for t in range(TT)])
            def landed_loop(it, m):
                loads = sum(len(chunks[n]) for n in range(m % SLOTS, NCH, SLOTS))
                pe.wait_ge(S[f"landed{m % SLOTS}"],
                           it * (16 * PAIR_CHUNKS // SLOTS) + 16 * (loads + m // SLOTS + 1))
                return slot(m, 8 if m < 4 * FQ else 4)

            def bank(b, n=1):
                return ps[:, b * 512:(b + n) * 512]

            wait_freed(pe, ("wt", PAIRS - 1))
            wait_freed(pe, ("wt", PAIRS - 2))
            pe.wait_ge(S["sel_ready"], TT)
            with pe.Fori(0, PAIRS) as it:
                pe.wait_ge(S["y_ready"], it * 2 + 1)
                for d in range(KT):
                    for t in range(TT):
                        last = pe.matmul(bank(6, 2)[:, d * P:(d + 1) * P], h2_tok[:, t, d * P:(d + 1) * P],
                                         sel[:, t, bass.ds(it * P, P)], start=(t == 0), stop=(t == TT - 1))
                    if d % 4 == 3:
                        last.then_inc(S["xe_full"], 1)
                pe.wait_ge(S["xe_ready"], it * 2 + 2)
                pe.wait_ge(S["x_added"], it * KT + 1)

                def turn_hidden(fq):
                    n = it * FQ + fq
                    pe.wait_ge(S["hm_ready"], n + 2)
                    pe.wait_ge(S["hmt_ready"], n + 1)
                    for j in range(4):
                        last = pe.transpose(bank(4)[:, j * P:(j + 1) * P],
                                            hmid[:, fq * 512 + j * P:fq * 512 + (j + 1) * P], ident)
                    last.then_inc(S["hmt_full"], 1)

                for fq in range(FQ):
                    if fq >= 2:
                        pe.wait_ge(S["hm_ready"], it * FQ + fq)
                    for gu in range(2):
                        m = 4 * fq + 2 * gu
                        wa, wb = landed_loop(it, m), landed_loop(it, m + 1)
                        b = bank(2 * (fq % 2) + gu)
                        for k in range(KT):
                            la = pe.matmul(b[0:64, :], xe[:, k, 0:64], wa[:, k, :],
                                           start=(k == 0), stop=(k == KT - 1))
                            lb = pe.matmul(b[64:128, :], xe[:, k, 64:128], wb[:, k, :],
                                           start=(k == 0), stop=(k == KT - 1))
                        la.then_inc(S["chunk_free"], 1)
                        lb.then_inc(S["chunk_free"], 1)
                    if fq:
                        turn_hidden(fq - 1)
                turn_hidden(FQ - 1)
                for kq in range(FQ):
                    pe.wait_ge(S["hmt_ready"], it * FQ + kq + 2)
                    m = 4 * FQ + 2 * kq
                    wa, wb = landed_loop(it, m), landed_loop(it, m + 1)
                    for k in range(4):
                        for hh in range(2):
                            la = pe.matmul(bank(6 + hh)[0:64, :], hmid_t[:, 4 * kq + k, 0:64],
                                           wa[:, k, hh * 512:(hh + 1) * 512],
                                           start=(kq == 0 and k == 0), stop=(kq == FQ - 1 and k == 3))
                            lb = pe.matmul(bank(6 + hh)[64:128, :], hmid_t[:, 4 * kq + k, 64:128],
                                           wb[:, k, hh * 512:(hh + 1) * 512],
                                           start=(kq == 0 and k == 0), stop=(kq == FQ - 1 and k == 3))
                    la.then_inc(S["chunk_free"], 1)
                    lb.then_inc(S["chunk_free"], 1)
                pe.wait_ge(S["y_ready"], it * 2 + 3)
                pe.wait_ge(S["hm_ready"], it * FQ + FQ + 1)
                for d in range(KT):
                    if d >= 4:
                        pe.wait_ge(S["x_added"], it * KT + 1 + d - 3)
                    pe.matmul(bank(d % 4), y_sb[:, d * P:(d + 1) * P], wsel_t[:, bass.ds(it, 1), :].rearrange(
                        "p a b -> p (a b)"), start=True, stop=True).then_inc(S["sc_full"], 1)
            norm(7, "nf2", L)
            pe.wait_ge(S["scaled"], 8 * 8)
            for t in range(TT):
                for hh in range(2):
                    turn(("ot", t, hh), [(k * P, xT[:, 4 * hh + k, t * P:(t + 1) * P]) for k in range(4)])

        @block.scalar
        def _(act_e):
            A = act_e.activation

            def copy_out(name, dst, func=ACT.Copy, width=512, **kw_):
                t = wait_full(act_e, name)[:, 0:width]
                free(name, "A", A(dst, t, func, **kw_))

            def norm_squares(m, tag, src, width):
                for k in range(KT):
                    A(sq8[:, k, 0:width], src[:, k, 0:width], ACT.Square).then_inc(S["sq_ready"], 1)
                if m:
                    act_e.wait_ge(S["recip_ready"], m)
                copy_out(tag, root[:, 0:width], ACT.Sqrt, width=width, bias=eps_col)

            def norm_affine(m, dst, width, a, shift):
                for k in range(KT):
                    act_e.wait_ge(S["scaled"], KT * m + k + 1)
                    A(dst[:, k, 0:width], dst[:, k, 0:width], ACT.Identity, bias=shift(k), scale=a(k)).then_inc(
                        S["h_ready"], 1)

            def modulation(tag, nth, vi):
                act_e.wait_ge(S["ones_ready"], 4)
                wait_freed(act_e, "vecs")
                for r in range(2):
                    A(sc_pad[:, :, r], cols[:, vi, 8 * r:8 * r + 8], ACT.Silu).then_inc(S["silu_ready"], 1)
                for c in range(12):
                    if c >= 2:
                        wait_full(act_e, (tag, "T", c - 2))
                    copy_out((tag, c), m_sb[:, c % 2, :])

            def rope_raw(tag, i, g, rawbuf, scale):
                if g >= 2:
                    act_e.wait_ge(S["rope_cos"], g - 1)
                    act_e.wait_ge(S["q_ready"], g - 1)
                copy_out((tag, i), rawbuf[:, i % 2, :], ACT.Copy, scale=scale)

            def merge_gates(tag, vi):
                _, gates = merge_views[tag]
                base = V1["b_gate"]
                for nq in range(2):
                    for pi, part in enumerate("ab"):
                        first = 8 if (tag == "m1") == (part == "a") else 0
                        if nq and part == "a":
                            wait_freed(act_e, (tag, "proj", "a", 0, 3))
                        elif nq:
                            act_e.wait_ge(S["merged_ready"], (0 if tag == "m1" else 8) + 4)
                        for n in range(4):
                            col = base + first + 4 * nq + n
                            copy_out((tag, "gate", part, nq, n), gates[:, pi, n, :], ACT.Sigmoid,
                                     bias=cols[:, vi, col:col + 1])

            act_e.wait_ge(S["ones_ready"], 4)
            for k in range(0, KT, 2):
                copy_out(("xT", k), xT[:, k, :])
            for k in range(0, KT // 2, 2):
                copy_out(("cT", k), hc[:, 2 * k:2 * k + 2, :].rearrange("p a b -> p (a b)"))
            modulation("mod1", 0, 0)
            for n in (("xT", 6), ("xT", 7), ("cT", 2), ("cT", 3)):
                wait_freed(act_e, n)
            norm_squares(0, "n1", xT, L)
            wait_full(act_e, "n1")
            norm_squares(1, "nc", hc, LC)
            act_e.wait_ge(S["mods_ready"], 1)
            norm_affine(0, hT, L, lambda k: scale_a[:, 0, k:k + 1], lambda k: mod_cols[:, k, 0:1])
            norm_affine(1, hc, LC, lambda k: scale_a[:, 1, k:k + 1], lambda k: mod_cols[:, k, 1:2])
            act_e.wait_ge(S["bcast_in"], 48)
            A(ea, decay, ACT.Exp).then_inc(S["decay_exp"], 1)
            act_e.wait_ge(S["decay_ready"], 1)
            for d in range(2):
                for t in range(CT):
                    c0 = CONST["age"][0] + 2 * d + t
                    A(ctxw[:, d, t, :], lg[:, 8 * d:8 * d + 8], ACT.Exp, scale=cst[:, c0:c0 + 1]).then_inc(
                        S["decay_exp"], 1)
            for i in range(4):
                rope_raw("qk1", i, i, raw, DK ** -0.5)
            for t in range(CT):
                copy_out(("kc", t), kc[:, t, :])
            for i in range(4, 8):
                rope_raw("qk1", i, i, raw, 1.0)
            def decayed_queries(j):
                if j:
                    wait_full(act_e, ("o", 2 * j - 1))
                    act_e.wait_ge(S["qdec_ready"], 2 * j)
                A(qdec[:, 0, :], tpos, ACT.Exp, scale=qcol[:, 0, j:j + 1]).then_inc(S["table_in"], 1)
                A(qdec[:, 1, :], tpos, ACT.Exp, scale=qcol[:, 1, j:j + 1],
                  bias=qcol[:, 2, j:j + 1]).then_inc(S["table_in"], 1)

            def decay_table(h):
                act_e.wait_ge(S["table_arg"], h + 1)
                A(table[:, h % 2, :], table[:, h % 2, :], ACT.Exp).then_inc(S["table_exp"], 1)

            act_e.wait_ge(S["dist_in"], 32)
            act_e.wait_ge(S["decay_ready"], 2)
            wait_freed(act_e, "S")
            decay_table(0)
            decayed_queries(0)
            decay_table(1)
            for h in range(H1):
                t = wait_full(act_e, ("o", h))
                if h:
                    wait_full(act_e, ("var", h - 1))
                A(osq, t, ACT.Square)
                free(("o", h), "A", A(obuf[:, h, :], t, ACT.Copy))
                if h % 2 and h + 1 < H1:
                    decayed_queries(h // 2 + 1)
                if h + 2 < H1:
                    decay_table(h + 2)
                if h:
                    act_e.wait_ge(S["o_square"], h)
                copy_out(("var", h), rinv, ACT.Sqrt, bias=eps_col)
            wait_full(act_e, ("g", 0))
            for n in range(KT):
                copy_out(("g", n), at(10240 + 512 * n, L), ACT.Silu)
            for t in range(TT):
                copy_out(("f", t), f_tok[:, t, :])
            for g in range(FG):
                for m in range(2):
                    if g == 0 and m == 0:
                        act_e.wait_ge(S["g_ready"], 8)
                    copy_out(("fa", g, m), fa[:, g, m, :])
            merge_gates("m1", 0)
            wait_freed(act_e, ("out1", KT - 1))
            norm_squares(2, "n2", xT, L)
            norm_affine(2, hT, L, lambda k: scale_a[:, 2, k:k + 1], lambda k: mod_cols[:, 24 + k, 0:1])
            for j in range(UPN):
                for n in range(4):
                    f = 2 * j + n % 2 + (FT if n >= 2 else 0)
                    t = wait_full(act_e, ("up", j, n))
                    if j:
                        act_e.wait_ge(S["act_ready"], 2 * (j - 1) + 1 + n % 2)
                    A(conv[:, n, :], t, ACT.Identity, bias=cols[:, 2, 44 + f:45 + f],
                      scale=cols[:, 1, 44 + f:45 + f]).then_inc(S["conv_mid"], 1)
                for n in range(2):
                    wait_freed(act_e, ("up", j, n))
                    A(gelu_a[:, n, :], conv[:, n, :], ACT.Gelu_apprx_tanh).then_inc(S["gelu_ready"], 1)
            for k in range(0, KT // 2, 2):
                copy_out(("cT2", k), hc2[:, 2 * k:2 * k + 2, :].rearrange("p a b -> p (a b)"))
            wait_freed(act_e, ("down", KT - 1))
            norm_squares(3, "nf1", xT, L)
            modulation("mod2", 1, 3)
            act_e.wait_ge(S["scaled"], 32)
            wait_freed(act_e, ("cT2", 2))
            wait_freed(act_e, ("cT2", 3))
            norm_squares(4, "n3", xT, L)
            norm_squares(5, "nc2", hc2, LC)
            act_e.wait_ge(S["mods_ready"], 2)
            norm_affine(4, hT, L, lambda k: scale_a[:, 0, k:k + 1], lambda k: mod_cols[:, k, 0:1])
            norm_affine(5, hc2, LC, lambda k: scale_a[:, 1, k:k + 1], lambda k: mod_cols[:, k, 1:2])
            for n in range(KT):
                copy_out(("u", n), ug[:, n, :], ACT.Gelu_apprx_tanh)
            for hh in range(2):
                for t in range(TT):
                    copy_out(("va", hh, t), va[:, t, hh * 512:(hh + 1) * 512], ACT.Gelu_apprx_tanh)
            for i in range(2):
                copy_out(("ws", i), ws_t[:, 4 * i:4 * i + 4, :].rearrange("p a b -> p (a b)"))
            act_e.wait_ge(S["ln_stats"], TT)
            A(stats[:, :, 14:15], stats[:, :, 13:14], ACT.Sqrt, bias=eps_col).then_inc(S["ln_root"], 1)
            for i in range(8):
                rope_raw("q2", i, 8 + i, raw2, HD ** -0.5)
            for i in range(2):
                rope_raw("k2", i, 16 + i, raw2, 1.0)
            act_e.wait_ge(S["q_ready"], 18)
            for t in range(TT):
                copy_out(("vb", t), vb[:, t, :], width=256)
            act_e.wait_ge(S["kdup_ready"], 1)
            for t in range(CT):
                copy_out(("vc2", t), vcx[:, t, :], width=256)
            def widths(i):
                n = (i // 4) % 4
                return (2 if n in (0, 3) else 3) * P

            def att_exp(i):
                h = 4 * (i // 16) + i % 4
                w = widths(i)
                act_e.wait_ge(S["row_max"], i + 1)
                t = tile(("as", i))
                if i >= NPB:
                    wait_full(act_e, ("at", i - NPB))
                if i >= 4:
                    act_e.wait_ge(S["p_scaled"], i - 3)
                free(("as", i), "A", A(prob2[:, i % NPB, 384 - w:640], t[:, 512 - w:768], ACT.Exp,
                                       bias=neg_m[:, i % 4:i % 4 + 1], accum_out=den[:, i % 4:i % 4 + 1]))
                A(sink_e[:, i % 4:i % 4 + 1], sink[:, h:h + 1], ACT.Exp,
                  bias=neg_m[:, i % 4:i % 4 + 1]).then_inc(S["sink_exp"], 1)

            def att_keep(i):
                nb = widths(i) // P + CT
                if i % 4 == 0 and i:
                    wait_full(act_e, ("pv", i // 4 - 1))
                t = wait_full(act_e, ("at", i))
                free(("at", i), "A", A(prob_t[:, 0:nb, i % 4, :],
                                       t[:, 0:nb * P].rearrange("p (b q) -> p b q", b=nb), ACT.Copy))

            for i in range(NH * TT + 1):
                if i < NH * TT:
                    att_exp(i)
                if i:
                    att_keep(i - 1)
            merge_gates("m2", 3)
            wait_freed(act_e, ("out2", KT - 1))
            norm_squares(6, "n4", xT, L)
            norm_affine(6, hT, L, lambda k: scale_a[:, 2, k:k + 1], lambda k: mod_cols[:, 24 + k, 0:1])
            for t in range(TT):
                copy_out(("ht", t, 0), h2_tok[:, t, 0:512])
            act_e.wait_ge(S["row_max"], NH * TT + 1)
            A(aff[:, :, :], aff[:, :, :], ACT.Exp).then_inc(S["exp_done"], 1)
            for q in range(0, PAIRS, 2):
                copy_out(("wt", q), wsel_t[:, q, :])
            act_e.sem_inc(S["y_ready"], 1)
            act_e.sem_inc(S["hmt_ready"], 1)
            with act_e.Fori(0, PAIRS) as it:
                for hh in range(2):
                    act_e.wait_ge(S["xe_full"], it * 2 + hh + 1)
                    A(xe[:, 4 * hh:4 * hh + 4, :].rearrange("p a b -> p (a b)"),
                      ps[:, (6 + hh) * 512:(7 + hh) * 512], ACT.Copy).then_inc(S["xe_ready"], 1)

                def keep_turned(fq):
                    act_e.wait_ge(S["hmt_full"], it * FQ + fq + 1)
                    A(hmid_t[:, 4 * fq:4 * fq + 4, :].rearrange("p a b -> p (a b)"), ps[:, 4 * 512:5 * 512],
                      ACT.Copy).then_inc(S["hmt_ready"], 1)

                for fq in range(FQ):
                    act_e.wait_ge(S["chunk_free"], it * PAIR_CHUNKS + LOOP_FREE + 4 * fq + 2)
                    if fq >= 2:
                        act_e.wait_ge(S["hm_ready"], it * FQ + fq)
                    A(sg[:, fq % 2, :], ps[:, 2 * (fq % 2) * 512:(2 * (fq % 2) + 1) * 512],
                      ACT.Silu).then_inc(S["silu_done"], 1)
                    if fq:
                        keep_turned(fq - 1)
                keep_turned(FQ - 1)
                act_e.wait_ge(S["chunk_free"], it * PAIR_CHUNKS + LOOP_FREE + PAIR_CHUNKS)
                for hh in range(2):
                    A(y_sb[:, hh * 512:(hh + 1) * 512], ps[:, (6 + hh) * 512:(7 + hh) * 512],
                      ACT.Copy).then_inc(S["y_ready"], 1)
            act_e.wait_ge(S["x_added"], 1 + KT * PAIRS)
            norm_squares(7, "nf2", xT, L)
            for t in range(TT):
                copy_out(("ot", t, 0), out_sb[:, t, 0:512])

        @block.vector
        def _(ve):
            chained = [0]

            def link(ins):
                chained[0] += 1
                ins.then_inc(S["dve_chain"], 1)
                ve.wait_ge(S["dve_chain"], chained[0])

            def wide(v, *shape):
                return v.broadcast_to(list(shape))

            def turned_modulation(tag, nth, vi):
                for c in range(12):
                    t = wait_full(ve, (tag, "T", c))
                    b = cols[:, vi, V1["b_mod"] + 4 * c:V1["b_mod"] + 4 * c + 4]
                    free((tag, "T", c), "D", ve.tensor_tensor(
                        mod_cols[:, 4 * c:4 * c + 4, :], t[:, 0:8].rearrange("p (a b) -> p a b", b=2),
                        wide(b.unsqueeze(2), P, 4, 2), ALU.add))
                wait_freed(ve, (tag, "T", 11))
                for i, (m, r, w) in enumerate(((8, 0, "norm1"), (8, 1, "norm1"), (32, 0, "norm2"))):
                    last = ve.scalar_tensor_tensor(scale_a[:, i, :], mod_cols[:, m:m + 8, r], 1.0,
                                                   cols[:, vi, V1[w]:V1[w] + 8], ALU.add, ALU.mult)
                last.then_inc(S["mods_ready"], 1)

            def norm_scale(m, tag, src, dst, width, weight=None):
                wait_freed(ve, tag)
                if m:
                    ve.wait_ge(S["scaled"], KT * m)
                ve.reciprocal(recip[:, 0:width], root[:, 0:width]).then_inc(S["recip_ready"], 1)
                ve.wait_ge(S["recip_ready"], m + 1)
                for k in range(KT):
                    if weight is None:
                        last = ve.tensor_tensor(dst[:, k, 0:width], src[:, k, 0:width], recip[:, 0:width], ALU.mult)
                    else:
                        last = ve.scalar_tensor_tensor(dst[:, k, 0:width], src[:, k, 0:width], weight(k),
                                                       recip[:, 0:width], ALU.mult, ALU.mult)
                    last.then_inc(S["scaled"], 1)

            def rope_sum(tag, i, g, cs, rsinbuf, rcosbuf, dst):
                t = wait_full(ve, (tag, "swap", i))
                if g == (0 if cs is rope_cs else 8):
                    ve.wait_ge(S["rope_in"], 16 if g == 0 else 32)
                free((tag, "swap", i), "D", ve.tensor_tensor(rsinbuf[:, i % 2, :], t, cs[:, 1, :], ALU.mult))
                wait_freed(ve, (tag, "swap", i))
                ve.wait_ge(S["rope_cos"], g + 1)
                ve.tensor_tensor(dst, rsinbuf[:, i % 2, :], rcosbuf[:, i % 2, :], ALU.add).then_inc(S["q_ready"], 1)

            def centred(name, dst):
                t = wait_full(ve, name).rearrange("p (h e) -> p h e", e=DV)
                link(ve.tensor_reduce(negmean[:, 0:4], t, AX.X, ALU.add))
                link(ve.tensor_scalar(negmean[:, 4:8], negmean[:, 0:4], -1.0 / DV, None, ALU.mult))
                free(name, "D", ve.tensor_tensor(dst.rearrange("p (h e) -> p h e", e=DV), t,
                                                 wide(negmean[:, 4:8].unsqueeze(2), P, 4, DV), ALU.add))

            def merged_tiles(tag):
                merged, gates = merge_views[tag]
                for nq in range(2):
                    for pi, part in enumerate("ab"):
                        for n in range(4):
                            name = (tag, "proj", part, nq, n)
                            wait_freed(ve, (tag, "gate", part, nq, n))
                            t = wait_full(ve, name)
                            dst = merged[:, 4 * nq + n, :] if part == "a" else gates[:, 1, n, :]
                            free(name, "D", ve.tensor_tensor(dst, t, gates[:, pi, n, :], ALU.mult))

            def residual(names, gate):
                for n, name in enumerate(names):
                    t = wait_full(ve, name)
                    free(name, "D", ve.scalar_tensor_tensor(xT[:, n, :], t, mod_cols[:, gate + n, 0:1], xT[:, n, :],
                                                            ALU.mult, ALU.add))

            wait_full(ve, "vecs")
            for i, r in enumerate((104, 88, 88, 104)):
                last = ve.tensor_copy(cols[:, i, 0:r], tile("vecs")[:, i * P:i * P + r])
            free("vecs", "D", last)
            for k in range(1, KT, 2):
                free(("xT", k), "D", ve.tensor_copy(xT[:, k, :], wait_full(ve, ("xT", k))))
            for k in range(1, KT // 2, 2):
                free(("cT", k), "D", ve.tensor_copy(hc[:, 2 * k:2 * k + 2, :].rearrange("p a b -> p (a b)"),
                                                    wait_full(ve, ("cT", k))))
            turned_modulation("mod1", 0, 0)
            norm_scale(0, "n1", xT, hT, L)
            wait_freed(ve, "nc")
            norm_scale(1, "nc", hc, hc, LC)
            ve.wait_ge(S["decay_exp"], 1)
            ve.tensor_scalar(lg, ea, -1.0, None, ALU.mult).then_inc(S["decay_ready"], 1)
            ve.wait_ge(S["decay_ready"], 1)
            for o in (0, 64):
                ve.tensor_copy(qcol[o:o + 64, 0, :], lg[o:o + 64, o // 64:8:2])
                last = ve.tensor_copy(qcol[o:o + 64, 1, :], ea[o:o + 64, 8 + o // 64:16:2])
            link(last)
            ve.tensor_scalar(qcol[:, 2, :], qcol[:, 1, :], -float(L + 1), None, ALU.mult).then_inc(
                S["decay_ready"], 1)
            for i in range(4):
                rope_sum("qk1", i, i, rope_cs, rsin, rcos, obuf[:, 2 + 2 * i, :])
            wait_freed(ve, ("kc", CT - 1))
            ve.wait_ge(S["decay_exp"], 5)
            for d in range(2):
                for t in range(CT):
                    ve.tensor_tensor(kw[:, d, t, :].rearrange("p (h e) -> p h e", e=DK),
                                     kc[:, t, :].rearrange("p (h e) -> p h e", e=DK),
                                     wide(ctxw[:, d, t, :].unsqueeze(2), P, H1, DK), ALU.mult).then_inc(
                                         S["kw_ready"], 1)
            for i in range(4):
                rope_sum("qk1", 4 + i, 4 + i, rope_cs, rsin, rcos, obuf[:, 3 + 2 * i, :])
            ve.wait_ge(S["q_ready"], 8)
            for hh in range(2):
                for t in range(CT):
                    centred(("vc", hh, t), vc[:, t, hh * 512:(hh + 1) * 512])
                for t in range(TT):
                    centred(("v", hh, t), v1[:, t, hh * 512:(hh + 1) * 512])
            t = wait_full(ve, "S")
            free("S", "D", ve.tensor_copy(state[:, :, :, :].rearrange("p d j e -> p (d j e)"), t))
            def finish_head(h):
                wait_freed(ve, ("var", h))
                link(ve.reciprocal(rinv, rinv))
                ve.tensor_tensor(obuf[:, h, :], obuf[:, h, :], rinv, ALU.mult).then_inc(S["o_square"], 1)

            for h in range(H1):
                ve.wait_ge(S["table_ready"], h + 1)
                for i in range(TT):
                    t = wait_full(ve, ("s", h, i))
                    free(("s", h, i), "D", ve.tensor_tensor(
                        probs[:, i, :], t, table[:, h % 2, 384 - i * P:896 - i * P], ALU.mult))
                if h:
                    finish_head(h - 1)
            finish_head(H1 - 1)
            ve.wait_ge(S["o_square"], H1)
            for n in range(KT):
                wait_freed(ve, ("g", n))
                ve.tensor_tensor(obuf[:, n, :], at(10240 + 512 * n, L), obuf[:, n, :], ALU.mult).then_inc(
                    S["g_ready"], 1)
            for g in range(FG):
                free(("z", g), "D", ve.tensor_copy(z[:, g, :], wait_full(ve, ("z", g))))
            merged_tiles("m1")
            residual([("out1", n) for n in range(KT)], 16)
            norm_scale(2, "n2", xT, hT, L)
            for j in range(UPN):
                for n in range(4):
                    f = 2 * j + n % 2 + (FT if n >= 2 else 0)
                    ve.wait_ge(S["conv_mid"], 4 * j + n + 1)
                    t = wait_full(ve, ("up", j, n))
                    link(ve.scalar_tensor_tensor(conv[:, n, 1:L], t[:, 0:L - 1], cols[:, 1, f:f + 1],
                                                 conv[:, n, 1:L], ALU.mult, ALU.add))
                    free(("up", j, n), "D", ve.scalar_tensor_tensor(
                        conv[:, n, 0:L - 1], t[:, 1:L], cols[:, 2, f:f + 1], conv[:, n, 0:L - 1],
                        ALU.mult, ALU.add))
                wait_freed(ve, ("up", j, 3))
                for n in range(2):
                    ve.wait_ge(S["gelu_ready"], 2 * j + n + 1)
                    ve.tensor_tensor(act[:, 2 * j + n, :], gelu_a[:, n, :], conv[:, 2 + n, :],
                                     ALU.mult).then_inc(S["act_ready"], 1)
            residual([("down", n) for n in range(KT)], 40)
            for k in range(1, KT // 2, 2):
                free(("cT2", k), "D", ve.tensor_copy(hc2[:, 2 * k:2 * k + 2, :].rearrange("p a b -> p (a b)"),
                                                     wait_full(ve, ("cT2", k))))
            wait_freed(ve, ("down", KT - 1))
            norm_scale(3, "nf1", xT, xT, L, weight=lambda k: cols[:, 0, V1["final"] + k:V1["final"] + k + 1])
            turned_modulation("mod2", 1, 3)
            ve.wait_ge(S["scaled"], 32)
            norm_scale(4, "n3", xT, hT, L)
            wait_freed(ve, "nc2")
            norm_scale(5, "nc2", hc2, hc2, LC)
            for t in range(TT):
                for hh in range(2):
                    wait_freed(ve, ("va", hh, t))
                    last = ve.bn_stats(stats[:, t, 6 * hh:6 * hh + 6], va[:, t, hh * 512:(hh + 1) * 512])
                link(last)
                ve.bn_aggr(stats[:, t, 12:14], stats[:, t, 0:12]).then_inc(S["ln_stats"], 1)
            ve.wait_ge(S["ln_stats"], TT)
            link(ve.tensor_scalar(stats[:, :, 15:16], stats[:, :, 12:13], -1.0, None, ALU.mult))
            ve.wait_ge(S["ln_root"], 1)
            link(ve.reciprocal(stats[:, :, 14:15], stats[:, :, 14:15]))
            ve.wait_ge(S["stage2_in"], 16 * 4)
            for t in range(TT):
                link(ve.scalar_tensor_tensor(va[:, t, :], va[:, t, :], stats[:, t, 15:16], ln_rows[:, 0, :],
                                             ALU.add, ALU.mult))
                ve.scalar_tensor_tensor(va[:, t, :], va[:, t, :], stats[:, t, 14:15], ln_rows[:, 1, :],
                                        ALU.mult, ALU.add).then_inc(S["ln_ready"], 1)
            for g in range(NG):
                t = wait_full(ve, ("mix", g)).rearrange("p (c q) -> p c q", q=P)
                if g >= 2:
                    ve.wait_ge(S["ya_ready"], g - 1)
                free(("mix", g), "D", ve.tensor_tensor(
                    mixed[:, g % 2, :].rearrange("p (c q) -> p c q", q=P), t,
                    wide(bs_rows[:, g, :].unsqueeze(1), P, TT, P), ALU.add))
            ve.wait_ge(S["ya_ready"], NG)
            for i in range(8):
                rope_sum("q2", i, 8 + i, rope_cs2, rsin2, rcos2, q2[:, i, :])
            for i in range(2):
                rope_sum("k2", i, 16 + i, rope_cs2, rsin2, rcos2, krot[:, i, :])
            ve.wait_ge(S["q_ready"], 18)
            for kv in range(NKV):
                for o in (0, 64):
                    last = ve.tensor_copy(kdup[o:o + 64, kv, :],
                                          krot[64 * (kv % 2):64 * (kv % 2) + 64, kv // 2, :])
            last.then_inc(S["kdup_ready"], 1)
            for i in range(2):
                t = wait_full(ve, ("kc2", i))
                for kv in (2 * i, 2 * i + 1):
                    for o in (0, 64):
                        last = ve.tensor_copy(kcdup[o:o + 64, kv, :],
                                              t[64 * (kv % 2):64 * (kv % 2) + 64, 0:LC])
                free(("kc2", i), "D", last)
            mask_rows = const("mask").rearrange("p (m s) -> p m s", m=2)

            def att_max(i):
                n, h = (i // 4) % 4, 4 * (i // 16) + i % 4
                w = (2 if n in (0, 3) else 3) * P
                t = wait_full(ve, ("as", i))
                if n == 0:
                    v, m = t[:, 384:512], mask_rows[:, 1, :]
                elif n == 3:
                    v, m = t[:, 256:384], mask_rows[:, 0, :]
                else:
                    v, m = t[:, 128:512].rearrange("p (b s) -> p b s", s=P)[:, 0:3:2, :], mask_rows
                link(ve.tensor_tensor(v, v, m, ALU.add))
                link(ve.tensor_reduce(row_top[:, 0:1], t[:, 512 - w:768], AX.X, ALU.max))
                if i >= 4:
                    ve.wait_ge(S["sink_exp"], i - 3)
                ve.tensor_scalar(neg_m[:, i % 4:i % 4 + 1], row_top[:, 0:1], sink[:, h:h + 1], -1.0,
                                 ALU.max, ALU.mult).then_inc(S["row_max"], 1)

            def att_scale(i):
                n = (i // 4) % 4
                w = (2 if n in (0, 3) else 3) * P
                c0 = i % 4
                ve.wait_ge(S["sink_exp"], i + 1)
                link(ve.tensor_tensor(row_top[:, 1:2], den[:, c0:c0 + 1], sink_e[:, c0:c0 + 1], ALU.add))
                link(ve.reciprocal(row_top[:, 2:3], row_top[:, 1:2]))
                p = prob2[:, i % NPB, 384 - w:640]
                ve.tensor_scalar(p, p, row_top[:, 2:3], None, ALU.mult).then_inc(S["p_scaled"], 1)

            def att_out(g):
                kv, n = g // 4, g % 4
                t = wait_full(ve, ("pv", g))
                free(("pv", g), "D", ve.tensor_copy(q2[:, 2 * kv:2 * kv + 2, n * P:(n + 1) * P],
                                                    t[:, 0:256].rearrange("p (a q) -> p a q", a=2)))

            for i in range(NH * TT + 1):
                if i < NH * TT:
                    att_max(i)
                if i:
                    att_scale(i - 1)
                if i % 4 == 2 and i > 4:
                    att_out(i // 4 - 1)
            att_out(NH * TT // 4 - 1)
            merged_tiles("m2")
            residual([("out2", n) for n in range(KT)], 16)
            norm_scale(6, "n4", xT, hT, L)
            for t in range(TT):
                free(("ht", t, 1), "D", ve.tensor_copy(h2_tok[:, t, 512:1024], wait_full(ve, ("ht", t, 1))))
            r = wait_full(ve, "router")[:, 0:TT * NE].rearrange("p (t e) -> p t e", e=NE)
            top = rt_small[:, 0:TT]
            link(ve.tensor_reduce(top, r, AX.X, ALU.max))
            free("router", "D", ve.tensor_tensor(aff, r, wide(top.unsqueeze(2), P, TT, NE), ALU.subtract))
            wait_freed(ve, "router")
            ve.sem_inc(S["row_max"], 1)
            ve.wait_ge(S["exp_done"], 1)
            link(ve.tensor_reduce(rt_small[:, 4:8], aff, AX.X, ALU.add))
            link(ve.reciprocal(rt_small[:, 4:8], rt_small[:, 4:8]))
            ve.tensor_tensor(aff, aff, wide(rt_small[:, 4:8].unsqueeze(2), P, TT, NE), ALU.mult).then_inc(
                S["aff_ready"], 1)
            free("affT", "D", ve.tensor_copy(aff_t[0:NE, :], wait_full(ve, "affT")[0:NE, :]))
            wait_freed(ve, "affT")
            src = aff_t[0:NE, :]
            for i in range(CAP // 8):
                link(ve.max(top8[0:NE, :], src))
                link(ve.match_replace(out=rt_work[0:NE, :], in_to_replace=top8[0:NE, :], in_values=src,
                                      imm_value=-1.0))
                src = rt_work[0:NE, :]
            link(ve.tensor_tensor(chosen[0:NE, :], rt_work[0:NE, :], aff_t[0:NE, :], ALU.not_equal))
            link(ve.tensor_tensor_scan(rank[0:NE, :], chosen[0:NE, :], chosen[0:NE, :], 0.0, ALU.add, ALU.bypass))
            link(ve.tensor_tensor(rank[0:NE, :], rank[0:NE, :], chosen[0:NE, :], ALU.mult))
            ve.tensor_scalar(rank[0:NE, :], rank[0:NE, :], -1.0, None, ALU.add).then_inc(S["rank_ready"], 1)
            free("slotT", "D", ve.tensor_copy(slot_of[:, :, :].rearrange("p a b -> p (a b)"),
                                              wait_full(ve, "slotT")[:, 0:TT * NE]))
            wait_freed(ve, "slotT")
            for t in range(TT):
                s3 = sel[:, t, :].rearrange("p (e j) -> p e j", e=NE)
                ve.tensor_tensor(s3, wide(const("iota").unsqueeze(1), P, NE, CAP),
                                 wide(slot_of[:, t, :].unsqueeze(2), P, NE, CAP), ALU.is_equal).then_inc(
                                     S["sel_ready"], 1)
                ve.wait_ge(S["sel_ready"], t + 1)
                ve.tensor_tensor(wsel[:, t, :].rearrange("p (e j) -> p e j", e=NE), s3,
                                 wide(aff[:, t, :].unsqueeze(2), P, NE, CAP), ALU.mult).then_inc(
                                     S["wsel_ready"], 1)
            for q in range(1, PAIRS, 2):
                free(("wt", q), "D", ve.tensor_copy(wsel_t[:, q, :], wait_full(ve, ("wt", q))))
            ve.sem_inc(S["hm_ready"], 1)
            ve.sem_inc(S["x_added"], 1)
            with ve.Fori(0, PAIRS) as it:
                for fq in range(FQ):
                    ve.wait_ge(S["chunk_free"], it * PAIR_CHUNKS + LOOP_FREE + 4 * fq + 4)
                    ve.wait_ge(S["silu_done"], it * FQ + fq + 1)
                    b = 2 * (fq % 2) + 1
                    ve.tensor_tensor(hmid[:, fq * 512:(fq + 1) * 512], sg[:, fq % 2, :],
                                     ps[:, b * 512:(b + 1) * 512], ALU.mult).then_inc(S["hm_ready"], 1)
                for d in range(KT):
                    ve.wait_ge(S["sc_full"], it * KT + d + 1)
                    b = d % 4
                    ve.scalar_tensor_tensor(xT[:, d, :], ps[:, b * 512:(b + 1) * 512],
                                            mod_cols[:, 40 + d, 0:1], xT[:, d, :],
                                            ALU.mult, ALU.add).then_inc(S["x_added"], 1)
            norm_scale(7, "nf2", xT, xT, L, weight=lambda k: cols[:, 3, V1["final"] + k:V1["final"] + k + 1])
            for t in range(TT):
                free(("ot", t, 1), "D", ve.tensor_copy(out_sb[:, t, 512:1024], wait_full(ve, ("ot", t, 1))))

        @block.gpsimd
        def _(po):
            po.memset(mean_ones[:, 0, :], 1.0 / D).then_inc(S["ones_ready"], 1)
            po.memset(mean_ones[:, 1, :], 1.0 / DV).then_inc(S["ones_ready"], 1)
            po.memset(eps_col, EPS).then_inc(S["ones_ready"], 1)
            po.memset(sc_pad[:, :, :], 0.0).then_inc(S["ones_ready"], 1)
            po.dma_start(w_route[:, :, :], w_router_2[0].rearrange("(k p) e -> p k e", p=P)).then_inc(
                S["router_in"], 16)

            def rope_cosines(tag, i, g, cs, rawbuf, rcosbuf):
                wait_freed(po, (tag, i))
                if g >= 2:
                    po.wait_ge(S["q_ready"], g - 1)
                po.tensor_tensor(rcosbuf[:, i % 2, :], rawbuf[:, i % 2, :], cs[:, 0, :], ALU.mult).then_inc(
                    S["rope_cos"], 1)

            wait_full(po, ("mod1", "T", 11))
            po.dma_start(rope_cs[:, :, :], rope1).then_inc(S["rope_in"], 16)
            po.wait_ge(S["rope_in"], 16)
            for i in range(8):
                rope_cosines("qk1", i, i, rope_cs, raw, rcos)
            wait_full(po, "S")
            po.dma_start(dist_sb, dist[:, 0:896]).then_inc(S["dist_in"], 16)
            po.dma_start(tpos, dist[:, 896:896 + L]).then_inc(S["dist_in"], 16)
            po.wait_ge(S["dist_in"], 32)
            po.wait_ge(S["decay_ready"], 2)

            def table_argument(h):
                if h >= 2:
                    wait_freed(po, ("s", h - 2, TT - 1))
                c0, c1 = (TT - 1) * P, TT * P
                tb, forward, backward = table[:, h % 2, :], lg[:, h:h + 1], ea[:, 8 + h:9 + h]
                po.tensor_scalar(tb[:, 0:c1], dist_sb[:, 0:c1], 0.0, backward, ALU.min, ALU.mult).then_inc(
                    S["pool_chain"], 1)
                if h:
                    po.wait_ge(S["table_arg"], h)
                po.tensor_scalar(band, dist_sb[:, c0:c1], 0.0, forward, ALU.max, ALU.mult).then_inc(
                    S["pool_chain"], 1)
                po.tensor_scalar(tb[:, c1:], dist_sb[:, c1:], forward, None, ALU.mult).then_inc(
                    S["pool_chain"], 1)
                po.wait_ge(S["pool_chain"], 3 * h + 3)
                po.tensor_tensor(tb[:, c0:c1], tb[:, c0:c1], band, ALU.add).then_inc(S["table_arg"], 1)

            def table_diagonal(h):
                po.wait_ge(S["table_exp"], h + 1)
                tb = table[:, h % 2, 384:512]
                po.tensor_tensor(tb, tb, ident, ALU.add).then_inc(S["table_ready"], 1)

            def decay_queries(j):
                for d in range(2):
                    po.wait_ge(S["table_in"], 2 * j + d + 1)
                    po.tensor_tensor(qdec[:, d, :], qdec[:, d, :], obuf[:, 2 + 2 * j, :], ALU.mult).then_inc(
                        S["qdec_ready"], 1)

            table_argument(0)
            table_argument(1)
            table_diagonal(0)
            decay_queries(0)
            table_diagonal(1)
            for h in range(H1):
                if h + 2 < H1:
                    table_argument(h + 2)
                if h % 2 and h + 1 < H1:
                    decay_queries(h // 2 + 1)
                if h + 2 < H1:
                    table_diagonal(h + 2)
            po.wait_ge(S["g_ready"], KT)
            po.dma_start(dftd[:, :, :], dft_dim).then_inc(S["dist_in"], 16)

            def add_parts(tag, base):
                merged, gates = merge_views[tag]
                for nq in range(2):
                    for n in range(4):
                        wait_freed(po, (tag, "proj", "b", nq, n))
                        po.tensor_tensor(merged[:, 4 * nq + n, :], merged[:, 4 * nq + n, :], gates[:, 1, n, :],
                                         ALU.add).then_inc(S["merged_ready"], 1)

            add_parts("m1", 0)
            wait_full(po, ("down", KT - 1))
            po.dma_start(ln_rows[:, 0, :], gmlp_ln_g_2[0].partition_broadcast(P)).then_inc(S["stage2_in"], 16)
            po.dma_start(ln_rows[:, 1, :], gmlp_ln_b_2[0].partition_broadcast(P)).then_inc(S["stage2_in"], 16)
            po.dma_start(bs_rows[:, :, :], b_spatial_2[0].partition_broadcast(P)).then_inc(S["stage2_in"], 16)
            po.dma_start(ws_raw[:, :, :], w_spatial_2[0].rearrange("g p q -> p g q")).then_inc(
                S["stage2_in"], 16)
            for g in range(NG):
                wait_freed(po, ("mix", g))
                wait_freed(po, ("u", g))
                po.tensor_tensor(ug[:, g, :], ug[:, g, :], mixed[:, g % 2, :], ALU.mult).then_inc(
                    S["ya_ready"], 1)
            wait_full(po, ("mix", NG - 1))
            po.dma_start(rope_cs2[:, :, :], rope2).then_inc(S["rope_in"], 16)
            po.wait_ge(S["rope_in"], 32)
            po.wait_ge(S["ya_ready"], NG)
            for i in range(8):
                rope_cosines("q2", i, 8 + i, rope_cs2, raw2, rcos2)
            for i in range(2):
                rope_cosines("k2", i, 16 + i, rope_cs2, raw2, rcos2)
            add_parts("m2", 8)


def rope_table(angles, sign_rows):
    return np.stack([np.cos(angles), np.sin(angles)], 1)


def shape_constants():
    f = np.float32
    c = np.zeros((P, NCONST), f)

    def put(name, v):
        a, b = CONST[name]
        c[:, a:b] = v

    p, n = np.arange(P)[:, None], np.arange(P)[None, :]
    put("ident", p == n)

    def swap(half):
        m = np.zeros((P, P), f)
        for i in range(P):
            if i % (2 * half) < half:
                m[i + half, i] = -1.0
            else:
                m[i - half, i] = 1.0
        return m

    put("swap1", swap(32))
    put("swap2", swap(16))
    mask = np.zeros((P, 2, P), f)
    mask[:, 0] = np.where(n >= p, 0.0, -1e30)
    mask[:, 1] = np.where(n <= p, 0.0, -1e30)
    put("mask", mask.reshape(P, 2 * P))
    put("iota", np.arange(CAP)[None, :])
    put("age", np.concatenate([LC - 1 - p, LC - 1 - P - p, p, P + p], 1))
    sel = np.zeros((P, 2), f)
    for g in range(4):
        sel[32 * g, 0] = sel[32 * g + 1, 1] = 1.0
    put("modsel", sel)

    t = np.arange(L)
    row, col = (t // 64).astype(f), (t % 64).astype(f)
    inv = (f(10000.0) ** (-np.arange(16, dtype=f) / f(16))).astype(f)
    a1 = np.concatenate([row[None] * inv[:, None], col[None] * inv[:, None]], 0)
    a1 = np.tile(a1, (4, 1)).astype(np.float64)
    a2 = np.concatenate([np.tile(row[None] * inv[:, None], (2, 1)), np.tile(col[None] * inv[:, None], (2, 1))], 0)
    a2 = np.tile(a2, (2, 1)).astype(np.float64)
    r1, r2 = rope_table(a1, 32).astype(f), rope_table(a2, 16).astype(f)

    k = np.arange(L)
    w = 2 * np.pi * ((k[:, None] * k[None, :]) % L) / L
    s = 1.0 / np.sqrt(L * 128.0)
    dl = np.stack([np.cos(w), np.sin(w)], 0) * s
    dl = dl.reshape(2, TT, P, L).transpose(2, 0, 1, 3)
    wd = 2 * np.pi * ((p * n) % P) / P
    dd = np.stack([np.cos(wd), -np.sin(wd)], 1)
    dist = np.concatenate([np.arange(896)[None, :] - 384 - p, np.tile(np.arange(1, L + 1), (P, 1))], 1)
    return dict(consts=c, rope1=r1, rope2=r2,
                dft_len=np.ascontiguousarray(dl.reshape(P, 4, 1024)).astype(f),
                dft_dim=dd.astype(f), dist=dist.astype(f))


_INS = ["x", "c", "ctx", "c_ctx", "w_mod", "b_mod", "norm1_w", "w_in", "ret_decay_f", "ret_decay_b",
        "w_ret_out", "w_four_out", "w_branch_gate", "b_branch_gate", "w_out", "norm2_w", "w_up",
        "conv_w", "conv_b", "w_down", "final_norm_w", "c_2", "ctx_2", "c_ctx_2", "w_ada_2", "b_ada_2",
        "norm1_g_2", "w_in_2", "b_merge_gate_2", "gmlp_ln_g_2", "gmlp_ln_b_2", "w_spatial_2",
        "b_spatial_2", "attn_sink_2", "w_proj_a_2", "w_proj_b_2", "w_out_2", "norm2_g_2", "w_router_2",
        "w_exp_gate_2", "w_exp_up_2", "w_exp_down_2", "final_g_2"]


def kernel(**inputs):
    import concourse.bacc as bacc
    from concourse.bass_utils import run_bass_kernel_spmd

    nc = bacc.Bacc("TRN2", target_bir_lowering=False, num_devices=1)
    arrays, args = {}, []
    tensors = {n: np.ascontiguousarray(inputs[n]) for n in _INS} | shape_constants()
    for name, a in tensors.items():
        arrays[f"in_{name}"] = a
        args.append(nc.dram_tensor(f"in_{name}", a.shape, mybir.dt.from_np(a.dtype), kind="ExternalInput").ap())
    out = nc.dram_tensor("out_0", (1, L, D), F32, kind="ExternalOutput").ap()
    build_two_blocks(nc, *args, out)
    r = run_bass_kernel_spmd(nc, [arrays], core_ids=[0])
    return r.results[0]["out_0"]
```

```python
from contextlib import ExitStack

import numpy as np

import concourse.bass as bass
from concourse import mybir

F32 = mybir.dt.float32
F32R = mybir.dt.float32r
ALU = mybir.AluOpType
ACT = mybir.ActivationFunctionType
AX = mybir.AxisListType

P = 128
D = 1024
KT = D // P
L = 512
TT = L // P
LC = 256
CT = LC // P
SLOTS = 6
RAW = 3
HIGH = 3
SLOT = 4096
EPS = 1e-6

H1, DK, DV = 8, 64, 128
FFN = 2816
FT = FFN // P
UPN = FFN // 256
FG = 4

NH, NKV, HD = 16, 4, 64
LAG = 2
NG = 8
AW = 18100
NE, DE, CAP = 16, 2048, 64
PAIRS = NE // 2
FQ = DE // 512
PAIR_CHUNKS = 6 * FQ

V1 = dict(c=0, c_ctx=8, norm1=16, norm2=24, final=32, b_gate=40, b_mod=56)
V2 = dict(w0=0, w1=44)
V3 = dict(w2=0, b=44)
V4 = V1

CONST = {}
_n = 0
for _name, _w in (("ident", 128), ("swap1", 128), ("swap2", 128), ("mask", 256), ("iota", 64),
                  ("age", 4), ("modsel", 2)):
    CONST[_name] = (_n, _n + _w)
    _n += _w
NCONST = _n


class Banks:

    def __init__(self):
        self.tiles, self.where, self.units = [], {}, []

    def add(self, name, by, width=1):
        if width == 2 and len(self.units) % 2:
            self.units.append(None)
        i = len(self.tiles)
        assert name not in self.where, name
        nth = sum(1 for t in self.tiles if t[1] == by) + 1
        self.tiles.append((name, by, len(self.units), nth, width))
        self.where[name] = i
        self.units += [i] * width

    def bank(self, name):
        return self.tiles[self.where[name]][2] % 8

    def before(self, name):
        _, _, u, _, w = self.tiles[self.where[name]]
        need = {}
        for v in range(u, u + w):
            for back in range(v - 8, -1, -8):
                if self.units[back] is not None:
                    _, by, _, nth, _ = self.tiles[self.units[back]]
                    need[by] = max(need.get(by, 0), nth)
                    break
        return sorted(need.items())


def plan_banks():
    b = Banks()
    b.add("vecs", "D")
    for k in range(KT):
        b.add(("xT", k), "AD"[k % 2])
    for k in range(KT // 2):
        b.add(("cT", k), "AD"[k % 2])

    def norm(tag):
        b.add(tag, "A")
        b.add((tag, "wide"), "D")

    def mod_step(tag, c, first):
        if c > first:
            b.add((tag, "T", c - 1), "D")
        b.add((tag, c), "A")

    def merge(tag):
        c = 4
        for nq in range(2):
            for part in "ab":
                for kind, by in (("gate", "A"), ("proj", "D")):
                    for n in range(4):
                        b.add((tag, kind, part, nq, n), by)
                    if tag == "m1":
                        mod_step("mod1", c, 4)
                        c += 1
        if tag == "m1":
            b.add(("mod1", "T", 11), "D")

    def rope(tag, n):
        for i in range(n + 1):
            if i < n:
                b.add((tag, i), "A")
            if i:
                b.add((tag, "swap", i - 1), "D")

    norm("n1")
    norm("nc")
    for c in range(4):
        mod_step("mod1", c, 0)
    b.add(("mod1", "T", 3), "D")
    for i in range(4):
        b.add(("qk1", i), "A")
    for i in range(4):
        b.add(("qk1", "swap", i), "D")
    for t in range(CT):
        b.add(("kc", t), "A")
    for i in range(5):
        if i < 4:
            b.add(("qk1", 4 + i), "A")
        if i:
            b.add(("qk1", "swap", 3 + i), "D")
    for hh in range(2):
        for t in range(CT):
            b.add(("vc", hh, t), "D")
        for t in range(TT):
            b.add(("v", hh, t), "D")
    b.add("S", "D", 2)
    for h in range(H1 + 1):
        if h:
            b.add(("o", h - 1), "A")
        if h < H1:
            for i in range(TT):
                b.add(("s", h, i), "D")
        if h:
            b.add(("var", h - 1), "A")
    for n in range(KT):
        b.add(("g", n), "A")
    for t in range(TT):
        b.add(("f", t), "A")
    for g in range(FG):
        for m in range(2):
            b.add(("fa", g, m), "A")
    for g in range(FG):
        b.add(("z", g), "D")
    merge("m1")
    for n in range(KT):
        b.add(("out1", n), "D")
    norm("n2")
    for j in range(UPN):
        for n in range(4):
            b.add(("up", j, n), "D")
        mod_step("mod2", j, 0)
    mod_step("mod2", 11, 0)
    b.add(("mod2", "T", 11), "D")
    for n in range(KT):
        b.add(("down", n), "D")
    b.add("nf1", "A")
    for k in range(KT // 2):
        b.add(("cT2", k), "AD"[k % 2])
    b.add(("nf1", "wide"), "D")
    norm("n3")
    for n in range(KT):
        if n == 4:
            b.add("nc2", "A")
        b.add(("u", n), "A")
        if n == 4:
            b.add(("nc2", "wide"), "D")
    for hh in range(2):
        for t in range(TT):
            b.add(("va", hh, t), "A")
    b.add(("ws", 0), "A")
    b.add(("ws", 1), "A")
    for g in range(NG):
        b.add(("mix", g), "D")
    rope("q2", 8)
    for i in range(3):
        if i < 2:
            b.add(("k2", i), "A")
        if i:
            b.add(("k2", "swap", i - 1), "D")
    for t in range(TT):
        b.add(("vb", t), "A")
    for i in range(2):
        b.add(("kc2", i), "D")
    for t in range(CT):
        b.add(("vc2", t), "A")
    for i in range(NH * TT + LAG):
        if i < NH * TT:
            b.add(("as", i), "A", 2)
        if i >= LAG:
            if (i - LAG) % 4 == 0 and i > LAG:
                b.add(("pv", (i - LAG) // 4 - 1), "D")
            b.add(("at", i - LAG), "A", 2)
    b.add(("pv", NH * TT // 4 - 1), "D")
    merge("m2")
    for n in range(KT):
        b.add(("out2", n), "D")
    norm("n4")
    b.add("router", "D")
    for t in range(TT):
        for hh in range(2):
            b.add(("ht", t, hh), "AD"[hh])
    b.add("affT", "D")
    b.add("slotT", "D")
    for q in range(PAIRS):
        b.add(("wt", q), "AD"[q % 2])
    norm("nf2")
    for t in range(TT):
        for hh in range(2):
            b.add(("ot", t, hh), "AD"[hh])
    return b


def build_two_blocks(nc, x, c, ctx, c_ctx, w_mod, b_mod, norm1_w, w_in, ret_decay_f, ret_decay_b,
                     w_ret_out, w_four_out, w_branch_gate, b_branch_gate, w_out, norm2_w, w_up,
                     conv_w, conv_b, w_down, final_norm_w, c_2, ctx_2, c_ctx_2, w_ada_2, b_ada_2,
                     norm1_g_2, w_in_2, b_merge_gate_2, gmlp_ln_g_2, gmlp_ln_b_2, w_spatial_2,
                     b_spatial_2, attn_sink_2, w_proj_a_2, w_proj_b_2, w_out_2, norm2_g_2,
                     w_router_2, w_exp_gate_2, w_exp_up_2, w_exp_down_2, final_g_2,
                     consts, rope1, rope2, dft_len, dft_dim, dist, out):
    banks = plan_banks()
    es = ExitStack()
    with es:
        def sb(name, *shape):
            return es.enter_context(nc.sbuf_tensor(name, [P, *shape], F32))

        def two_types(name, *shape):
            with nc.sbuf_tensor(name + "_r", [P, *shape], F32R) as r:
                pass
            return sb(name, *shape), r

        slots, slots_r = zip(*(two_types(f"weights{i}", SLOT) for i in range(SLOTS)))
        hT, hT_r = two_types("hT", KT, L)
        arena, arena_r = two_types("arena", AW)
        xT = sb("xT", KT, L)
        cst = sb("cst", NCONST)
        mean_ones = sb("mean_ones", 2, P)
        cols = sb("cols", 4, P)
        mod_cols, mod_cols2 = sb("mod_cols", 48, 2), sb("mod_cols2", 48, 2)
        scale_a = sb("scale_a", 3, KT)
        sc_pad = sb("sc_pad", KT, 32)
        small = sb("small", 160)
        w_route = sb("w_route", KT, NE)
        ps = es.enter_context(nc.psum_tensor("ps", [P, 8 * 512], F32))

        def const(name):
            a, b = CONST[name]
            return cst[:, a:b]

        ident = const("ident")
        eps_col = small[:, 0:1]

        def at(off, *dims, rounded=False):
            n = int(np.prod(dims))
            assert off + n <= AW, (off, n)
            v = (arena_r if rounded else arena)[:, off:off + n]
            if len(dims) == 2:
                v = v.rearrange("p (a b) -> p a b", a=dims[0])
            if len(dims) == 3:
                v = v.rearrange("p (a b c) -> p a b c", a=dims[0], b=dims[1])
            if len(dims) == 4:
                v = v.rearrange("p (a b c d) -> p a b c d", a=dims[0], b=dims[1], c=dims[2])
            return v

        def slot(i, k):
            return slots[i % SLOTS][:, :].rearrange("p (k n) -> p k n", k=k)

        names = """landed0 landed1 landed2 landed3 landed4 landed5 chunk_free tile_full freed_a freed_d
            consts_in vecs_in bcast_in dve_chain act_chain pool_chain ones_ready silu_ready mods_ready
            high_ready low_ready loads_turn merged_high merged_low act_high act_low h_plain h_rounded h4_ready
            sq_ready root_ready recip_ready scaled h_ready raw_done rope_cos rope_sin rope_in q_ready
            kw_ready vc_ready decay_ready qdec_ready dist_in table_in table_arg table_exp table_ready table_used
            o_square o_sq_used o_root p_ready g_silu g_ready gate_sig merged_ready conv_mid conv_done gelu_ready act_ready
            ln_ready ln_stats ln_root lnrow_in mix_add ya_ready row_max exp_done p_scaled sink_exp pt_ready kdup_ready
            h2t_ready router_in aff_ready rank_ready sel_ready wsel_ready
            xe_full xe_ready g_full silu_done hm_ready hmt_full hmt_ready y_full y_ready sc_full x_added
            out_full out_ready stored x_final decay_exp stage2_in""".split()
        S = {n: es.enter_context(nc.semaphore(n)) for n in names}
        FREED = {"A": S["freed_a"], "D": S["freed_d"]}

        def tile(name, width=None):
            w = banks.tiles[banks.where[name]][4]
            k = banks.bank(name)
            return ps[:, k * 512:k * 512 + 512 * w]

        filled = []

        def claim(pe, name):
            for by, count in banks.before(name):
                pe.wait_ge(FREED[by], count)
            return tile(name)

        def fill(name, last):
            assert banks.where[name] == len(filled), name
            filled.append(name)
            last.then_inc(S["tile_full"], 1)

        def wait_full(eng, name):
            eng.wait_ge(S["tile_full"], banks.where[name] + 1)
            return tile(name)

        evacuated = {"A": 0, "D": 0}

        def free(name, by, last):
            _, b, _, nth, _ = banks.tiles[banks.where[name]]
            evacuated[by] += 1
            assert b == by and nth == evacuated[by], name
            if last is None:
                nc.vector.sem_inc(FREED[by], 1)
            else:
                last.then_inc(FREED[by], 1)

        def wait_freed(eng, name):
            _, by, _, nth, _ = banks.tiles[banks.where[name]]
            eng.wait_ge(FREED[by], nth)

        def kmaj(w, n0, n1):
            return w[:, n0:n1].rearrange("(k p) n -> p k n", p=P)

        chunks = []
        chunk_at = {}

        def chunk(name, *parts):
            chunk_at[name] = len(chunks)
            chunks.append(parts)

        chunk("x", x[0].rearrange("(t p) d -> p t d", p=P))
        chunk("ctx", ctx[0].rearrange("(t p) d -> p t d", p=P))
        def mod1(i):
            chunk(("mod1", i), kmaj(w_mod[0], 512 * i, 512 * i + 512))

        def in1(i):
            chunk(("in1", i), kmaj(w_in[0], 512 * i, 512 * i + 512))

        for i in range(3):
            mod1(i)
        in1(0)
        mod1(3)
        for i in range(1, 7):
            in1(i)
        chunk("dft", dft_len)
        for nq in range(2):
            o = 512 * nq
            chunk(("m1", "gate", "a", nq), kmaj(w_branch_gate[0], D + o, D + o + 512))
            mod1(4 + 4 * nq)
            chunk(("m1", "proj", "a", nq), kmaj(w_four_out[0], o, o + 512))
            mod1(5 + 4 * nq)
            chunk(("m1", "gate", "b", nq), kmaj(w_branch_gate[0], o, o + 512))
            mod1(6 + 4 * nq)
            chunk(("m1", "proj", "b", nq), kmaj(w_ret_out[0], o, o + 512))
            mod1(7 + 4 * nq)
        for nq in range(2):
            chunk(("out1", nq), kmaj(w_out[0], 512 * nq, 512 * nq + 512))
        for j in range(UPN):
            chunk(("up", j), kmaj(w_up[0], 256 * j, 256 * j + 256),
                  kmaj(w_up[0], FFN + 256 * j, FFN + 256 * j + 256))
            for i in ((j,) if j < UPN - 1 else (j, j + 1)):
                chunk(("mod2", i), kmaj(w_ada_2[0], 512 * i, 512 * i + 512))
        for j in range(6):
            part = w_down[0][512 * j:min(512 * j + 512, FFN), :].rearrange("(k p) n -> p k n", p=P)
            if j < 5:
                chunk(("down", j), part)
            else:
                chunk(("down", j), part, ctx_2[0].rearrange("(t p) d -> p t d", p=P))
        for i in range(7):
            chunk(("in2", i), kmaj(w_in_2[0], 512 * i, 512 * i + 512))
        for nq in range(2):
            o = 512 * nq
            chunk(("m2", "gate", "a", nq), kmaj(w_in_2[0], 3584 + o, 3584 + o + 512))
            chunk(("m2", "proj", "a", nq), kmaj(w_proj_a_2[0], o, o + 512))
            chunk(("m2", "gate", "b", nq), kmaj(w_in_2[0], 3584 + D + o, 3584 + D + o + 512))
            chunk(("m2", "proj", "b", nq), kmaj(w_proj_b_2[0], o, o + 512))
        for nq in range(2):
            chunk(("out2", nq), kmaj(w_out_2[0], 512 * nq, 512 * nq + 512))
        NCH = len(chunks)
        order = {n: name for name, n in chunk_at.items()}
        assert NCH % RAW == 0
        split = [n for n, name in enumerate(chunk_at) if name[0] in ("in1", "in2", "up", "down", "out1", "out2") or name[1:2] == ("gate",)]

        def landed(eng, name):
            n = chunk_at[name]
            loads = sum(len(chunks[m]) for m in range(n % RAW, n + 1, RAW))
            eng.wait_ge(S[f"landed{n % RAW}"], 16 * loads)
            return n % RAW

        def split_words(i):
            return SLOT // 2 if order[split[i]] == ("down", 5) else SLOT

        def high_slot(i):
            return HIGH + i % 2

        def next_splits(issued, name):
            n = chunk_at[name]
            ahead = [i for i, m in enumerate(split) if m > n][:1]
            upto = ahead[0] + 1 if ahead and split[ahead[0]] <= n + 2 else len([m for m in split if m <= n])
            todo = range(issued[0], upto)
            issued[0] = max(issued[0], upto)
            return todo

        last_tile = {"x": ("xT", 7), "ctx": ("cT", 3), "dft": ("fa", 3, 1), ("down", 5): ("cT2", 3),
                     ("in1", 0): ("qk1", 3), ("in1", 1): ("qk1", 7), ("in1", 2): ("v", 0, 3),
                     ("in1", 3): ("v", 1, 3), ("in1", 4): ("g", 3), ("in1", 5): ("g", 7), ("in1", 6): ("f", 3),
                     ("in2", 0): ("u", 3), ("in2", 1): ("u", 7), ("in2", 2): ("va", 0, 3),
                     ("in2", 3): ("va", 1, 3), ("in2", 4): ("q2", 3), ("in2", 5): ("q2", 7),
                     ("in2", 6): ("vc2", 1)}
        for i in range(12):
            last_tile["mod1", i], last_tile["mod2", i] = ("mod1", i), ("mod2", i)
        for nq in range(2):
            for tag in ("m1", "m2"):
                for part in "ab":
                    for kind in ("gate", "proj"):
                        last_tile[tag, kind, part, nq] = (tag, kind, part, nq, 3)
            last_tile["out1", nq], last_tile["out2", nq] = ("out1", 4 * nq + 3), ("out2", 4 * nq + 3)
        for j in range(UPN):
            last_tile["up", j] = ("up", j, 3)

        def wait_spent(sp, n):
            if order[n] in last_tile:
                sp.wait_ge(S["tile_full"], banks.where[last_tile[order[n]]] + 1)
            else:
                sp.wait_ge(S["chunk_free"], order[n][1] + 1)

        LOOP_FREE = 5

        merge_views = {"m1": (at(5120, KT, L), at(13696, 2, 4, L)),
                       "m2": (at(8192, KT, L), at(12288, 2, 4, L))}
        norm_tags = ["n1", "nc", "n2", "nf1", "n3", "nc2", "n4", "nf2"]
        sq8 = at(0, KT, L)
        merged_low = {"m1": at(5120, KT, L, rounded=True), "m2": at(8192, KT, L, rounded=True)}
        sqc = at(4096, KT, LC)
        root, recip = small[:, 40:44], small[:, 44:48]
        rows_v = at(5120, 4, P)
        m_sbs = [at(5632, 2, L), at(9216, 2, L), at(16384, 2, L)]

        def m_sb(tag, c):
            return m_sbs[2 if tag == "mod2" else 1 if c >= 4 else 0][:, c % 2, :]

        h_high = slots_r[SLOTS - 1][:, :].rearrange("p (k n) -> p k n", k=KT)
        h_low = hT_r
        h_parts = (lambda k, a, b: h_high[:, k, a:b], lambda k, a, b: h_low[:, k, a:b])

        hc = at(10240, KT, LC)
        hc_highs = [at(0, 4, LC, rounded=True), at(9216, 4, LC, rounded=True)]
        hc_low = at(10240, KT, LC, rounded=True)
        hc_parts = (lambda k, a, b: hc_highs[k // 4][:, k % 4, a:b], lambda k, a, b: hc_low[:, k, a:b])
        obuf = at(0, 10, L)
        v1 = at(5120, TT, D)
        rope_cs = at(5120, 2, L)
        raw = at(6144, 2, L)
        rcos = at(7168, 2, L)
        rsin = at(8192, 2, L)
        kc = at(12288, CT, 512)
        kw = at(13312, 2, CT, 512)
        vc = at(15360, CT, D)
        state = at(9216, 2, 4, P)
        dist_sb = at(10240, 896)
        tpos = at(11136, L)
        probs = at(11648, 4, L)
        table = at(13696, 2, 896)
        qdec = at(15488, 2, L)
        osq = at(16512, L)
        band = at(17600, P)
        rinv = at(17024, L)
        f_tok = at(5120, TT, 512)
        fa = at(7168, FG, 2, L)
        z = at(11264, FG, L)
        dftd = at(13312, 2, P)
        act = at(0, FT, L)
        act_low_v = at(0, FT, L, rounded=True)
        act_highs = [at(14336, 4, L, rounded=True), h_high, h_low, at(11264, 2, L, rounded=True)]

        def act_high(k):
            return act_highs[(k + 4) // 8][:, k if k < 4 else (k - 4) % 8, :]

        conv = at(11264, 4, L)
        gelu_a = at(13312, 2, L)
        hc2 = at(14336, KT, LC)
        hc2_slot = high_slot(split.index(chunk_at["in2", 5]))
        hc2_high = slots_r[hc2_slot][:, 0:KT * LC].rearrange("p (k n) -> p k n", k=KT)
        hc2_low = at(14336, KT, LC, rounded=True)
        hc2_parts = (lambda k, a, b: hc2_high[:, k, a:b], lambda k, a, b: hc2_low[:, k, a:b])
        ug = at(0, KT, L)
        va = at(4096, TT, D)
        ln_rows = at(8192, 2, D)
        bs_rows = at(10240, NG, P)
        ws_t = at(11264, NG, P)
        ws_raw = at(12288, NG, P)
        mixed = at(13312, 2, L)
        stats = at(16384, TT, 16)
        q2 = at(4096, KT, L)
        kdup = at(8192, NKV, L)
        krot = at(10240, 2, L)
        rope_cs2 = at(11264, 2, L)
        raw2 = at(12288, 2, L)
        rcos2 = at(13312, 2, L)
        rsin2 = at(16384, 2, L)
        vb = at(11264, TT, NKV * HD)
        kcdup = at(12288, NKV, LC)
        vcx = at(10240, CT, NKV * HD)
        NPB = 3
        prob2 = at(13312, NPB, 640)
        prob_t = at(15232, 5, 4, P)
        h2_tok = at(0, TT, D)
        sel = at(4096, TT, D)
        wsel_t = at(8192, PAIRS, L)
        xe = at(12288, KT, P)
        y_sb = at(13312, D)
        sg = at(14336, 2, 512)
        rt_work = at(15360, L)
        aff_t = at(15872, L)
        rank = at(16384, L)
        chosen = at(16896, L)
        aff = at(17408, TT, NE)
        rt_small = at(17472, 64)
        slot_of = at(17536, TT, NE)
        top8 = at(17600, 8)
        wsel = hT[:, :, :].rearrange("p a b -> p (a b)").rearrange("p (t n) -> p t n", t=TT)
        hmid = hT[:, 0:4, :].rearrange("p a b -> p (a b)")
        hmid_t = hT[:, 4:8, :].rearrange("p a b -> p (a b)").rearrange("p (k n) -> p k n", k=16)
        out_sb = at(0, TT, D)
        decay = small[:, 8:24]
        sink = small[:, 24:40]
        ea = small[:, 64:80]
        lg = small[:, 80:96]
        qcol = small[:, 96:108].rearrange("p (a b) -> p a b", a=3)
        ctxw = small[:, 112:144].rearrange("p (d t h) -> p d t h", d=2, t=CT)
        neg_m = small[:, 144:148]
        den = small[:, 148:152]
        sink_e = small[:, 152:156]
        negmean = at(17536, 8)
        row_top = at(17792, 4)

        block = es.enter_context(nc.Block())

        @block.sync
        def _(sp):
            sp.dma_start(cst[:, :], consts).then_inc(S["consts_in"], 16)
            rows = [
                (0, V1["c"], c), (0, V1["c_ctx"], c_ctx), (0, V1["norm1"], norm1_w), (0, V1["norm2"], norm2_w),
                (0, V1["final"], final_norm_w), (0, V1["b_gate"], b_branch_gate), (0, V1["b_mod"], b_mod),
                (3, V4["c"], c_2), (3, V4["c_ctx"], c_ctx_2), (3, V4["norm1"], norm1_g_2),
                (3, V4["norm2"], norm2_g_2), (3, V4["final"], final_g_2), (3, V4["b_gate"], b_merge_gate_2),
                (3, V4["b_mod"], b_ada_2), (2, V3["b"], conv_b)]
            for i, r, v in rows:
                flat = v if len(v.shape) == 1 else v.rearrange("a n -> (a n)")
                n = flat.shape[0] // P
                sp.dma_start(rows_v[r:r + n, i, :], flat.rearrange("(r p) -> r p", p=P)).then_inc(S["vecs_in"], 16)
            for i, r, t in ((1, V2["w0"], 0), (1, V2["w1"], 1), (2, V3["w2"], 2)):
                sp.dma_start(rows_v[r:r + 44, i, :],
                             conv_w[0, t].rearrange("(r p) -> r p", p=P)).then_inc(S["vecs_in"], 16)
            for k, v in enumerate((ret_decay_f[0], ret_decay_b[0])):
                sp.dma_start(small[:, 8 + 8 * k:16 + 8 * k], v.partition_broadcast(P)).then_inc(S["bcast_in"], 16)
            sp.dma_start(small[:, 24:40], attn_sink_2[0].partition_broadcast(P)).then_inc(S["bcast_in"], 16)
            for n in range(NCH):
                if n >= RAW:
                    wait_spent(sp, n - RAW)
                sl = n % RAW
                src = chunks[n]
                if len(src) == 1 or src[0].shape[2] == D:
                    o = 0
                    for part in src:
                        k, w = part.shape[1], part.shape[2]
                        sp.dma_start(slots[sl][:, o:o + k * w].rearrange("p (k n) -> p k n", k=k),
                                     part).then_inc(S[f"landed{sl}"], 16)
                        o += k * w
                else:
                    v = slot(sl, 8)
                    sp.dma_start(v[:, :, 0:256], src[0]).then_inc(S[f"landed{sl}"], 16)
                    sp.dma_start(v[:, :, 256:512], src[1]).then_inc(S[f"landed{sl}"], 16)
            def gate_up(w, it, e, fq):
                return w[0, e:, :, :][bass.ds(it * 2, 1), :, 512 * fq:512 * fq + 512].rearrange("a (k p) n -> p (a k) n", p=P)

            def down(it, e, kq):
                return w_exp_down_2[0, e:, :, :][bass.ds(it * 2, 1), 512 * kq:512 * kq + 512, :].rearrange(
                    "a (k p) n -> p (a k) n", p=P)

            def load(it, m, ahead=0):
                if m < 4 * FQ:
                    fq, gu, e = m // 4, m // 2 % 2, m % 2
                    src = gate_up((w_exp_gate_2, w_exp_up_2)[gu], it, 2 * ahead + e, fq)
                else:
                    kq, e = (m - 4 * FQ) // 2, m % 2
                    src = down(it, 2 * ahead + e, kq)
                sp.dma_start(slot(m, 8 if m < 4 * FQ else 4), src).then_inc(S[f"landed{m % SLOTS}"], 16)

            def load_when_free(it, m, ahead=0):
                sp.wait_ge(S["chunk_free"], it * PAIR_CHUNKS + (ahead * PAIR_CHUNKS + LOOP_FREE + m - SLOTS + 1))
                if m == 4 * FQ:
                    sp.sem_inc(S["loads_turn"], 1)
                load(it, m, ahead)

            for m in range(RAW):
                wait_spent(sp, NCH - RAW + m)
                load(0, m)
            for i in sorted(range(len(split) - 2, len(split)), key=high_slot):
                wait_spent(sp, split[i])
                load(0, high_slot(i))
            load(0, SLOTS - 1)
            with sp.Fori(0, PAIRS - 1) as it:
                for m in range(SLOTS, PAIR_CHUNKS):
                    load_when_free(it, m)
                for m in range(SLOTS):
                    load_when_free(it, m, 1)
            for m in range(SLOTS, PAIR_CHUNKS):
                load_when_free(PAIRS - 1, m)
            for t in range(TT):
                for hh in range(2):
                    wait_freed(sp, ("ot", t, hh))
                sp.dma_start(out[0, t * P:(t + 1) * P, :], out_sb[:, t, :]).then_inc(S["stored"], 16)
            sp.wait_ge(S["stored"], 16 * TT)

        @block.tensor
        def _(pe):
            def parts_of(cname, kt=KT):
                if chunk_at[cname] in split:
                    i = split.index(chunk_at[cname])
                    pe.wait_ge(S["low_ready"], i + 1)
                    sl = chunk_at[cname] % RAW, high_slot(i)
                    low, high = (slots_r[q][:, 0:split_words(i)].rearrange("p (k n) -> p k n", k=kt) for q in sl)
                    return high, low
                return (slots[landed(pe, cname)][:, 0:kt * 512].rearrange("p (k n) -> p k n", k=kt),)

            def product(t, w, x, k, kt, w_range, x_range, w_first, kw=None):
                pairs = [(0, 0), (0, 1), (1, 0)] if len(w) == 2 else [(0, 0)]
                for n, (i, j) in enumerate(pairs):
                    a, b = w[i][:, k if kw is None else kw, w_range[0]:w_range[1]], x[j](k, *x_range)
                    last = pe.matmul(t, a if w_first else b, b if w_first else a,
                                     start=(k == 0 and n == 0), stop=(k == kt - 1 and n == len(pairs) - 1))
                return last

            def feature_tiles(cname, tnames, src, kt=KT, width=512, c0=0):
                w = parts_of(cname, kt)
                for n, tn in enumerate(tnames):
                    t = claim(pe, tn)[:, 0:width]
                    for k in range(kt):
                        last = product(t, w, src, k, kt, (c0 + n * P, c0 + n * P + P), (0, width), True)
                    fill(tn, last)

            def first_tiles(cname, tnames, x, sem, ready):
                w = parts_of(cname)
                ts = [claim(pe, tn) for tn in tnames]
                for k in range(KT):
                    pe.wait_ge(S[sem], ready + k + 1)
                    for n, t in enumerate(ts):
                        last = product(t, w, x, k, KT, (n * P, n * P + P), (0, L), True)
                        if k == KT - 1:
                            fill(tnames[n], last)

            def token_tiles(cname, tnames, src, c0=0, width=512):
                w = parts_of(cname)
                for t, tn in enumerate(tnames):
                    o = claim(pe, tn)[:, 0:width]
                    for k in range(KT):
                        last = product(o, w, src, k, KT, (c0, c0 + width), (t * P, t * P + P), False)
                    fill(tn, last)

            def turn(name, parts):
                t = claim(pe, name)
                for o, src in parts:
                    rows = src.shape[0]
                    last = pe.transpose(t[:, o:o + rows], src, ident[0:rows, 0:rows])
                fill(name, last)

            def norm_step(m, tag, width, k):
                t = claim(pe, tag) if k == 0 else tile(tag)
                pe.wait_ge(S["sq_ready"], KT * m + k + 1)
                for j in range(width // P):
                    last = pe.matmul(t[:, j:j + 1], (sqc if m == 5 else sq8)[:, k, j * P:(j + 1) * P], mean_ones[:, 0, 0:1],
                                     start=(k + j == 0), stop=(k == KT - 1 and j == width // P - 1))
                if k == KT - 1:
                    fill(tag, last)

            def norm(m, tag, width, between=None, k0=0):
                for k in range(k0, KT):
                    norm_step(m, tag, width, k)
                if between:
                    between()
                pe.wait_ge(S["recip_ready"], m + 1)
                t = claim(pe, (tag, "wide"))
                for j in range(width // P):
                    last = pe.matmul(t[:, j * P:(j + 1) * P], recip[:, j:j + 1].broadcast_to([P, P]), ident,
                                     start=True, stop=True)
                fill((tag, "wide"), last)

            def mod_turn(tag, c):
                wait_freed(pe, (tag, c))
                t = claim(pe, (tag, "T", c))
                for j in range(4):
                    last = pe.matmul(t[:, 2 * j:2 * j + 2], m_sb(tag, c)[:, j * P:(j + 1) * P],
                                     const("modsel"), start=True, stop=True)
                fill((tag, "T", c), last)

            def mod_step(tag, c, first):
                if c > first:
                    mod_turn(tag, c - 1)
                w = slot(landed(pe, (tag, c)), KT)
                t = claim(pe, (tag, c))
                for k in range(KT):
                    g = 32 * (k % 4)
                    last = pe.matmul(t[g:g + 32, :], sc_pad[:, k, :], w[:, k, :],
                                     start=(k < 4), stop=(k >= 4), tile_position=(0, g))
                fill((tag, c), last)

            def swap(tag, i, matrix, rawbuf):
                wait_freed(pe, (tag, i))
                t = claim(pe, (tag, "swap", i))
                fill((tag, "swap", i), pe.matmul(t, const(matrix), rawbuf[:, i % 2, :], start=True, stop=True))

            def roped(tag, cname, i0, n, matrix, rawbuf, first=None):
                for i in range(i0, i0 + n):
                    feature_tiles(cname, [(tag, i)], h_parts, c0=(i - i0) * P)
                    if i > i0 or first is not None:
                        if i > i0:
                            swap(tag, i - 1, matrix, rawbuf)
                        else:
                            first()

            def plain(v):
                return (lambda k, a, b: v[:, k, a:b],)

            def merge(tag, src_a, kt_a, src_b, kt_b):
                c = 4
                for nq in range(2):
                    for part, src, kt in (("a", src_a, kt_a), ("b", src_b, kt_b)):
                        for kind, x, k in (("gate", h_parts, KT), ("proj", plain(src), kt)):
                            feature_tiles((tag, kind, part, nq), [(tag, kind, part, nq, n) for n in range(4)], x, kt=k)
                            if tag == "m1":
                                mod_step("mod1", c, 4)
                                c += 1
                if tag == "m1":
                    mod_turn("mod1", 11)

            def out_proj(tag, mtag, m, norm_tag):
                low = merged_low[mtag]
                x = (h_parts[0], lambda k, a, b: low[:, k, a:b])
                first_tiles((tag, 0), [(tag, n) for n in range(4)], x, "merged_low", 0 if mtag == "m1" else KT)
                for n in range(4, KT):
                    feature_tiles((tag, 1), [(tag, n)], x, c0=n % 4 * P)
                    for k in {4: (0, 1, 2), 5: (3,), 6: (4,), 7: (5,)}[n]:
                        norm_step(m, norm_tag, L, k)

            pe.wait_ge(S["consts_in"], 16)
            pe.wait_ge(S["vecs_in"], 16 * 18)
            turn("vecs", [(i * P, rows_v[0:r, i, :]) for i, r in enumerate((104, 88, 88, 104))])
            w = slot(landed(pe, "x"), TT)
            for k in range(KT):
                turn(("xT", k), [(t * P, w[:, t, k * P:(k + 1) * P]) for t in range(TT)])
            w = slot(landed(pe, "ctx"), TT)
            for k in range(KT // 2):
                turn(("cT", k), [(j * LC + t * P, w[:, t, (2 * k + j) * P:(2 * k + j + 1) * P])
                                 for j in range(2) for t in range(CT)])
            pe.wait_ge(S["ones_ready"], 4)
            norm(0, "n1", L)
            norm(1, "nc", LC)
            pe.wait_ge(S["silu_ready"], 2)
            for c in range(4):
                mod_step("mod1", c, 0)
            mod_turn("mod1", 3)
            first_tiles(("in1", 0), [("qk1", i) for i in range(4)], h_parts, "h_ready", 0)
            for i in range(4):
                swap("qk1", i, "swap1", raw)
            pe.wait_ge(S["h_ready"], 16)
            token_tiles(("in1", 1), [("kc", t) for t in range(CT)], hc_parts)
            roped("qk1", ("in1", 1), 4, 4, "swap1", raw)
            swap("qk1", 7, "swap1", raw)
            for hh in range(2):
                token_tiles(("in1", 2 + hh), [("vc", hh, t) for t in range(CT)], hc_parts)
                token_tiles(("in1", 2 + hh), [("v", hh, t) for t in range(TT)], h_parts)
            pe.wait_ge(S["kw_ready"], 4)
            wait_freed(pe, ("vc", 1, CT - 1))
            t = claim(pe, "S").rearrange("p (d j e) -> p d j e", d=2, j=4)
            for d in range(2):
                for h in range(H1):
                    o = 64 * (h % 2)
                    for tt in range(CT):
                        last = pe.matmul(t[o:o + 64, d, h // 2, :], kw[:, d, tt, h * DK:(h + 1) * DK],
                                         vc[:, tt, h * DV:(h + 1) * DV], start=(tt == 0), stop=(tt == CT - 1))
            fill("S", last)
            def scores(h):
                o = 64 * (h % 2)
                for i in range(TT):
                    t = claim(pe, ("s", h, i))
                    fill(("s", h, i), pe.matmul(t, obuf[o:o + 64, 3 + 2 * (h // 2), i * P:(i + 1) * P],
                                                obuf[o:o + 64, 2 + 2 * (h // 2), :], start=True, stop=True))

            def outputs(h):
                o = 64 * (h % 2)
                t = claim(pe, ("o", h))
                for i in range(TT):
                    wait_freed(pe, ("s", h, i))
                    pe.matmul(t, v1[:, i, h * DV:(h + 1) * DV], probs[:, i, :], start=(i == 0), stop=False)
                pe.wait_ge(S["qdec_ready"], 2 * (h // 2) + 2)
                for d in range(2):
                    last = pe.matmul(t, state[o:o + 64, d, h // 2, :], qdec[o:o + 64, d, :],
                                     start=False, stop=(d == 1))
                fill(("o", h), last)

            pe.wait_ge(S["q_ready"], 8)
            wait_freed(pe, ("v", 1, TT - 1))
            wait_freed(pe, "S")
            for h in range(H1 + 1):
                if h:
                    outputs(h - 1)
                if h < H1:
                    scores(h)
                if h:
                    wait_freed(pe, ("o", h - 1))
                    t = claim(pe, ("var", h - 1))
                    fill(("var", h - 1), pe.matmul(t, mean_ones[:, 1, :], osq, start=True, stop=True))
            for n in range(2):
                feature_tiles(("in1", 4 + n), [("g", 4 * n + i) for i in range(4)], h_parts)
            token_tiles(("in1", 6), [("f", t) for t in range(TT)], h_parts)
            wl = slots[landed(pe, "dft")][:, :].rearrange("p (m k n) -> p m k n", m=2, k=TT)
            for g in range(FG):
                for m in range(2):
                    t = claim(pe, ("fa", g, m))
                    wait_freed(pe, ("f", TT - 1))
                    for k in range(TT):
                        last = pe.matmul(t, f_tok[:, k, g * P:(g + 1) * P], wl[:, m, k, :],
                                         start=(k == 0), stop=(k == TT - 1))
                    fill(("fa", g, m), last)
            pe.wait_ge(S["dist_in"], 48)
            for g in range(FG):
                t = claim(pe, ("z", g))
                wait_freed(pe, ("fa", g, 1))
                pe.matmul(t, dftd[:, 0, :], fa[:, g, 0, :], start=True, stop=False)
                fill(("z", g), pe.matmul(t, dftd[:, 1, :], fa[:, g, 1, :], start=False, stop=True))
            wait_freed(pe, ("z", FG - 1))
            pe.wait_ge(S["g_ready"], 8)
            merge("m1", z, 4, obuf, KT)
            out_proj("out1", "m1", 2, "n2")
            norm(2, "n2", L, k0=6)
            for j in range(UPN):
                if j == 0:
                    first_tiles(("up", 0), [("up", 0, n) for n in range(4)], h_parts, "h_ready", 2 * KT)
                else:
                    feature_tiles(("up", j), [("up", j, n) for n in range(4)], h_parts)
                if j == 0:
                    pe.wait_ge(S["silu_ready"], 4)
                mod_step("mod2", j, 0)
            mod_step("mod2", 11, 0)
            mod_turn("mod2", 11)
            for n in range(KT):
                claim(pe, ("down", n))
            for j in range(6):
                kt = 4 if j < 5 else 2
                w = parts_of(("down", j), kt)
                for n in range(KT):
                    t = tile(("down", n))
                    for k in range(kt):
                        if n == 0:
                            pe.wait_ge(S["act_low"], 4 * j + k + 1)
                        last = product(t, w, (lambda k, a, b: act_high(k)[:, a:b],
                                                                     lambda k, a, b: act_low_v[:, k, a:b]),
                                       4 * j + k, FT, (n * P, n * P + P), (0, L), True, kw=k)
                    if j == 5:
                        fill(("down", n), last)
                        if n >= 2:
                            norm_step(3, "nf1", L, n - 2)
                if j < 5:
                    last.then_inc(S["chunk_free"], 1)
            def context():
                w = slot(chunk_at["down", 5] % RAW, 4)
                for k in range(KT // 2):
                    turn(("cT2", k), [(j * LC + t * P, w[:, 2 + t, (2 * k + j) * P:(2 * k + j + 1) * P])
                                      for j in range(2) for t in range(CT)])

            norm(3, "nf1", L, context, 6)
            norm(4, "n3", L)
            first_tiles(("in2", 0), [("u", i) for i in range(4)], h_parts, "h_ready", 3 * KT)
            norm(5, "nc2", LC, lambda: feature_tiles(("in2", 1), [("u", 4)], h_parts))
            for i in range(1, 4):
                feature_tiles(("in2", 1), [("u", 4 + i)], h_parts, c0=i * P)
            for hh in range(2):
                token_tiles(("in2", 2 + hh), [("va", hh, t) for t in range(TT)], h_parts)
            pe.wait_ge(S["stage2_in"], 16 * 4)
            for i in range(2):
                turn(("ws", i), [(j * P, ws_raw[:, 4 * i + j, :]) for j in range(4)])
            wait_freed(pe, ("ws", 1))
            for cc in range(TT):
                pe.wait_ge(S["ln_ready"], cc + 1)
                for g in range(NG):
                    t = claim(pe, ("mix", g)) if cc == 0 else tile(("mix", g))
                    last = pe.matmul(t[:, cc * P:(cc + 1) * P], va[:, cc, g * P:(g + 1) * P], ws_t[:, g, :],
                                     start=True, stop=True)
                    if cc == TT - 1:
                        fill(("mix", g), last)
            roped("q2", ("in2", 4), 0, 4, "swap2", raw2)
            roped("q2", ("in2", 5), 4, 4, "swap2", raw2, first=lambda: swap("q2", 3, "swap2", raw2))
            swap("q2", 7, "swap2", raw2)
            roped("k2", ("in2", 6), 0, 2, "swap2", raw2)
            swap("k2", 1, "swap2", raw2)
            token_tiles(("in2", 6), [("vb", t) for t in range(TT)], h_parts, c0=256, width=256)
            pe.wait_ge(S["h_ready"], 5 * KT)
            feature_tiles(("in2", 6), [("kc2", i) for i in range(2)], hc2_parts, width=LC)
            token_tiles(("in2", 6), [("vc2", t) for t in range(CT)], hc2_parts, c0=256, width=256)
            def item(i):
                kv, n, r = i // 16, (i // 4) % 4, i % 4
                return kv, n, r, max(n - 1, 0), min(n + 2, TT)

            def att_scores(i):
                kv, n, r, b0, b1 = item(i)
                h = 4 * kv + r
                o = 64 * (h % 2)
                t = claim(pe, ("as", i))
                lq = q2[o:o + 64, h // 2, n * P:(n + 1) * P]
                pe.matmul(t[:, 512 - (b1 - b0) * P:512], lq, kdup[o:o + 64, kv, b0 * P:b1 * P],
                          start=True, stop=True)
                fill(("as", i), pe.matmul(t[:, 512:512 + LC], lq, kcdup[o:o + 64, kv, :],
                                          start=True, stop=True))

            def att_turn(i):
                _, _, _, b0, b1 = item(i)
                pe.wait_ge(S["p_scaled"], i + 1)
                t = claim(pe, ("at", i))
                nb = b1 - b0 + CT
                o = (3 - (b1 - b0)) * P
                for b in range(nb):
                    last = pe.transpose(t[:, b * P:(b + 1) * P],
                                        prob2[:, i % NPB, o + b * P:o + (b + 1) * P], ident)
                fill(("at", i), last)

            def att_values(g):
                kv, n, _, b0, b1 = item(4 * g)
                wait_freed(pe, ("at", 4 * g + 3))
                t = claim(pe, ("pv", g))
                nb = b1 - b0 + CT
                for b in range(nb):
                    vals = (vb[:, b0 + b, :] if b < b1 - b0 else vcx[:, b - (b1 - b0), :])
                    for par in range(2):
                        last = pe.matmul(t[64 * par:64 * par + 64, 0:256].rearrange("p (a q) -> p a q", a=2),
                                         vals[:, kv * HD:(kv + 1) * HD], prob_t[:, b, par:4:2, :],
                                         start=(b == 0), stop=(b == nb - 1))
                fill(("pv", g), last)

            pe.wait_ge(S["kdup_ready"], 1)
            wait_freed(pe, ("kc2", 1))
            wait_freed(pe, ("vc2", CT - 1))
            for i in range(NH * TT + LAG):
                if i < NH * TT:
                    att_scores(i)
                if i >= LAG:
                    if (i - LAG) % 4 == 0 and i > LAG:
                        att_values((i - LAG) // 4 - 1)
                    att_turn(i - LAG)
            att_values(NH * TT // 4 - 1)
            pe.wait_ge(S["ya_ready"], NG)
            wait_freed(pe, ("pv", NH * TT // 4 - 1))
            merge("m2", ug, KT, q2, KT)
            out_proj("out2", "m2", 6, "n4")
            norm(6, "n4", L, k0=6)
            pe.wait_ge(S["h4_ready"], KT)
            pe.wait_ge(S["router_in"], 16)
            r = claim(pe, "router")
            for t in range(TT):
                for k in range(KT):
                    last = pe.matmul(r[:, t * NE:(t + 1) * NE], hT[:, k, t * P:(t + 1) * P], w_route[:, k, :],
                                     start=(k == 0), stop=(k == KT - 1))
            fill("router", last)
            for t in range(TT):
                for hh in range(2):
                    turn(("ht", t, hh), [(k * P, hT[:, 4 * hh + k, t * P:(t + 1) * P]) for k in range(4)])
            pe.wait_ge(S["aff_ready"], 1)
            a = claim(pe, "affT")
            for t in range(TT):
                last = pe.transpose(a[0:NE, t * P:(t + 1) * P], aff[:, t, :], ident)
            fill("affT", last)
            pe.wait_ge(S["rank_ready"], 1)
            a = claim(pe, "slotT")
            for t in range(TT):
                last = pe.transpose(a[:, t * NE:(t + 1) * NE], rank[0:NE, t * P:(t + 1) * P], ident[0:NE, 0:NE])
            fill("slotT", last)
            pe.wait_ge(S["wsel_ready"], TT)
            for q in range(PAIRS):
                turn(("wt", q), [(t * P, wsel[:, t, q * P:(q + 1) * P]) for t in range(TT)])
            def landed_loop(it, m):
                loads = sum(len(chunks[n]) for n in range(m % SLOTS, NCH, RAW)) if m % SLOTS < RAW else 0
                pe.wait_ge(S[f"landed{m % SLOTS}"],
                           it * (16 * PAIR_CHUNKS // SLOTS) + 16 * (loads + m // SLOTS + 1))
                return slot(m, 8 if m < 4 * FQ else 4)

            def bank(b, n=1):
                return ps[:, b * 512:(b + n) * 512]

            wait_freed(pe, ("wt", PAIRS - 1))
            wait_freed(pe, ("wt", PAIRS - 2))
            pe.wait_ge(S["sel_ready"], TT)
            with pe.Fori(0, PAIRS) as it:
                pe.wait_ge(S["y_ready"], it * 2 + 1)
                for d in range(KT):
                    for t in range(TT):
                        last = pe.matmul(bank(6, 2)[:, d * P:(d + 1) * P], h2_tok[:, t, d * P:(d + 1) * P],
                                         sel[:, t, bass.ds(it * P, P)], start=(t == 0), stop=(t == TT - 1))
                    if d % 4 == 3:
                        last.then_inc(S["xe_full"], 1)
                pe.wait_ge(S["xe_ready"], it * 2 + 2)
                pe.wait_ge(S["x_added"], it * KT + 1)

                def turn_hidden(fq):
                    n = it * FQ + fq
                    pe.wait_ge(S["hm_ready"], n + 2)
                    pe.wait_ge(S["hmt_ready"], n + 1)
                    for j in range(4):
                        last = pe.transpose(bank(4)[:, j * P:(j + 1) * P],
                                            hmid[:, fq * 512 + j * P:fq * 512 + (j + 1) * P], ident)
                    last.then_inc(S["hmt_full"], 1)

                for fq in range(FQ):
                    if fq >= 2:
                        pe.wait_ge(S["hm_ready"], it * FQ + fq)
                    for gu in range(2):
                        m = 4 * fq + 2 * gu
                        wa, wb = landed_loop(it, m), landed_loop(it, m + 1)
                        b = bank(2 * (fq % 2) + gu)
                        for k in range(KT):
                            la = pe.matmul(b[0:64, :], xe[:, k, 0:64], wa[:, k, :],
                                           start=(k == 0), stop=(k == KT - 1))
                            lb = pe.matmul(b[64:128, :], xe[:, k, 64:128], wb[:, k, :],
                                           start=(k == 0), stop=(k == KT - 1))
                        la.then_inc(S["chunk_free"], 1)
                        lb.then_inc(S["chunk_free"], 1)
                    if fq:
                        turn_hidden(fq - 1)
                turn_hidden(FQ - 1)
                for kq in range(FQ):
                    pe.wait_ge(S["hmt_ready"], it * FQ + kq + 2)
                    m = 4 * FQ + 2 * kq
                    wa, wb = landed_loop(it, m), landed_loop(it, m + 1)
                    for k in range(4):
                        for hh in range(2):
                            la = pe.matmul(bank(6 + hh)[0:64, :], hmid_t[:, 4 * kq + k, 0:64],
                                           wa[:, k, hh * 512:(hh + 1) * 512],
                                           start=(kq == 0 and k == 0), stop=(kq == FQ - 1 and k == 3))
                            lb = pe.matmul(bank(6 + hh)[64:128, :], hmid_t[:, 4 * kq + k, 64:128],
                                           wb[:, k, hh * 512:(hh + 1) * 512],
                                           start=(kq == 0 and k == 0), stop=(kq == FQ - 1 and k == 3))
                    la.then_inc(S["chunk_free"], 1)
                    lb.then_inc(S["chunk_free"], 1)
                pe.wait_ge(S["y_ready"], it * 2 + 3)
                pe.wait_ge(S["hm_ready"], it * FQ + FQ + 1)
                for d in range(KT):
                    if d >= 4:
                        pe.wait_ge(S["x_added"], it * KT + 1 + d - 3)
                    pe.matmul(bank(d % 4), y_sb[:, d * P:(d + 1) * P], wsel_t[:, bass.ds(it, 1), :].rearrange(
                        "p a b -> p (a b)"), start=True, stop=True).then_inc(S["sc_full"], 1)
            norm(7, "nf2", L)
            pe.wait_ge(S["scaled"], 8 * 8)
            for t in range(TT):
                for hh in range(2):
                    turn(("ot", t, hh), [(k * P, xT[:, 4 * hh + k, t * P:(t + 1) * P]) for k in range(4)])

        @block.scalar
        def _(act_e):
            A = act_e.activation

            def copy_out(name, dst, func=ACT.Copy, width=512, **kw_):
                t = wait_full(act_e, name)[:, 0:width]
                free(name, "A", A(dst, t, func, **kw_))

            def norm_squares(m, tag, src, width, written=None):
                A(small[:, 4:5], eps_col, ACT.Sqrt)
                for k in range(KT):
                    if written:
                        written(k)
                    A((sqc if m == 5 else sq8)[:, k, 0:width], src[:, k, 0:width], ACT.Square).then_inc(S["sq_ready"], 1)
                if m:
                    act_e.wait_ge(S["recip_ready"], m)
                n = width // P
                copy_out(tag, root[:, 0:n], ACT.Sqrt, width=n, bias=eps_col)

            def norm_affine(m, dst, width, a, shift, high=None, nth=None):
                for k in range(KT + 1):
                    if k < KT:
                        act_e.wait_ge(S["scaled"], KT * m + k + 1)
                        A(dst[:, k, 0:width], dst[:, k, 0:width], ACT.Identity, bias=shift(k), scale=a(k)).then_inc(
                            S["h4_ready"] if m == 6 else S["h_plain"], 1)
                    if k and high:
                        round_h(nth, k - 1, high, dst)

            def round_h(nth, k, high, src):
                act_e.wait_ge(S["h_plain"], KT * nth + k + 1)
                A(high(k, 0, src.shape[2]), src[:, k, :], ACT.Copy).then_inc(S["h_rounded"], 1)

            issued = [0]

            def prepare(name):
                for i in next_splits(issued, name):
                    sl = landed(act_e, order[split[i]])
                    if i >= 2:
                        wait_spent(act_e, split[i - 2])
                    if i == split.index(chunk_at["in2", 5]) + 2:
                        wait_full(act_e, ("vc2", CT - 1))
                    n = split_words(i)
                    A(slots_r[high_slot(i)][:, 0:n], slots[sl][:, 0:n], ACT.Copy).then_inc(S["high_ready"], 1)

            def mod_silu(vi):
                for r in range(2):
                    A(sc_pad[:, :, r], cols[:, vi, 8 * r:8 * r + 8], ACT.Silu).then_inc(S["silu_ready"], 1)

            def mod_rows(tag, c, ahead=True):
                if ahead:
                    prepare((tag, c))
                if c >= 2:
                    wait_full(act_e, (tag, "T", c - 2))
                copy_out((tag, c), m_sb(tag, c))

            def rope_raw(tag, i, g, rawbuf, scale):
                if g >= 2:
                    act_e.wait_ge(S["rope_cos"], g - 1)
                    act_e.wait_ge(S["q_ready"], g - 1)
                copy_out((tag, i), rawbuf[:, i % 2, :], ACT.Copy, scale=scale)

            def merge_gates(tag, vi):
                _, gates = merge_views[tag]
                base = V1["b_gate"]
                c = 4
                for nq in range(2):
                    for pi, part in enumerate("ab"):
                        prepare((tag, "gate", part, nq))
                        first = 8 if (tag == "m1") == (part == "a") else 0
                        if nq and part == "a":
                            wait_freed(act_e, (tag, "proj", "a", 0, 3))
                        elif nq:
                            act_e.wait_ge(S["merged_ready"], (0 if tag == "m1" else 8) + 4)
                        for n in range(4):
                            col = base + first + 4 * nq + n
                            copy_out((tag, "gate", part, nq, n), gates[:, pi, n, :], ACT.Sigmoid,
                                     bias=cols[:, vi, col:col + 1])
                        if tag == "m1":
                            mod_rows("mod1", c)
                        prepare((tag, "proj", part, nq))
                        if nq and part == "b":
                            for k in range(KT):
                                act_e.wait_ge(S["merged_ready"], (0 if tag == "m1" else KT) + k + 1)
                                A(h_high[:, k, :], merge_views[tag][0][:, k, :], ACT.Copy).then_inc(
                                    S["merged_high"], 1)
                        if tag == "m1":
                            mod_rows("mod1", c + 1)
                            c += 2

            act_e.wait_ge(S["ones_ready"], 4)
            for k in range(0, KT, 2):
                copy_out(("xT", k), xT[:, k, :])
            for k in range(0, KT // 2, 2):
                copy_out(("cT", k), hc[:, 2 * k:2 * k + 2, :].rearrange("p a b -> p (a b)"))
            for n in (("xT", 6), ("xT", 7), ("cT", 2), ("cT", 3)):
                wait_freed(act_e, n)
            norm_squares(0, "n1", xT, L)
            wait_full(act_e, "n1")
            norm_squares(1, "nc", hc, LC)
            mod_silu(0)
            for c in range(4):
                if c == 3:
                    prepare(("mod1", 2))
                mod_rows("mod1", c, ahead=False)
            act_e.wait_ge(S["mods_ready"], 1)
            norm_affine(0, hT, L, lambda k: scale_a[:, 0, k:k + 1], lambda k: mod_cols[:, k, 0:1],
                        h_parts[0], 0)
            norm_affine(1, hc, LC, lambda k: scale_a[:, 1, k:k + 1], lambda k: mod_cols[:, k, 1:2],
                        hc_parts[0], 1)
            act_e.wait_ge(S["bcast_in"], 48)
            A(ea, decay, ACT.Exp).then_inc(S["decay_exp"], 1)
            act_e.wait_ge(S["decay_ready"], 1)
            for d in range(2):
                for t in range(CT):
                    c0 = CONST["age"][0] + 2 * d + t
                    A(ctxw[:, d, t, :], lg[:, 8 * d:8 * d + 8], ACT.Exp, scale=cst[:, c0:c0 + 1]).then_inc(
                        S["decay_exp"], 1)
            prepare(("in1", 0))
            for i in range(4):
                rope_raw("qk1", i, i, raw, DK ** -0.5)
            prepare(("in1", 1))
            for t in range(CT):
                copy_out(("kc", t), kc[:, t, :])
            for i in range(4, 8):
                rope_raw("qk1", i, i, raw, 1.0)
            for i in range(2, 4):
                prepare(("in1", i))
            def decayed_queries(j):
                if j:
                    wait_full(act_e, ("o", 2 * j - 1))
                    act_e.wait_ge(S["qdec_ready"], 2 * j)
                A(qdec[:, 0, :], tpos, ACT.Exp, scale=qcol[:, 0, j:j + 1]).then_inc(S["table_in"], 1)
                A(qdec[:, 1, :], tpos, ACT.Exp, scale=qcol[:, 1, j:j + 1],
                  bias=qcol[:, 2, j:j + 1]).then_inc(S["table_in"], 1)

            def decay_table(h):
                act_e.wait_ge(S["table_arg"], h + 1)
                A(table[:, h % 2, :], table[:, h % 2, :], ACT.Exp).then_inc(S["table_exp"], 1)

            act_e.wait_ge(S["dist_in"], 32)
            act_e.wait_ge(S["decay_ready"], 2)
            wait_freed(act_e, "S")
            decay_table(0)
            decayed_queries(0)
            decay_table(1)
            for h in range(H1):
                t = wait_full(act_e, ("o", h))
                if h:
                    wait_full(act_e, ("var", h - 1))
                A(osq, t, ACT.Square)
                free(("o", h), "A", A(obuf[:, h, :], t, ACT.Copy))
                if h % 2 and h + 1 < H1:
                    decayed_queries(h // 2 + 1)
                if h + 2 < H1:
                    decay_table(h + 2)
                if h:
                    act_e.wait_ge(S["o_square"], h)
                copy_out(("var", h), rinv, ACT.Sqrt, bias=eps_col)
            wait_full(act_e, ("g", 0))
            for n in range(KT):
                if n % 4 == 0:
                    prepare(("in1", 4 + n // 4))
                copy_out(("g", n), at(10240 + 512 * n, L), ACT.Silu)
            prepare(("in1", 6))
            for t in range(TT):
                copy_out(("f", t), f_tok[:, t, :])
            prepare("dft")
            for g in range(FG):
                for m in range(2):
                    if g == 0 and m == 0:
                        act_e.wait_ge(S["g_ready"], 8)
                    copy_out(("fa", g, m), fa[:, g, m, :])
            merge_gates("m1", 0)
            for nq in range(2):
                prepare(("out1", nq))
            wait_full(act_e, ("mod1", 11))
            mod_silu(3)
            norm_squares(2, "n2", xT, L, lambda k: wait_freed(act_e, ("out1", k)))
            act_e.wait_ge(S["mods_ready"], 2)
            norm_affine(2, hT, L, lambda k: scale_a[:, 2, k:k + 1], lambda k: mod_cols[:, 24 + k, 0:1],
                        h_parts[0], 2)
            def round_act(k):
                act_e.wait_ge(S["act_ready"], k + 1)
                A(act_high(k), act[:, k, :], ACT.Copy).then_inc(S["act_high"], 1)

            for j in range(UPN):
                prepare(("up", j))
                for n in range(4):
                    f = 2 * j + n % 2 + (FT if n >= 2 else 0)
                    t = wait_full(act_e, ("up", j, n))
                    if j:
                        act_e.wait_ge(S["act_ready"], 2 * (j - 1) + 1 + n % 2)
                    A(conv[:, n, :], t, ACT.Identity, bias=cols[:, 2, 44 + f:45 + f],
                      scale=cols[:, 1, 44 + f:45 + f]).then_inc(S["conv_mid"], 1)
                for n in range(2):
                    wait_freed(act_e, ("up", j, n))
                    A(gelu_a[:, n, :], conv[:, n, :], ACT.Gelu_apprx_tanh).then_inc(S["gelu_ready"], 1)
                mod_rows("mod2", j)
                if j == UPN - 2:
                    for k in range(4):
                        round_act(k)
            mod_rows("mod2", 11)
            wait_full(act_e, ("up", UPN - 1, 3))
            act_e.wait_ge(S["act_ready"], FT)
            for j in range(6):
                for k in range(4 * j + 4, min(4 * j + 8, FT)):
                    round_act(k)
                prepare(("down", j))
            norm_squares(3, "nf1", xT, L, lambda k: wait_freed(act_e, ("down", k)))
            for k in range(0, KT // 2, 2):
                copy_out(("cT2", k), hc2[:, 2 * k:2 * k + 2, :].rearrange("p a b -> p (a b)"))
            norm_squares(4, "n3", xT, L, lambda k: act_e.wait_ge(S["scaled"], 3 * KT + k + 1))
            act_e.wait_ge(S["mods_ready"], 3)
            norm_affine(4, hT, L, lambda k: scale_a[:, 0, k:k + 1], lambda k: mod_cols2[:, k, 0:1],
                        h_parts[0], 3)
            for n in range(KT):
                if n % 4 == 0:
                    prepare(("in2", n // 4))
                if n == 4:
                    wait_freed(act_e, ("cT2", 2))
                    wait_freed(act_e, ("cT2", 3))
                    wait_full(act_e, "n3")
                    norm_squares(5, "nc2", hc2, LC)
                copy_out(("u", n), ug[:, n, :], ACT.Gelu_apprx_tanh)
            norm_affine(5, hc2, LC, lambda k: scale_a[:, 1, k:k + 1], lambda k: mod_cols2[:, k, 1:2])
            for hh in range(2):
                prepare(("in2", 2 + hh))
                for t in range(TT):
                    copy_out(("va", hh, t), va[:, t, hh * 512:(hh + 1) * 512], ACT.Gelu_apprx_tanh)
                    if hh:
                        act_e.wait_ge(S["ln_stats"], t + 1)
                        A(stats[:, t, 14:15], stats[:, t, 13:14], ACT.Sqrt, bias=eps_col).then_inc(S["ln_root"], 1)
            for i in range(2):
                copy_out(("ws", i), ws_t[:, 4 * i:4 * i + 4, :].rearrange("p a b -> p (a b)"))
            for i in range(8):
                if i % 4 == 0:
                    prepare(("in2", 4 + i // 4))
                rope_raw("q2", i, 8 + i, raw2, HD ** -0.5)
            wait_full(act_e, last_tile["in2", 5])
            for k in range(KT):
                round_h(4, k, hc2_parts[0], hc2)
            for i in range(2):
                rope_raw("k2", i, 16 + i, raw2, 1.0)
            act_e.wait_ge(S["q_ready"], 18)
            for t in range(TT):
                copy_out(("vb", t), vb[:, t, :], width=256)
            act_e.wait_ge(S["kdup_ready"], 1)
            for t in range(CT):
                copy_out(("vc2", t), vcx[:, t, :], width=256)
            prepare(("in2", 6))
            def widths(i):
                n = (i // 4) % 4
                return (2 if n in (0, 3) else 3) * P

            def att_exp(i):
                h = 4 * (i // 16) + i % 4
                w = widths(i)
                act_e.wait_ge(S["row_max"], i + 1)
                t = tile(("as", i))
                if i >= NPB:
                    wait_full(act_e, ("at", i - NPB))
                if i >= 4:
                    act_e.wait_ge(S["p_scaled"], i - 3)
                free(("as", i), "A", A(prob2[:, i % NPB, 384 - w:640], t[:, 512 - w:768], ACT.Exp,
                                       bias=neg_m[:, i % 4:i % 4 + 1], accum_out=den[:, i % 4:i % 4 + 1]))
                A(sink_e[:, i % 4:i % 4 + 1], sink[:, h:h + 1], ACT.Exp,
                  bias=neg_m[:, i % 4:i % 4 + 1]).then_inc(S["sink_exp"], 1)

            def att_keep(i):
                nb = widths(i) // P + CT
                if i % 4 == 0 and i:
                    wait_full(act_e, ("pv", i // 4 - 1))
                t = wait_full(act_e, ("at", i))
                free(("at", i), "A", A(prob_t[:, 0:nb, i % 4, :],
                                       t[:, 0:nb * P].rearrange("p (b q) -> p b q", b=nb), ACT.Copy))

            for i in range(NH * TT + LAG):
                if i < NH * TT:
                    att_exp(i)
                if i >= LAG:
                    att_keep(i - LAG)
            merge_gates("m2", 3)
            for nq in range(2):
                prepare(("out2", nq))
            norm_squares(6, "n4", xT, L, lambda k: wait_freed(act_e, ("out2", k)))
            norm_affine(6, hT, L, lambda k: scale_a[:, 2, k:k + 1], lambda k: mod_cols2[:, 24 + k, 0:1])
            act_e.wait_ge(S["row_max"], NH * TT + 1)
            A(aff[:, :, :], aff[:, :, :], ACT.Exp).then_inc(S["exp_done"], 1)
            for t in range(TT):
                copy_out(("ht", t, 0), h2_tok[:, t, 0:512])
            for q in range(0, PAIRS, 2):
                copy_out(("wt", q), wsel_t[:, q, :])
            act_e.sem_inc(S["y_ready"], 1)
            act_e.sem_inc(S["hmt_ready"], 1)
            with act_e.Fori(0, PAIRS) as it:
                for hh in range(2):
                    act_e.wait_ge(S["xe_full"], it * 2 + hh + 1)
                    A(xe[:, 4 * hh:4 * hh + 4, :].rearrange("p a b -> p (a b)"),
                      ps[:, (6 + hh) * 512:(7 + hh) * 512], ACT.Copy).then_inc(S["xe_ready"], 1)

                def keep_turned(fq):
                    act_e.wait_ge(S["hmt_full"], it * FQ + fq + 1)
                    A(hmid_t[:, 4 * fq:4 * fq + 4, :].rearrange("p a b -> p (a b)"), ps[:, 4 * 512:5 * 512],
                      ACT.Copy).then_inc(S["hmt_ready"], 1)

                for fq in range(FQ):
                    act_e.wait_ge(S["chunk_free"], it * PAIR_CHUNKS + LOOP_FREE + 4 * fq + 2)
                    if fq >= 2:
                        act_e.wait_ge(S["hm_ready"], it * FQ + fq)
                    A(sg[:, fq % 2, :], ps[:, 2 * (fq % 2) * 512:(2 * (fq % 2) + 1) * 512],
                      ACT.Silu).then_inc(S["silu_done"], 1)
                    if fq:
                        keep_turned(fq - 1)
                keep_turned(FQ - 1)
                act_e.wait_ge(S["chunk_free"], it * PAIR_CHUNKS + LOOP_FREE + PAIR_CHUNKS)
                for hh in range(2):
                    A(y_sb[:, hh * 512:(hh + 1) * 512], ps[:, (6 + hh) * 512:(7 + hh) * 512],
                      ACT.Copy).then_inc(S["y_ready"], 1)
            norm_squares(7, "nf2", xT, L, lambda k: act_e.wait_ge(S["x_added"], 2 + KT * (PAIRS - 1) + k))
            for t in range(TT):
                copy_out(("ot", t, 0), out_sb[:, t, 0:512])

        @block.vector
        def _(ve):
            chained = [0]

            def link(ins):
                chained[0] += 1
                ins.then_inc(S["dve_chain"], 1)
                ve.wait_ge(S["dve_chain"], chained[0])

            def wide(v, *shape):
                return v.broadcast_to(list(shape))

            issued = [0]

            def prepare(name):
                for i in next_splits(issued, name):
                    sl, n = split[i] % RAW, split_words(i)
                    ve.wait_ge(S["high_ready"], i + 1)
                    ve.tensor_tensor(slots_r[sl][:, 0:n], slots[sl][:, 0:n],
                                     slots_r[high_slot(i)][:, 0:n].bitcast(F32), ALU.subtract).then_inc(
                        S["low_ready"], 1)

            def low_h(nth, k, high, low, src):
                ve.wait_ge(S["h_rounded"], KT * nth + k + 1)
                ve.tensor_tensor(low(k, 0, src.shape[2]), src[:, k, :], high(k, 0, src.shape[2]).bitcast(F32),
                                 ALU.subtract).then_inc(S["h_ready"], 1)

            def mod_columns(tag, c):
                cc, vi = (mod_cols, 0) if tag == "mod1" else (mod_cols2, 3)
                t = wait_full(ve, (tag, "T", c))
                b = cols[:, vi, V1["b_mod"] + 4 * c:V1["b_mod"] + 4 * c + 4]
                free((tag, "T", c), "D", ve.tensor_tensor(
                    cc[:, 4 * c:4 * c + 4, :], t[:, 0:8].rearrange("p (a b) -> p a b", b=2),
                    wide(b.unsqueeze(2), P, 4, 2), ALU.add))

            def mod_scales(tag, which):
                cc, vi = (mod_cols, 0) if tag == "mod1" else (mod_cols2, 3)
                for i in which:
                    m, r, w = ((8, 0, "norm1"), (8, 1, "norm1"), (32, 0, "norm2"))[i]
                    wait_freed(ve, (tag, "T", m // 4 + 1))
                    last = ve.scalar_tensor_tensor(scale_a[:, i, :], cc[:, m:m + 8, r], 1.0,
                                                   cols[:, vi, V1[w]:V1[w] + 8], ALU.add, ALU.mult)
                last.then_inc(S["mods_ready"], 1)

            def norm_scale(m, tag, src, dst, width, weight=None, between=None, split_h=None):
                n = width // P
                wait_freed(ve, tag)
                if m:
                    wait_full(ve, (norm_tags[m - 1], "wide"))
                ve.reciprocal(recip[:, 0:n], root[:, 0:n]).then_inc(S["recip_ready"], 1)
                if between:
                    between()
                r = wait_full(ve, (tag, "wide"))[:, 0:width]
                for k in range(KT + 2):
                    if split_h and k >= 2:
                        low_h(split_h[0], k - 2, *split_h[1:], dst)
                    if k >= KT:
                        continue
                    if weight is None:
                        last = ve.tensor_tensor(dst[:, k, 0:width], src[:, k, 0:width], r, ALU.mult)
                    else:
                        last = ve.scalar_tensor_tensor(dst[:, k, 0:width], src[:, k, 0:width], weight(k),
                                                       r, ALU.mult, ALU.mult)
                    last.then_inc(S["scaled"], 1)
                ve.wait_ge(S["scaled"], KT * (m + 1))
                free((tag, "wide"), "D", None)

            def rope_sum(tag, i, g, cs, rsinbuf, rcosbuf, dst):
                t = wait_full(ve, (tag, "swap", i))
                if g == (0 if cs is rope_cs else 8):
                    ve.wait_ge(S["rope_in"], 16 if g == 0 else 32)
                free((tag, "swap", i), "D", ve.tensor_tensor(rsinbuf[:, i % 2, :], t, cs[:, 1, :], ALU.mult))
                wait_freed(ve, (tag, "swap", i))
                ve.wait_ge(S["rope_cos"], g + 1)
                ve.tensor_tensor(dst, rsinbuf[:, i % 2, :], rcosbuf[:, i % 2, :], ALU.add).then_inc(S["q_ready"], 1)

            def centred(name, dst):
                t = wait_full(ve, name).rearrange("p (h e) -> p h e", e=DV)
                link(ve.tensor_reduce(negmean[:, 0:4], t, AX.X, ALU.add))
                link(ve.tensor_scalar(negmean[:, 4:8], negmean[:, 0:4], -1.0 / DV, None, ALU.mult))
                free(name, "D", ve.tensor_tensor(dst.rearrange("p (h e) -> p h e", e=DV), t,
                                                 wide(negmean[:, 4:8].unsqueeze(2), P, 4, DV), ALU.add))

            def merged_rest(tag, k):
                ve.wait_ge(S["merged_high"], (0 if tag == "m1" else KT) + k + 1)
                ve.tensor_tensor(merged_low[tag][:, k, :], merge_views[tag][0][:, k, :],
                                 h_high[:, k, :].bitcast(F32), ALU.subtract).then_inc(S["merged_low"], 1)

            def merged_tiles(tag):
                merged, gates = merge_views[tag]
                c = 4
                for nq in range(2):
                    for pi, part in enumerate("ab"):
                        prepare((tag, "gate", part, nq))
                        if tag == "m1" and c > 4:
                            mod_columns("mod1", c - 1)
                        prepare((tag, "proj", part, nq))
                        if nq and part == "b":
                            for k in range(4):
                                merged_rest(tag, k)
                        for n in range(4):
                            name = (tag, "proj", part, nq, n)
                            wait_freed(ve, (tag, "gate", part, nq, n))
                            t = wait_full(ve, name)
                            dst = merged[:, 4 * nq + n, :] if part == "a" else gates[:, 1, n, :]
                            free(name, "D", ve.tensor_tensor(dst, t, gates[:, pi, n, :], ALU.mult))
                        if nq and part == "b":
                            for k in range(4, KT):
                                merged_rest(tag, k)
                        if tag == "m1":
                            mod_columns("mod1", c)
                            c += 2
                if tag == "m1":
                    mod_columns("mod1", 11)
                    mod_scales("mod1", (2,))

            def residual(names, gate, cc, n0=0):
                for n, name in enumerate(names, n0):
                    t = wait_full(ve, name)
                    free(name, "D", ve.scalar_tensor_tensor(xT[:, n, :], t, cc[:, gate + n, 0:1], xT[:, n, :],
                                                            ALU.mult, ALU.add))

            wait_full(ve, "vecs")
            for i, r in enumerate((104, 88, 88, 104)):
                last = ve.tensor_copy(cols[:, i, 0:r], tile("vecs")[:, i * P:i * P + r])
            free("vecs", "D", last)
            for k in range(1, KT, 2):
                free(("xT", k), "D", ve.tensor_copy(xT[:, k, :], wait_full(ve, ("xT", k))))
            for k in range(1, KT // 2, 2):
                free(("cT", k), "D", ve.tensor_copy(hc[:, 2 * k:2 * k + 2, :].rearrange("p a b -> p (a b)"),
                                                    wait_full(ve, ("cT", k))))
            norm_scale(0, "n1", xT, hT, L)
            norm_scale(1, "nc", hc, hc, LC)
            for c in range(4):
                if c == 3:
                    prepare(("mod1", 2))
                mod_columns("mod1", c)
            mod_scales("mod1", (0, 1))
            for k in range(KT):
                low_h(0, k, *h_parts, hT)
            for k in range(KT):
                low_h(1, k, *hc_parts, hc)
            ve.wait_ge(S["decay_exp"], 1)
            ve.tensor_scalar(lg, ea, -1.0, None, ALU.mult).then_inc(S["decay_ready"], 1)
            ve.wait_ge(S["decay_ready"], 1)
            for o in (0, 64):
                ve.tensor_copy(qcol[o:o + 64, 0, :], lg[o:o + 64, o // 64:8:2])
                last = ve.tensor_copy(qcol[o:o + 64, 1, :], ea[o:o + 64, 8 + o // 64:16:2])
            link(last)
            ve.tensor_scalar(qcol[:, 2, :], qcol[:, 1, :], -float(L + 1), None, ALU.mult).then_inc(
                S["decay_ready"], 1)
            prepare(("in1", 0))
            for i in range(4):
                rope_sum("qk1", i, i, rope_cs, rsin, rcos, obuf[:, 2 + 2 * i, :])
            prepare(("in1", 1))
            wait_freed(ve, ("kc", CT - 1))
            ve.wait_ge(S["decay_exp"], 5)
            for d in range(2):
                for t in range(CT):
                    ve.tensor_tensor(kw[:, d, t, :].rearrange("p (h e) -> p h e", e=DK),
                                     kc[:, t, :].rearrange("p (h e) -> p h e", e=DK),
                                     wide(ctxw[:, d, t, :].unsqueeze(2), P, H1, DK), ALU.mult).then_inc(
                                         S["kw_ready"], 1)
            for i in range(4):
                rope_sum("qk1", 4 + i, 4 + i, rope_cs, rsin, rcos, obuf[:, 3 + 2 * i, :])
            ve.wait_ge(S["q_ready"], 8)
            for hh in range(2):
                prepare(("in1", 2 + hh))
                for t in range(CT):
                    centred(("vc", hh, t), vc[:, t, hh * 512:(hh + 1) * 512])
                for t in range(TT):
                    centred(("v", hh, t), v1[:, t, hh * 512:(hh + 1) * 512])
            t = wait_full(ve, "S")
            free("S", "D", ve.tensor_copy(state[:, :, :, :].rearrange("p d j e -> p (d j e)"), t))
            def finish_head(h):
                wait_freed(ve, ("var", h))
                link(ve.reciprocal(rinv, rinv))
                ve.tensor_tensor(obuf[:, h, :], obuf[:, h, :], rinv, ALU.mult).then_inc(S["o_square"], 1)

            for h in range(H1):
                ve.wait_ge(S["table_ready"], h + 1)
                for i in range(TT):
                    t = wait_full(ve, ("s", h, i))
                    free(("s", h, i), "D", ve.tensor_tensor(
                        probs[:, i, :], t, table[:, h % 2, 384 - i * P:896 - i * P], ALU.mult))
                if h:
                    finish_head(h - 1)
            finish_head(H1 - 1)
            ve.wait_ge(S["o_square"], H1)
            for n in range(KT):
                if n % 4 == 0:
                    prepare(("in1", 4 + n // 4))
                wait_freed(ve, ("g", n))
                ve.tensor_tensor(obuf[:, n, :], at(10240 + 512 * n, L), obuf[:, n, :], ALU.mult).then_inc(
                    S["g_ready"], 1)
            prepare(("in1", 6))
            prepare("dft")
            for g in range(FG):
                free(("z", g), "D", ve.tensor_copy(z[:, g, :], wait_full(ve, ("z", g))))
            merged_tiles("m1")
            for nq in range(2):
                prepare(("out1", nq))
                residual([("out1", 4 * nq + n) for n in range(4)], 16, mod_cols, 4 * nq)
            norm_scale(2, "n2", xT, hT, L, split_h=(2, *h_parts))
            for j in range(UPN):
                prepare(("up", j))
                for n in range(4):
                    f = 2 * j + n % 2 + (FT if n >= 2 else 0)
                    ve.wait_ge(S["conv_mid"], 4 * j + n + 1)
                    t = wait_full(ve, ("up", j, n))
                    link(ve.scalar_tensor_tensor(conv[:, n, 1:L], t[:, 0:L - 1], cols[:, 1, f:f + 1],
                                                 conv[:, n, 1:L], ALU.mult, ALU.add))
                    free(("up", j, n), "D", ve.scalar_tensor_tensor(
                        conv[:, n, 0:L - 1], t[:, 1:L], cols[:, 2, f:f + 1], conv[:, n, 0:L - 1],
                        ALU.mult, ALU.add))
                wait_freed(ve, ("up", j, 3))
                for n in range(2):
                    ve.wait_ge(S["gelu_ready"], 2 * j + n + 1)
                    ve.tensor_tensor(act[:, 2 * j + n, :], gelu_a[:, n, :], conv[:, 2 + n, :],
                                     ALU.mult).then_inc(S["act_ready"], 1)
                prepare(("mod2", j))
                if j:
                    mod_columns("mod2", j - 1)
            prepare(("mod2", 11))
            mod_columns("mod2", 10)
            mod_columns("mod2", 11)
            mod_scales("mod2", (0, 1, 2))
            for j in range(6):
                for k in range(4 * j, min(4 * j + 4, FT)):
                    ve.wait_ge(S["act_high"], k + 1)
                    ve.tensor_tensor(act_low_v[:, k, :], act[:, k, :], act_high(k).bitcast(F32),
                                     ALU.subtract).then_inc(S["act_low"], 1)
                prepare(("down", j))
            residual([("down", n) for n in range(KT)], 40, mod_cols)
            def context():
                for k in range(1, KT // 2, 2):
                    free(("cT2", k), "D", ve.tensor_copy(hc2[:, 2 * k:2 * k + 2, :].rearrange("p a b -> p (a b)"),
                                                         wait_full(ve, ("cT2", k))))

            norm_scale(3, "nf1", xT, xT, L, lambda k: cols[:, 0, V1["final"] + k:V1["final"] + k + 1], context)
            ve.wait_ge(S["scaled"], 4 * KT)
            norm_scale(4, "n3", xT, hT, L, split_h=(3, *h_parts))
            prepare(("in2", 0))
            norm_scale(5, "nc2", hc2, hc2, LC)
            for i in range(4):
                prepare(("in2", i))
            ve.wait_ge(S["stage2_in"], 16 * 4)
            for t in range(TT):
                for hh in range(2):
                    wait_freed(ve, ("va", hh, t))
                    last = ve.bn_stats(stats[:, t, 6 * hh:6 * hh + 6], va[:, t, hh * 512:(hh + 1) * 512])
                link(last)
                ve.bn_aggr(stats[:, t, 12:14], stats[:, t, 0:12]).then_inc(S["ln_stats"], 1)
                ve.wait_ge(S["ln_stats"], t + 1)
                link(ve.tensor_scalar(stats[:, t, 15:16], stats[:, t, 12:13], -1.0, None, ALU.mult))
                link(ve.scalar_tensor_tensor(va[:, t, :], va[:, t, :], stats[:, t, 15:16], ln_rows[:, 0, :],
                                             ALU.add, ALU.mult))
                ve.wait_ge(S["ln_root"], t + 1)
                link(ve.reciprocal(stats[:, t, 14:15], stats[:, t, 14:15]))
                ve.scalar_tensor_tensor(va[:, t, :], va[:, t, :], stats[:, t, 14:15], ln_rows[:, 1, :],
                                        ALU.mult, ALU.add).then_inc(S["ln_ready"], 1)
            for g in range(NG):
                t = wait_full(ve, ("mix", g)).rearrange("p (c q) -> p c q", q=P)
                if g >= 2:
                    ve.wait_ge(S["ya_ready"], g - 1)
                free(("mix", g), "D", ve.tensor_tensor(
                    mixed[:, g % 2, :].rearrange("p (c q) -> p c q", q=P), t,
                    wide(bs_rows[:, g, :].unsqueeze(1), P, TT, P), ALU.add))
            ve.wait_ge(S["ya_ready"], NG)
            for i in range(8):
                if i % 4 == 0:
                    prepare(("in2", 4 + i // 4))
                rope_sum("q2", i, 8 + i, rope_cs2, rsin2, rcos2, q2[:, i, :])
            for k in range(KT):
                low_h(4, k, *hc2_parts, hc2)
            for i in range(2):
                rope_sum("k2", i, 16 + i, rope_cs2, rsin2, rcos2, krot[:, i, :])
            ve.wait_ge(S["q_ready"], 18)
            for kv in range(NKV):
                for o in (0, 64):
                    last = ve.tensor_copy(kdup[o:o + 64, kv, :],
                                          krot[64 * (kv % 2):64 * (kv % 2) + 64, kv // 2, :])
            last.then_inc(S["kdup_ready"], 1)
            for i in range(2):
                t = wait_full(ve, ("kc2", i))
                for kv in (2 * i, 2 * i + 1):
                    for o in (0, 64):
                        last = ve.tensor_copy(kcdup[o:o + 64, kv, :],
                                              t[64 * (kv % 2):64 * (kv % 2) + 64, 0:LC])
                free(("kc2", i), "D", last)
            prepare(("in2", 6))
            mask_rows = const("mask").rearrange("p (m s) -> p m s", m=2)

            def att_max(i):
                n, h = (i // 4) % 4, 4 * (i // 16) + i % 4
                w = (2 if n in (0, 3) else 3) * P
                t = wait_full(ve, ("as", i))
                if n == 0:
                    v, m = t[:, 384:512], mask_rows[:, 1, :]
                elif n == 3:
                    v, m = t[:, 256:384], mask_rows[:, 0, :]
                else:
                    v, m = t[:, 128:512].rearrange("p (b s) -> p b s", s=P)[:, 0:3:2, :], mask_rows
                link(ve.tensor_tensor(v, v, m, ALU.add))
                link(ve.tensor_reduce(row_top[:, 0:1], t[:, 512 - w:768], AX.X, ALU.max))
                if i >= 4:
                    ve.wait_ge(S["sink_exp"], i - 3)
                ve.tensor_scalar(neg_m[:, i % 4:i % 4 + 1], row_top[:, 0:1], sink[:, h:h + 1], -1.0,
                                 ALU.max, ALU.mult).then_inc(S["row_max"], 1)

            def att_scale(i):
                n = (i // 4) % 4
                w = (2 if n in (0, 3) else 3) * P
                c0 = i % 4
                ve.wait_ge(S["sink_exp"], i + 1)
                link(ve.tensor_tensor(row_top[:, 1:2], den[:, c0:c0 + 1], sink_e[:, c0:c0 + 1], ALU.add))
                link(ve.reciprocal(row_top[:, 2:3], row_top[:, 1:2]))
                p = prob2[:, i % NPB, 384 - w:640]
                ve.tensor_scalar(p, p, row_top[:, 2:3], None, ALU.mult).then_inc(S["p_scaled"], 1)

            def att_out(g):
                kv, n = g // 4, g % 4
                t = wait_full(ve, ("pv", g))
                free(("pv", g), "D", ve.tensor_copy(q2[:, 2 * kv:2 * kv + 2, n * P:(n + 1) * P],
                                                    t[:, 0:256].rearrange("p (a q) -> p a q", a=2)))

            for i in range(NH * TT + LAG):
                if i < NH * TT:
                    att_max(i)
                if 0 < i <= NH * TT:
                    att_scale(i - 1)
                if (i - LAG) % 4 == 1 and i > LAG + 1:
                    att_out((i - LAG) // 4 - 1)
            att_out(NH * TT // 4 - 1)
            merged_tiles("m2")
            for nq in range(2):
                prepare(("out2", nq))
                residual([("out2", 4 * nq + n) for n in range(4)], 16, mod_cols2, 4 * nq)
            norm_scale(6, "n4", xT, hT, L)
            r = wait_full(ve, "router")[:, 0:TT * NE].rearrange("p (t e) -> p t e", e=NE)
            top = rt_small[:, 0:TT]
            link(ve.tensor_reduce(top, r, AX.X, ALU.max))
            free("router", "D", ve.tensor_tensor(aff, r, wide(top.unsqueeze(2), P, TT, NE), ALU.subtract))
            wait_freed(ve, "router")
            ve.sem_inc(S["row_max"], 1)
            for t in range(TT):
                free(("ht", t, 1), "D", ve.tensor_copy(h2_tok[:, t, 512:1024], wait_full(ve, ("ht", t, 1))))
            ve.wait_ge(S["exp_done"], 1)
            link(ve.tensor_reduce(rt_small[:, 4:8], aff, AX.X, ALU.add))
            link(ve.reciprocal(rt_small[:, 4:8], rt_small[:, 4:8]))
            ve.tensor_tensor(aff, aff, wide(rt_small[:, 4:8].unsqueeze(2), P, TT, NE), ALU.mult).then_inc(
                S["aff_ready"], 1)
            free("affT", "D", ve.tensor_copy(aff_t[0:NE, :], wait_full(ve, "affT")[0:NE, :]))
            wait_freed(ve, "affT")
            src = aff_t[0:NE, :]
            for i in range(CAP // 8):
                link(ve.max(top8[0:NE, :], src))
                link(ve.match_replace(out=rt_work[0:NE, :], in_to_replace=top8[0:NE, :], in_values=src,
                                      imm_value=-1.0))
                src = rt_work[0:NE, :]
            link(ve.tensor_tensor(chosen[0:NE, :], rt_work[0:NE, :], aff_t[0:NE, :], ALU.not_equal))
            link(ve.tensor_tensor_scan(rank[0:NE, :], chosen[0:NE, :], chosen[0:NE, :], 0.0, ALU.add, ALU.bypass))
            link(ve.tensor_tensor(rank[0:NE, :], rank[0:NE, :], chosen[0:NE, :], ALU.mult))
            ve.tensor_scalar(rank[0:NE, :], rank[0:NE, :], -1.0, None, ALU.add).then_inc(S["rank_ready"], 1)
            free("slotT", "D", ve.tensor_copy(slot_of[:, :, :].rearrange("p a b -> p (a b)"),
                                              wait_full(ve, "slotT")[:, 0:TT * NE]))
            wait_freed(ve, "slotT")
            for t in range(TT):
                s3 = sel[:, t, :].rearrange("p (e j) -> p e j", e=NE)
                ve.tensor_tensor(s3, wide(const("iota").unsqueeze(1), P, NE, CAP),
                                 wide(slot_of[:, t, :].unsqueeze(2), P, NE, CAP), ALU.is_equal).then_inc(
                                     S["sel_ready"], 1)
                ve.wait_ge(S["sel_ready"], t + 1)
                ve.tensor_tensor(wsel[:, t, :].rearrange("p (e j) -> p e j", e=NE), s3,
                                 wide(aff[:, t, :].unsqueeze(2), P, NE, CAP), ALU.mult).then_inc(
                                     S["wsel_ready"], 1)
            for q in range(1, PAIRS, 2):
                free(("wt", q), "D", ve.tensor_copy(wsel_t[:, q, :], wait_full(ve, ("wt", q))))
            ve.sem_inc(S["hm_ready"], 1)
            ve.sem_inc(S["x_added"], 1)
            with ve.Fori(0, PAIRS) as it:
                for fq in range(FQ):
                    ve.wait_ge(S["chunk_free"], it * PAIR_CHUNKS + LOOP_FREE + 4 * fq + 4)
                    ve.wait_ge(S["silu_done"], it * FQ + fq + 1)
                    b = 2 * (fq % 2) + 1
                    ve.tensor_tensor(hmid[:, fq * 512:(fq + 1) * 512], sg[:, fq % 2, :],
                                     ps[:, b * 512:(b + 1) * 512], ALU.mult).then_inc(S["hm_ready"], 1)
                for d in range(KT):
                    ve.wait_ge(S["sc_full"], it * KT + d + 1)
                    b = d % 4
                    ve.scalar_tensor_tensor(xT[:, d, :], ps[:, b * 512:(b + 1) * 512],
                                            mod_cols2[:, 40 + d, 0:1], xT[:, d, :],
                                            ALU.mult, ALU.add).then_inc(S["x_added"], 1)
            norm_scale(7, "nf2", xT, xT, L, weight=lambda k: cols[:, 3, V1["final"] + k:V1["final"] + k + 1])
            for t in range(TT):
                free(("ot", t, 1), "D", ve.tensor_copy(out_sb[:, t, 512:1024], wait_full(ve, ("ot", t, 1))))

        @block.gpsimd
        def _(po):
            po.memset(mean_ones[:, 0, :], 1.0 / D).then_inc(S["ones_ready"], 1)
            po.memset(mean_ones[:, 1, :], 1.0 / DV).then_inc(S["ones_ready"], 1)
            po.memset(eps_col, EPS).then_inc(S["ones_ready"], 1)
            po.memset(sc_pad[:, :, :], 0.0).then_inc(S["ones_ready"], 1)
            po.dma_start(w_route[:, :, :], w_router_2[0].rearrange("(k p) e -> p k e", p=P)).then_inc(
                S["router_in"], 16)

            def rope_cosines(tag, i, g, cs, rawbuf, rcosbuf):
                wait_freed(po, (tag, i))
                if g >= 2:
                    po.wait_ge(S["q_ready"], g - 1)
                po.tensor_tensor(rcosbuf[:, i % 2, :], rawbuf[:, i % 2, :], cs[:, 0, :], ALU.mult).then_inc(
                    S["rope_cos"], 1)

            wait_full(po, ("mod1", "T", 3))
            po.dma_start(rope_cs[:, :, :], rope1).then_inc(S["rope_in"], 16)
            po.wait_ge(S["rope_in"], 16)
            for i in range(8):
                rope_cosines("qk1", i, i, rope_cs, raw, rcos)
            wait_full(po, "S")
            po.dma_start(dist_sb, dist[:, 0:896]).then_inc(S["dist_in"], 16)
            po.dma_start(tpos, dist[:, 896:896 + L]).then_inc(S["dist_in"], 16)
            po.wait_ge(S["dist_in"], 32)
            po.wait_ge(S["decay_ready"], 2)

            def table_argument(h):
                if h >= 2:
                    wait_freed(po, ("s", h - 2, TT - 1))
                c0, c1 = (TT - 1) * P, TT * P
                tb, forward, backward = table[:, h % 2, :], lg[:, h:h + 1], ea[:, 8 + h:9 + h]
                po.tensor_scalar(tb[:, 0:c1], dist_sb[:, 0:c1], 0.0, backward, ALU.min, ALU.mult).then_inc(
                    S["pool_chain"], 1)
                if h:
                    po.wait_ge(S["table_arg"], h)
                po.tensor_scalar(band, dist_sb[:, c0:c1], 0.0, forward, ALU.max, ALU.mult).then_inc(
                    S["pool_chain"], 1)
                po.tensor_scalar(tb[:, c1:], dist_sb[:, c1:], forward, None, ALU.mult).then_inc(
                    S["pool_chain"], 1)
                po.wait_ge(S["pool_chain"], 3 * h + 3)
                po.tensor_tensor(tb[:, c0:c1], tb[:, c0:c1], band, ALU.add).then_inc(S["table_arg"], 1)

            def table_diagonal(h):
                po.wait_ge(S["table_exp"], h + 1)
                tb = table[:, h % 2, 384:512]
                po.tensor_tensor(tb, tb, ident, ALU.add).then_inc(S["table_ready"], 1)

            def decay_queries(j):
                for d in range(2):
                    po.wait_ge(S["table_in"], 2 * j + d + 1)
                    po.tensor_tensor(qdec[:, d, :], qdec[:, d, :], obuf[:, 2 + 2 * j, :], ALU.mult).then_inc(
                        S["qdec_ready"], 1)

            table_argument(0)
            table_argument(1)
            table_diagonal(0)
            decay_queries(0)
            table_diagonal(1)
            for h in range(H1):
                if h + 2 < H1:
                    table_argument(h + 2)
                if h % 2 and h + 1 < H1:
                    decay_queries(h // 2 + 1)
                if h + 2 < H1:
                    table_diagonal(h + 2)
            po.wait_ge(S["g_ready"], KT)
            po.dma_start(dftd[:, :, :], dft_dim).then_inc(S["dist_in"], 16)

            def add_parts(tag, base):
                merged, gates = merge_views[tag]
                for nq in range(2):
                    for n in range(4):
                        wait_freed(po, (tag, "proj", "b", nq, n))
                        po.tensor_tensor(merged[:, 4 * nq + n, :], merged[:, 4 * nq + n, :], gates[:, 1, n, :],
                                         ALU.add).then_inc(S["merged_ready"], 1)

            add_parts("m1", 0)
            wait_full(po, ("down", KT - 1))
            po.dma_start(ln_rows[:, 0, :], gmlp_ln_g_2[0].partition_broadcast(P)).then_inc(S["stage2_in"], 16)
            po.dma_start(ln_rows[:, 1, :], gmlp_ln_b_2[0].partition_broadcast(P)).then_inc(S["stage2_in"], 16)
            po.dma_start(bs_rows[:, :, :], b_spatial_2[0].partition_broadcast(P)).then_inc(S["stage2_in"], 16)
            po.dma_start(ws_raw[:, :, :], w_spatial_2[0].rearrange("g p q -> p g q")).then_inc(
                S["stage2_in"], 16)
            for g in range(NG):
                wait_freed(po, ("mix", g))
                wait_freed(po, ("u", g))
                po.tensor_tensor(ug[:, g, :], ug[:, g, :], mixed[:, g % 2, :], ALU.mult).then_inc(
                    S["ya_ready"], 1)
            wait_full(po, ("mix", NG - 1))
            po.dma_start(rope_cs2[:, :, :], rope2).then_inc(S["rope_in"], 16)
            po.wait_ge(S["rope_in"], 32)
            po.wait_ge(S["ya_ready"], NG)
            for i in range(8):
                rope_cosines("q2", i, 8 + i, rope_cs2, raw2, rcos2)
            for i in range(2):
                rope_cosines("k2", i, 16 + i, rope_cs2, raw2, rcos2)
            add_parts("m2", 8)


def rope_table(angles, sign_rows):
    return np.stack([np.cos(angles), np.sin(angles)], 1)


def shape_constants():
    f = np.float32
    c = np.zeros((P, NCONST), f)

    def put(name, v):
        a, b = CONST[name]
        c[:, a:b] = v

    p, n = np.arange(P)[:, None], np.arange(P)[None, :]
    put("ident", p == n)

    def swap(half):
        m = np.zeros((P, P), f)
        for i in range(P):
            if i % (2 * half) < half:
                m[i + half, i] = -1.0
            else:
                m[i - half, i] = 1.0
        return m

    put("swap1", swap(32))
    put("swap2", swap(16))
    mask = np.zeros((P, 2, P), f)
    mask[:, 0] = np.where(n >= p, 0.0, -1e30)
    mask[:, 1] = np.where(n <= p, 0.0, -1e30)
    put("mask", mask.reshape(P, 2 * P))
    put("iota", np.arange(CAP)[None, :])
    put("age", np.concatenate([LC - 1 - p, LC - 1 - P - p, p, P + p], 1))
    sel = np.zeros((P, 2), f)
    for g in range(4):
        sel[32 * g, 0] = sel[32 * g + 1, 1] = 1.0
    put("modsel", sel)

    t = np.arange(L)
    row, col = (t // 64).astype(f), (t % 64).astype(f)
    inv = (f(10000.0) ** (-np.arange(16, dtype=f) / f(16))).astype(f)
    a1 = np.concatenate([row[None] * inv[:, None], col[None] * inv[:, None]], 0)
    a1 = np.tile(a1, (4, 1)).astype(np.float64)
    a2 = np.concatenate([np.tile(row[None] * inv[:, None], (2, 1)), np.tile(col[None] * inv[:, None], (2, 1))], 0)
    a2 = np.tile(a2, (2, 1)).astype(np.float64)
    r1, r2 = rope_table(a1, 32).astype(f), rope_table(a2, 16).astype(f)

    k = np.arange(L)
    w = 2 * np.pi * ((k[:, None] * k[None, :]) % L) / L
    s = 1.0 / np.sqrt(L * 128.0)
    dl = np.stack([np.cos(w), np.sin(w)], 0) * s
    dl = dl.reshape(2, TT, P, L).transpose(2, 0, 1, 3)
    wd = 2 * np.pi * ((p * n) % P) / P
    dd = np.stack([np.cos(wd), -np.sin(wd)], 1)
    dist = np.concatenate([np.arange(896)[None, :] - 384 - p, np.tile(np.arange(1, L + 1), (P, 1))], 1)
    return dict(consts=c, rope1=r1, rope2=r2,
                dft_len=np.ascontiguousarray(dl.reshape(P, 4, 1024)).astype(f),
                dft_dim=dd.astype(f), dist=dist.astype(f))


_INS = ["x", "c", "ctx", "c_ctx", "w_mod", "b_mod", "norm1_w", "w_in", "ret_decay_f", "ret_decay_b",
        "w_ret_out", "w_four_out", "w_branch_gate", "b_branch_gate", "w_out", "norm2_w", "w_up",
        "conv_w", "conv_b", "w_down", "final_norm_w", "c_2", "ctx_2", "c_ctx_2", "w_ada_2", "b_ada_2",
        "norm1_g_2", "w_in_2", "b_merge_gate_2", "gmlp_ln_g_2", "gmlp_ln_b_2", "w_spatial_2",
        "b_spatial_2", "attn_sink_2", "w_proj_a_2", "w_proj_b_2", "w_out_2", "norm2_g_2", "w_router_2",
        "w_exp_gate_2", "w_exp_up_2", "w_exp_down_2", "final_g_2"]


def kernel(**inputs):
    import concourse.bacc as bacc
    from concourse.bass_utils import run_bass_kernel_spmd

    nc = bacc.Bacc("TRN2", target_bir_lowering=False, num_devices=1)
    arrays, args = {}, []
    tensors = {n: np.ascontiguousarray(inputs[n]) for n in _INS} | shape_constants()
    for name, a in tensors.items():
        arrays[f"in_{name}"] = a
        args.append(nc.dram_tensor(f"in_{name}", a.shape, mybir.dt.from_np(a.dtype), kind="ExternalInput").ap())
    out = nc.dram_tensor("out_0", (1, L, D), F32, kind="ExternalOutput").ap()
    build_two_blocks(nc, *args, out)
    r = run_bass_kernel_spmd(nc, [arrays], core_ids=[0])
    return r.results[0]["out_0"]
```

```python
from contextlib import ExitStack

import numpy as np

import concourse.bass as bass
from concourse import mybir

F32 = mybir.dt.float32
F32R = mybir.dt.float32r
ALU = mybir.AluOpType
ACT = mybir.ActivationFunctionType
AX = mybir.AxisListType

P = 128
D = 1024
KT = D // P
L = 512
TT = L // P
LC = 256
CT = LC // P
SLOTS = 6
RAW = 3
HIGH = 3
SLOT = 4096
EPS = 1e-6

H1, DK, DV = 8, 64, 128
FFN = 2816
FT = FFN // P
UPN = FFN // 256
FG = 4

NH, NKV, HD = 16, 4, 64
LAG = 2
NG = 8
AW = 18100
NE, DE, CAP = 16, 2048, 64
PAIRS = NE // 2
FQ = DE // 512
PAIR_CHUNKS = 6 * FQ

V1 = dict(c=0, c_ctx=8, norm1=16, norm2=24, final=32, b_gate=40, b_mod=56)
V2 = dict(w0=0, w1=44)
V3 = dict(w2=0, b=44)
V4 = V1

CONST = {}
_n = 0
for _name, _w in (("ident", 128), ("swap1", 128), ("swap2", 128), ("mask", 256), ("iota", 64),
                  ("age", 4), ("modsel", 2), ("routesel", NE)):
    CONST[_name] = (_n, _n + _w)
    _n += _w
NCONST = _n


MERGE = [(kind, part, nq) for kind in ("gate", "proj") for part in "ab" for nq in range(2)]


class Banks:

    def __init__(self):
        self.tiles, self.where, self.units = [], {}, []

    def add(self, name, by, width=1):
        if width == 2 and len(self.units) % 2:
            self.units.append(None)
        i = len(self.tiles)
        assert name not in self.where, name
        nth = sum(1 for t in self.tiles if t[1] == by) + 1
        self.tiles.append((name, by, len(self.units), nth, width))
        self.where[name] = i
        self.units += [i] * width

    def bank(self, name):
        return self.tiles[self.where[name]][2] % 8

    def before(self, name):
        _, _, u, _, w = self.tiles[self.where[name]]
        need = {}
        for v in range(u, u + w):
            for back in range(v - 8, -1, -8):
                if self.units[back] is not None:
                    _, by, _, nth, _ = self.tiles[self.units[back]]
                    need[by] = max(need.get(by, 0), nth)
                    break
        return sorted(need.items())


def plan_banks():
    b = Banks()
    b.add("vecs", "D")
    for k in range(KT):
        b.add(("xT", k), "AD"[k % 2])
    for k in range(KT // 2):
        b.add(("cT", k), "AD"[k % 2])

    def norm(tag):
        b.add(tag, "A")
        b.add((tag, "wide"), "D")

    def mod_step(tag, c, first):
        if c > first:
            b.add((tag, "T", c - 1), "D")
        b.add((tag, c), "A")

    def merge(tag):
        for i, (kind, part, nq) in enumerate(MERGE):
            for n in range(4):
                b.add((tag, kind, part, nq, n), "A" if kind == "gate" else "D")
            if tag == "m1":
                mod_step("mod1", 4 + i, 4)
        if tag == "m1":
            b.add(("mod1", "T", 11), "D")

    def rope(tag, n):
        for i in range(n + 1):
            if i < n:
                b.add((tag, i), "A")
            if i:
                b.add((tag, "swap", i - 1), "D")

    mod_step("mod1", 0, 0)
    for c, tag in ((1, "n1"), (2, "nc")):
        b.add(tag, "A")
        mod_step("mod1", c, 0)
        b.add((tag, "wide"), "D")
    mod_step("mod1", 3, 0)
    b.add(("mod1", "T", 3), "D")
    for i in range(4):
        b.add(("qk1", i), "A")
    for i in range(4):
        b.add(("qk1", "swap", i), "D")
    for t in range(CT):
        b.add(("kc", t), "A")
    for i in range(5):
        if i < 4:
            b.add(("qk1", 4 + i), "A")
        if i:
            b.add(("qk1", "swap", 3 + i), "D")
    for hh in range(2):
        for t in range(CT):
            b.add(("vc", hh, t), "D")
        for t in range(TT):
            b.add(("v", hh, t), "D")
    b.add("S", "D", 2)
    for h in range(H1 + 1):
        if h:
            b.add(("o", h - 1), "A")
        if h < H1:
            for i in range(TT):
                b.add(("s", h, i), "D")
        if h:
            b.add(("var", h - 1), "A")
    for n in range(KT):
        b.add(("g", n), "A")
    for t in range(TT):
        b.add(("f", t), "A")
    for g in range(FG):
        for m in range(2):
            b.add(("fa", g, m), "A")
    for g in range(FG):
        b.add(("z", g), "D")
    merge("m1")
    for n in range(KT):
        b.add(("out1", n), "D")
        if n == 3:
            mod_step("mod2", 0, 0)
    norm("n2")
    for j in range(UPN):
        for n in range(4):
            b.add(("up", j, n), "D")
        mod_step("mod2", j + 1, 0)
    b.add(("mod2", "T", 11), "D")
    for n in range(KT):
        b.add(("down", n), "D")
    b.add("nf1", "A")
    for k in range(KT // 2):
        b.add(("cT2", k), "AD"[k % 2])
    b.add(("nf1", "wide"), "D")
    norm("n3")
    for n in range(KT):
        if n == 4:
            b.add("nc2", "A")
        b.add(("u", n), "A")
        if n == 4:
            b.add(("nc2", "wide"), "D")
    for hh in range(2):
        for t in range(TT):
            b.add(("va", hh, t), "A")
    b.add(("ws", 0), "A")
    b.add(("ws", 1), "A")
    for g in range(NG):
        b.add(("mix", g), "D")
    rope("q2", 8)
    for i in range(3):
        if i < 2:
            b.add(("k2", i), "A")
        if i:
            b.add(("k2", "swap", i - 1), "D")
    for t in range(TT):
        b.add(("vb", t), "A")
    for i in range(2):
        b.add(("kc2", i), "D")
    for t in range(CT):
        b.add(("vc2", t), "A")
    for i in range(NH * TT + LAG):
        if i < NH * TT:
            b.add(("as", i), "A", 2)
        if i >= LAG:
            if (i - LAG) % 4 == 1 and i > LAG + 1:
                b.add(("pv", (i - LAG) // 4 - 1), "D")
            b.add(("at", i - LAG), "A", 2)
    b.add(("pv", NH * TT // 4 - 1), "D")
    merge("m2")
    for n in range(KT):
        b.add(("out2", n), "D")
    norm("n4")
    b.add("routeT", "A")
    b.add("router", "D")
    for t in range(TT):
        for hh in range(2):
            b.add(("ht", t, hh), "AD"[hh])
    b.add("affT", "D")
    b.add("slotT", "D")
    for q in range(PAIRS):
        b.add(("wt", q), "AD"[q % 2])
    b.add("nf2", "A")
    for t in range(TT):
        for hh in range(2):
            b.add(("ot", t, hh), "AD"[hh])
    return b


def build_two_blocks(nc, x, c, ctx, c_ctx, w_mod, b_mod, norm1_w, w_in, ret_decay_f, ret_decay_b,
                     w_ret_out, w_four_out, w_branch_gate, b_branch_gate, w_out, norm2_w, w_up,
                     conv_w, conv_b, w_down, final_norm_w, c_2, ctx_2, c_ctx_2, w_ada_2, b_ada_2,
                     norm1_g_2, w_in_2, b_merge_gate_2, gmlp_ln_g_2, gmlp_ln_b_2, w_spatial_2,
                     b_spatial_2, attn_sink_2, w_proj_a_2, w_proj_b_2, w_out_2, norm2_g_2,
                     w_router_2, w_exp_gate_2, w_exp_up_2, w_exp_down_2, final_g_2,
                     consts, rope1, rope2, dft_len, dft_dim, dist, out):
    banks = plan_banks()
    es = ExitStack()
    with es:
        def sb(name, *shape):
            return es.enter_context(nc.sbuf_tensor(name, [P, *shape], F32))

        def two_types(name, *shape):
            with nc.sbuf_tensor(name + "_r", [P, *shape], F32R) as r:
                pass
            return sb(name, *shape), r

        slots, slots_r = zip(*(two_types(f"weights{i}", SLOT) for i in range(SLOTS)))
        hT, hT_r = two_types("hT", KT, L)
        arena, arena_r = two_types("arena", AW)
        xT = sb("xT", KT, L)
        cst = sb("cst", NCONST)
        mean_ones = sb("mean_ones", 2, P)
        cols = sb("cols", 4, P)
        mod_cols, mod_cols2 = sb("mod_cols", 48, 2), sb("mod_cols2", 48, 2)
        scale_a = sb("scale_a", 3, KT)
        sc_pad = sb("sc_pad", KT, 32)
        small = sb("small", 160)
        ps = es.enter_context(nc.psum_tensor("ps", [P, 8 * 512], F32))

        def const(name):
            a, b = CONST[name]
            return cst[:, a:b]

        ident = const("ident")
        eps_col = small[:, 0:1]

        def at(off, *dims, rounded=False):
            n = int(np.prod(dims))
            assert off + n <= AW, (off, n)
            v = (arena_r if rounded else arena)[:, off:off + n]
            if len(dims) == 2:
                v = v.rearrange("p (a b) -> p a b", a=dims[0])
            if len(dims) == 3:
                v = v.rearrange("p (a b c) -> p a b c", a=dims[0], b=dims[1])
            if len(dims) == 4:
                v = v.rearrange("p (a b c d) -> p a b c d", a=dims[0], b=dims[1], c=dims[2])
            return v

        def slot(i, k):
            return slots[i % SLOTS][:, :].rearrange("p (k n) -> p k n", k=k)

        names = """landed0 landed1 landed2 landed3 landed4 landed5 chunk_free tile_full freed_a freed_d consts_in
            vecs_in bcast_in dve_chain pool_chain ones_ready silu_ready mods_ready high_ready low_ready
            loads_turn wsel_half merged_high merged_low branch_high branch_low act_high act_low h_plain
            h_rounded h4_ready sq_ready recip_ready scaled h_ready rope_cos rope_in q_ready kw_ready
            decay_ready qdec_ready dist_in table_in table_arg table_exp table_ready o_square g_ready
            merged_ready conv_mid gelu_ready act_ready ln_ready ln_stats ln_root ya_ready row_max exp_done
            p_scaled sink_exp kdup_ready router_in aff_ready rank_ready sel_ready wsel_ready xe_full
            xe_ready silu_done hm_ready hmt_full hmt_ready y_ready sc_full x_added stored decay_exp
            stage2_in""".split()
        S = {n: es.enter_context(nc.semaphore(n)) for n in names}
        FREED = {"A": S["freed_a"], "D": S["freed_d"]}

        def tile(name):
            w = banks.tiles[banks.where[name]][4]
            k = banks.bank(name)
            return ps[:, k * 512:k * 512 + 512 * w]

        filled = []

        def claim(pe, name):
            for by, count in banks.before(name):
                pe.wait_ge(FREED[by], count)
            return tile(name)

        def fill(name, last):
            assert banks.where[name] == len(filled), name
            filled.append(name)
            last.then_inc(S["tile_full"], 1)

        def wait_full(eng, name):
            eng.wait_ge(S["tile_full"], banks.where[name] + 1)
            return tile(name)

        evacuated = {"A": 0, "D": 0}

        def free(name, by, last):
            _, b, _, nth, _ = banks.tiles[banks.where[name]]
            evacuated[by] += 1
            assert b == by and nth == evacuated[by], name
            if last is None:
                nc.vector.sem_inc(FREED[by], 1)
            else:
                last.then_inc(FREED[by], 1)

        def wait_freed(eng, name):
            _, by, _, nth, _ = banks.tiles[banks.where[name]]
            eng.wait_ge(FREED[by], nth)

        def kmaj(w, n0, n1):
            return w[:, n0:n1].rearrange("(k p) n -> p k n", p=P)

        chunks = []
        chunk_at = {}

        def chunk(name, *parts):
            chunk_at[name] = len(chunks)
            chunks.append(parts)

        chunk("x", x[0].rearrange("(t p) d -> p t d", p=P))
        chunk("ctx", ctx[0].rearrange("(t p) d -> p t d", p=P))
        def mod1(i):
            chunk(("mod1", i), kmaj(w_mod[0], 512 * i, 512 * i + 512))

        def in1(i):
            chunk(("in1", i), kmaj(w_in[0], 512 * i, 512 * i + 512))

        for i in range(3):
            mod1(i)
        in1(0)
        mod1(3)
        for i in range(1, 7):
            in1(i)
        chunk("dft", dft_len)
        for i, (kind, part, nq) in enumerate(MERGE):
            w, o = {("gate", "a"): (w_branch_gate, D), ("gate", "b"): (w_branch_gate, 0),
                    ("proj", "a"): (w_four_out, 0), ("proj", "b"): (w_ret_out, 0)}[kind, part]
            chunk(("m1", kind, part, nq), kmaj(w[0], o + 512 * nq, o + 512 * nq + 512))
            mod1(4 + i)
        def mod2(i):
            chunk(("mod2", i), kmaj(w_ada_2[0], 512 * i, 512 * i + 512))

        for nq in range(2):
            chunk(("out1", nq), kmaj(w_out[0], 512 * nq, 512 * nq + 512))
            if nq == 0:
                mod2(0)
        for j in range(UPN):
            chunk(("up", j), kmaj(w_up[0], 256 * j, 256 * j + 256),
                  kmaj(w_up[0], FFN + 256 * j, FFN + 256 * j + 256))
            mod2(j + 1)
        for j in range(6):
            part = w_down[0][512 * j:min(512 * j + 512, FFN), :].rearrange("(k p) n -> p k n", p=P)
            if j < 5:
                chunk(("down", j), part)
            else:
                chunk(("down", j), part, ctx_2[0].rearrange("(t p) d -> p t d", p=P))
        for i in range(7):
            chunk(("in2", i), kmaj(w_in_2[0], 512 * i, 512 * i + 512))
        for kind, part, nq in MERGE:
            w, o = {("gate", "a"): (w_in_2, 3584), ("gate", "b"): (w_in_2, 3584 + D),
                    ("proj", "a"): (w_proj_a_2, 0), ("proj", "b"): (w_proj_b_2, 0)}[kind, part]
            chunk(("m2", kind, part, nq), kmaj(w[0], o + 512 * nq, o + 512 * nq + 512))
        for nq in range(2):
            chunk(("out2", nq), kmaj(w_out_2[0], 512 * nq, 512 * nq + 512))
        NCH = len(chunks)
        order = {n: name for name, n in chunk_at.items()}
        assert NCH % RAW == 0
        split = [n for n, name in enumerate(chunk_at)
                 if name[0] in ("in1", "in2", "m1", "m2", "up", "down", "out1", "out2")]

        def landed(eng, name):
            n = chunk_at[name]
            loads = sum(len(chunks[m]) for m in range(n % RAW, n + 1, RAW))
            eng.wait_ge(S[f"landed{n % RAW}"], 16 * loads)
            return n % RAW

        def split_words(i):
            name = order[split[i]]
            return SLOT // 2 if name == ("down", 5) or name[:3] == ("m1", "proj", "a") else SLOT

        gate_split = split.index(chunk_at["m2", "gate", "a", 0])

        def high_slot(i):
            return HIGH + i % 2

        def next_splits(issued, name):
            n = chunk_at[name]
            ahead = [i for i, m in enumerate(split) if m > n][:1]
            upto = ahead[0] + 1 if ahead and split[ahead[0]] <= n + 2 else len([m for m in split if m <= n])
            todo = range(issued[0], upto)
            issued[0] = max(issued[0], upto)
            return todo

        last_tile = {"x": ("xT", 7), "ctx": ("cT", 3), "dft": ("fa", 3, 1), ("down", 5): ("cT2", 3),
                     ("in1", 0): ("qk1", 3), ("in1", 1): ("qk1", 7), ("in1", 2): ("v", 0, 3),
                     ("in1", 3): ("v", 1, 3), ("in1", 4): ("g", 3), ("in1", 5): ("g", 7), ("in1", 6): ("f", 3),
                     ("in2", 0): ("u", 3), ("in2", 1): ("u", 7), ("in2", 2): ("va", 0, 3),
                     ("in2", 3): ("va", 1, 3), ("in2", 4): ("q2", 3), ("in2", 5): ("q2", 7),
                     ("in2", 6): ("vc2", 1)}
        for i in range(12):
            last_tile["mod1", i], last_tile["mod2", i] = ("mod1", i), ("mod2", i)
        for nq in range(2):
            for tag in ("m1", "m2"):
                for part in "ab":
                    for kind in ("gate", "proj"):
                        last_tile[tag, kind, part, nq] = (tag, kind, part, nq, 3)
            last_tile["out1", nq], last_tile["out2", nq] = ("out1", 4 * nq + 3), ("out2", 4 * nq + 3)
        for j in range(UPN):
            last_tile["up", j] = ("up", j, 3)

        def wait_spent(sp, n):
            if order[n] in last_tile:
                sp.wait_ge(S["tile_full"], banks.where[last_tile[order[n]]] + 1)
            else:
                sp.wait_ge(S["chunk_free"], order[n][1] + 1)

        LOOP_FREE = 5

        merge_views = {"m1": (at(5120, KT, L), at(13312, KT, L)),
                       "m2": (at(8192, KT, L), at(12288, KT, L))}
        branches = {"m1": ((11264, FG), (0, KT)), "m2": ((0, KT), (4096, KT))}
        branch_views = {t: [at(o, k, L) for o, k in v] for t, v in branches.items()}
        branch_lows = {t: [at(o, k, L, rounded=True) for o, k in v] for t, v in branches.items()}
        norm_tags = ["n1", "nc", "n2", "nf1", "n3", "nc2", "n4", "nf2"]
        sq8 = at(0, KT, L)
        merged_low = {"m1": at(5120, KT, L, rounded=True), "m2": at(8192, KT, L, rounded=True)}
        sqc = at(4096, KT, LC)

        def squares(m):
            return sqc if norm_tags[m] == "nc2" else sq8

        root, recip = small[:, 40:44], small[:, 44:48]
        rows_v = at(5120, 4, P)
        m_sbs = [at(5632, 2, L), at(9216, 2, L), at(16384, 2, L)]

        def m_sb(tag, c):
            return m_sbs[2 if tag == "mod2" else 1 if c >= 4 else 0][:, c % 2, :]

        h_high = slots_r[SLOTS - 1][:, :].rearrange("p (k n) -> p k n", k=KT)
        h_low = hT_r
        h_parts = (lambda k, a, b: h_high[:, k, a:b], lambda k, a, b: h_low[:, k, a:b])

        hc = at(10240, KT, LC)
        hc_highs = [at(0, 4, LC, rounded=True), at(9216, 4, LC, rounded=True)]
        hc_low = at(10240, KT, LC, rounded=True)
        hc_parts = (lambda k, a, b: hc_highs[k // 4][:, k % 4, a:b], lambda k, a, b: hc_low[:, k, a:b])
        obuf = at(0, 10, L)
        v1 = at(5120, TT, D)
        rope_cs = at(5120, 2, L)
        raw = at(6144, 2, L)
        rcos = at(7168, 2, L)
        rsin = at(8192, 2, L)
        kc = at(12288, CT, 512)
        kw = at(13312, 2, CT, 512)
        vc = at(15360, CT, D)
        state = at(9216, 2, 4, P)
        dist_sb = at(10240, 896)
        tpos = at(11136, L)
        probs = at(11648, 4, L)
        table = at(13696, 2, 896)
        qdec = at(15488, 2, L)
        osq = at(16512, L)
        band = at(17600, P)
        rinv = at(17024, L)
        f_tok = at(5120, TT, 512)
        fa = at(7168, FG, 2, L)
        z = at(11264, FG, L)
        dftd = at(13312, 2, P)
        act = at(0, FT, L)
        act_low_v = at(0, FT, L, rounded=True)
        act_highs = [at(14336, 4, L, rounded=True), h_high, h_low, at(11264, 2, L, rounded=True)]

        def act_high(k):
            return act_highs[(k + 4) // 8][:, k if k < 4 else (k - 4) % 8, :]

        conv = at(11264, 4, L)
        gelu_a = at(13312, 2, L)
        hc2 = at(14336, KT, LC)
        hc2_slot = high_slot(split.index(chunk_at["in2", 5]))
        hc2_high = slots_r[hc2_slot][:, 0:KT * LC].rearrange("p (k n) -> p k n", k=KT)
        hc2_low = at(14336, KT, LC, rounded=True)
        hc2_parts = (lambda k, a, b: hc2_high[:, k, a:b], lambda k, a, b: hc2_low[:, k, a:b])
        ug = at(0, KT, L)
        va = at(4096, TT, D)
        ln_rows = at(8192, 2, D)
        bs_rows = at(10240, NG, P)
        ws_t = at(11264, NG, P)
        ws_raw = at(12288, NG, P)
        mixed = at(13312, 2, L)
        stats = at(16384, TT, 16)
        q2 = at(4096, KT, L)
        kdup = at(8192, NKV, L)
        krot = at(10240, 2, L)
        rope_cs2 = at(11264, 2, L)
        raw2 = at(12288, 2, L)
        rcos2 = at(13312, 2, L)
        rsin2 = at(16384, 2, L)
        vb = at(11264, TT, NKV * HD)
        kcdup = at(12288, NKV, LC)
        vcx = at(10240, CT, NKV * HD)
        NPB = 3
        prob2 = at(13312, NPB, 640)
        prob_ts = [at(15232, 5, 4, P), slots[high_slot(gate_split - 1)][:, 0:5 * 4 * P].rearrange(
            "p (a b c) -> p a b c", a=5, b=4)]
        h2_tok = at(0, TT, D)
        sel = at(4096, TT, D)
        wsel_t = at(8192, PAIRS, L)
        xe = at(12288, KT, P)
        y_sb = at(13312, D)
        sg = at(14336, 2, 512)
        rt_work = at(15360, L)
        aff_t = at(15872, L)
        rank = at(16384, L)
        chosen = at(16896, L)
        aff = at(17408, TT, NE)
        rt_small = at(17472, 64)
        slot_of = at(17536, TT, NE)
        top8 = at(17600, 8)
        wsel = hT[:, :, :].rearrange("p a b -> p (a b)").rearrange("p (t n) -> p t n", t=TT)
        hmid = hT[:, 0:4, :].rearrange("p a b -> p (a b)")
        hmid_t = hT[:, 4:8, :].rearrange("p a b -> p (a b)").rearrange("p (k n) -> p k n", k=16)
        out_sb = at(0, TT, D)
        decay = small[:, 8:24]
        sink = small[:, 24:40]
        ea = small[:, 64:80]
        lg = small[:, 80:96]
        qcol = small[:, 96:108].rearrange("p (a b) -> p a b", a=3)
        ctxw = small[:, 112:144].rearrange("p (d t h) -> p d t h", d=2, t=CT)
        neg_m = small[:, 144:148]
        den = small[:, 148:152]
        sink_e = small[:, 152:156]
        negmean = at(17536, 8)
        row_top = at(17792, 4)

        block = es.enter_context(nc.Block())

        @block.sync
        def _(sp):
            sp.dma_start(cst[:, :], consts).then_inc(S["consts_in"], 16)
            rows = [
                (0, V1["c"], c), (0, V1["c_ctx"], c_ctx), (0, V1["norm1"], norm1_w), (0, V1["norm2"], norm2_w),
                (0, V1["final"], final_norm_w), (0, V1["b_gate"], b_branch_gate), (0, V1["b_mod"], b_mod),
                (3, V4["c"], c_2), (3, V4["c_ctx"], c_ctx_2), (3, V4["norm1"], norm1_g_2),
                (3, V4["norm2"], norm2_g_2), (3, V4["final"], final_g_2), (3, V4["b_gate"], b_merge_gate_2),
                (3, V4["b_mod"], b_ada_2), (2, V3["b"], conv_b)]
            for i, r, v in rows:
                flat = v if len(v.shape) == 1 else v.rearrange("a n -> (a n)")
                n = flat.shape[0] // P
                sp.dma_start(rows_v[r:r + n, i, :], flat.rearrange("(r p) -> r p", p=P)).then_inc(S["vecs_in"], 16)
            for i, r, t in ((1, V2["w0"], 0), (1, V2["w1"], 1), (2, V3["w2"], 2)):
                sp.dma_start(rows_v[r:r + 44, i, :],
                             conv_w[0, t].rearrange("(r p) -> r p", p=P)).then_inc(S["vecs_in"], 16)
            for k, v in enumerate((ret_decay_f[0], ret_decay_b[0])):
                sp.dma_start(small[:, 8 + 8 * k:16 + 8 * k], v.partition_broadcast(P)).then_inc(S["bcast_in"], 16)
            sp.dma_start(small[:, 24:40], attn_sink_2[0].partition_broadcast(P)).then_inc(S["bcast_in"], 16)
            for n in range(NCH):
                if n >= RAW:
                    wait_spent(sp, n - RAW)
                sl = n % RAW
                src = chunks[n]
                if len(src) == 1 or src[0].shape[2] == D:
                    o = 0
                    for part in src:
                        k, w = part.shape[1], part.shape[2]
                        sp.dma_start(slots[sl][:, o:o + k * w].rearrange("p (k n) -> p k n", k=k),
                                     part).then_inc(S[f"landed{sl}"], 16)
                        o += k * w
                else:
                    v = slot(sl, 8)
                    sp.dma_start(v[:, :, 0:256], src[0]).then_inc(S[f"landed{sl}"], 16)
                    sp.dma_start(v[:, :, 256:512], src[1]).then_inc(S[f"landed{sl}"], 16)
            def gate_up(w, it, e, fq):
                return w[0, e:, :, :][bass.ds(it * 2, 1), :, 512 * fq:512 * fq + 512].rearrange(
                    "a (k p) n -> p (a k) n", p=P)

            def down(it, e, kq):
                return w_exp_down_2[0, e:, :, :][bass.ds(it * 2, 1), 512 * kq:512 * kq + 512, :].rearrange(
                    "a (k p) n -> p (a k) n", p=P)

            def load(it, m, ahead=0):
                if m < 4 * FQ:
                    fq, gu, e = m // 4, m // 2 % 2, m % 2
                    src = gate_up((w_exp_gate_2, w_exp_up_2)[gu], it, 2 * ahead + e, fq)
                else:
                    kq, e = (m - 4 * FQ) // 2, m % 2
                    src = down(it, 2 * ahead + e, kq)
                sp.dma_start(slot(m, 8 if m < 4 * FQ else 4), src).then_inc(S[f"landed{m % SLOTS}"], 16)

            def load_when_free(it, m, ahead=0):
                sp.wait_ge(S["chunk_free"], it * PAIR_CHUNKS + (ahead * PAIR_CHUNKS + LOOP_FREE + m - SLOTS + 1))
                if m == 4 * FQ:
                    sp.sem_inc(S["loads_turn"], 1)
                load(it, m, ahead)

            for m in range(RAW):
                wait_spent(sp, NCH - RAW + m)
                load(0, m)
            for i in sorted(range(len(split) - 2, len(split)), key=high_slot):
                wait_spent(sp, split[i])
                load(0, high_slot(i))
            load(0, SLOTS - 1)
            with sp.Fori(0, PAIRS - 1) as it:
                for m in range(SLOTS, PAIR_CHUNKS):
                    load_when_free(it, m)
                for m in range(SLOTS):
                    load_when_free(it, m, 1)
            for m in range(SLOTS, PAIR_CHUNKS):
                load_when_free(PAIRS - 1, m)
            for t in range(TT):
                for hh in range(2):
                    wait_freed(sp, ("ot", t, hh))
                sp.dma_start(out[0, t * P:(t + 1) * P, :], out_sb[:, t, :]).then_inc(S["stored"], 16)
            sp.wait_ge(S["stored"], 16 * TT)

        @block.tensor
        def _(pe):
            def parts_of(cname, kt=KT):
                if chunk_at[cname] in split:
                    i = split.index(chunk_at[cname])
                    pe.wait_ge(S["low_ready"], i + 1)
                    sl = chunk_at[cname] % RAW, high_slot(i)
                    low, high = (slots_r[q][:, 0:split_words(i)].rearrange("p (k n) -> p k n", k=kt) for q in sl)
                    return high, low
                return (slots[landed(pe, cname)][:, 0:kt * 512].rearrange("p (k n) -> p k n", k=kt),)

            def product(t, w, x, k, kt, w_range, x_range, w_first, kw=None):
                pairs = [(0, 0), (0, 1), (1, 0)] if len(w) == 2 else [(0, 0)]
                for n, (i, j) in enumerate(pairs):
                    a, b = w[i][:, k if kw is None else kw, w_range[0]:w_range[1]], x[j](k, *x_range)
                    last = pe.matmul(t, a if w_first else b, b if w_first else a,
                                     start=(k == 0 and n == 0), stop=(k == kt - 1 and n == len(pairs) - 1))
                return last

            def feature_tiles(cname, tnames, src, kt=KT, width=512, c0=0):
                w = parts_of(cname, kt)
                for n, tn in enumerate(tnames):
                    t = claim(pe, tn)[:, 0:width]
                    for k in range(kt):
                        last = product(t, w, src, k, kt, (c0 + n * P, c0 + n * P + P), (0, width), True)
                    fill(tn, last)

            def first_tiles(cname, tnames, x, sem, ready, kt=KT):
                w = parts_of(cname, kt)
                ts = [claim(pe, tn) for tn in tnames]
                for k in range(kt):
                    pe.wait_ge(S[sem], ready + k + 1)
                    for n, t in enumerate(ts):
                        last = product(t, w, x, k, kt, (n * P, n * P + P), (0, L), True)
                        if k == kt - 1:
                            fill(tnames[n], last)

            def token_tiles(cname, tnames, src, c0=0, width=512):
                w = parts_of(cname)
                for t, tn in enumerate(tnames):
                    o = claim(pe, tn)[:, 0:width]
                    for k in range(KT):
                        last = product(o, w, src, k, KT, (c0, c0 + width), (t * P, t * P + P), False)
                    fill(tn, last)

            def turn(name, parts):
                t = claim(pe, name)
                for o, src in parts:
                    rows = src.shape[0]
                    last = pe.transpose(t[:, o:o + rows], src, ident[0:rows, 0:rows])
                fill(name, last)

            def norm_step(m, tag, width, k):
                t = claim(pe, tag) if k == 0 else tile(tag)
                pe.wait_ge(S["sq_ready"], KT * m + k + 1)
                for j in range(width // P):
                    last = pe.matmul(t[:, j:j + 1], squares(m)[:, k, j * P:(j + 1) * P], mean_ones[:, 0, 0:1],
                                     start=(k + j == 0), stop=(k == KT - 1 and j == width // P - 1))
                if k == KT - 1:
                    fill(tag, last)

            def norm(m, tag, width, between=None, k0=0):
                for k in range(k0, KT):
                    norm_step(m, tag, width, k)
                if between:
                    between()
                pe.wait_ge(S["recip_ready"], m + 1)
                t = claim(pe, (tag, "wide"))
                for j in range(width // P):
                    last = pe.matmul(t[:, j * P:(j + 1) * P], recip[:, j:j + 1].broadcast_to([P, P]), ident,
                                     start=True, stop=True)
                fill((tag, "wide"), last)

            def mod_turn(tag, c):
                wait_freed(pe, (tag, c))
                t = claim(pe, (tag, "T", c))
                for j in range(4):
                    last = pe.matmul(t[:, 2 * j:2 * j + 2], m_sb(tag, c)[:, j * P:(j + 1) * P],
                                     const("modsel"), start=True, stop=True)
                fill((tag, "T", c), last)

            def mod_step(tag, c, first):
                if c > first:
                    mod_turn(tag, c - 1)
                w = slot(landed(pe, (tag, c)), KT)
                t = claim(pe, (tag, c))
                for k in range(KT):
                    g = 32 * (k % 4)
                    last = pe.matmul(t[g:g + 32, :], sc_pad[:, k, :], w[:, k, :],
                                     start=(k < 4), stop=(k >= 4), tile_position=(0, g))
                fill((tag, c), last)

            def swap(tag, i, matrix, rawbuf):
                wait_freed(pe, (tag, i))
                t = claim(pe, (tag, "swap", i))
                fill((tag, "swap", i), pe.matmul(t, const(matrix), rawbuf[:, i % 2, :], start=True, stop=True))

            def roped(tag, cname, i0, n, matrix, rawbuf, first=None):
                for i in range(i0, i0 + n):
                    feature_tiles(cname, [(tag, i)], h_parts, c0=(i - i0) * P)
                    if i > i0 or first is not None:
                        if i > i0:
                            swap(tag, i - 1, matrix, rawbuf)
                        else:
                            first()

            def merge(tag):
                ready = 0 if tag == "m1" else FG + KT
                for i, (kind, part, nq) in enumerate(MERGE):
                    name = (tag, kind, part, nq)
                    tiles = [(*name, n) for n in range(4)]
                    if kind == "gate":
                        feature_tiles(name, tiles, h_parts)
                    else:
                        p = "ab".index(part)
                        high, low = (h_high, h_low)[p], branch_lows[tag][p]
                        x = (lambda k, a, b, v=high: v[:, k, a:b], lambda k, a, b, v=low: v[:, k, a:b])
                        kt = branches[tag][p][1]
                        if nq == 0:
                            first_tiles(name, tiles, x, "branch_low", ready, kt)
                            ready += kt
                        else:
                            feature_tiles(name, tiles, x, kt=kt)
                    if tag == "m1":
                        mod_step("mod1", 4 + i, 4)
                if tag == "m1":
                    mod_turn("mod1", 11)

            def out_proj(tag, mtag, m, norm_tag):
                low = merged_low[mtag]
                x = (h_parts[0], lambda k, a, b: low[:, k, a:b])
                first_tiles((tag, 0), [(tag, n) for n in range(4)], x, "merged_low", 0 if mtag == "m1" else KT)
                if tag == "out1":
                    pe.wait_ge(S["silu_ready"], 4)
                    mod_step("mod2", 0, 0)
                for n in range(4, KT):
                    feature_tiles((tag, 1), [(tag, n)], x, c0=n % 4 * P)
                    for k in {4: (0, 1, 2), 5: (3,), 6: (4,), 7: (5,)}[n]:
                        norm_step(m, norm_tag, L, k)

            pe.wait_ge(S["consts_in"], 16)
            pe.wait_ge(S["vecs_in"], 16 * 18)
            turn("vecs", [(i * P, rows_v[0:r, i, :]) for i, r in enumerate((104, 88, 88, 104))])
            w = slot(landed(pe, "x"), TT)
            for k in range(KT):
                turn(("xT", k), [(t * P, w[:, t, k * P:(k + 1) * P]) for t in range(TT)])
            w = slot(landed(pe, "ctx"), TT)
            for k in range(KT // 2):
                turn(("cT", k), [(j * LC + t * P, w[:, t, (2 * k + j) * P:(2 * k + j + 1) * P])
                                 for j in range(2) for t in range(CT)])
            pe.wait_ge(S["ones_ready"], 4)
            pe.wait_ge(S["silu_ready"], 2)
            mod_step("mod1", 0, 0)
            norm(0, "n1", L, lambda: mod_step("mod1", 1, 0))
            norm(1, "nc", LC, lambda: mod_step("mod1", 2, 0))
            mod_step("mod1", 3, 0)
            mod_turn("mod1", 3)
            first_tiles(("in1", 0), [("qk1", i) for i in range(4)], h_parts, "h_ready", 0)
            for i in range(4):
                swap("qk1", i, "swap1", raw)
            pe.wait_ge(S["h_ready"], 16)
            token_tiles(("in1", 1), [("kc", t) for t in range(CT)], hc_parts)
            roped("qk1", ("in1", 1), 4, 4, "swap1", raw)
            swap("qk1", 7, "swap1", raw)
            for hh in range(2):
                token_tiles(("in1", 2 + hh), [("vc", hh, t) for t in range(CT)], hc_parts)
                token_tiles(("in1", 2 + hh), [("v", hh, t) for t in range(TT)], h_parts)
            pe.wait_ge(S["kw_ready"], 4)
            wait_freed(pe, ("vc", 1, CT - 1))
            t = claim(pe, "S").rearrange("p (d j e) -> p d j e", d=2, j=4)
            for d in range(2):
                for h in range(H1):
                    o = 64 * (h % 2)
                    for tt in range(CT):
                        last = pe.matmul(t[o:o + 64, d, h // 2, :], kw[:, d, tt, h * DK:(h + 1) * DK],
                                         vc[:, tt, h * DV:(h + 1) * DV], start=(tt == 0), stop=(tt == CT - 1))
            fill("S", last)
            def scores(h):
                o = 64 * (h % 2)
                for i in range(TT):
                    t = claim(pe, ("s", h, i))
                    fill(("s", h, i), pe.matmul(t, obuf[o:o + 64, 3 + 2 * (h // 2), i * P:(i + 1) * P],
                                                obuf[o:o + 64, 2 + 2 * (h // 2), :], start=True, stop=True))

            def outputs(h):
                o = 64 * (h % 2)
                t = claim(pe, ("o", h))
                for i in range(TT):
                    wait_freed(pe, ("s", h, i))
                    pe.matmul(t, v1[:, i, h * DV:(h + 1) * DV], probs[:, i, :], start=(i == 0), stop=False)
                pe.wait_ge(S["qdec_ready"], 2 * (h // 2) + 2)
                for d in range(2):
                    last = pe.matmul(t, state[o:o + 64, d, h // 2, :], qdec[o:o + 64, d, :],
                                     start=False, stop=(d == 1))
                fill(("o", h), last)

            pe.wait_ge(S["q_ready"], 8)
            wait_freed(pe, ("v", 1, TT - 1))
            wait_freed(pe, "S")
            for h in range(H1 + 1):
                if h:
                    outputs(h - 1)
                if h < H1:
                    scores(h)
                if h:
                    wait_freed(pe, ("o", h - 1))
                    t = claim(pe, ("var", h - 1))
                    fill(("var", h - 1), pe.matmul(t, mean_ones[:, 1, :], osq, start=True, stop=True))
            for n in range(2):
                feature_tiles(("in1", 4 + n), [("g", 4 * n + i) for i in range(4)], h_parts)
            token_tiles(("in1", 6), [("f", t) for t in range(TT)], h_parts)
            wl = slots[landed(pe, "dft")][:, :].rearrange("p (m k n) -> p m k n", m=2, k=TT)
            for g in range(FG):
                for m in range(2):
                    t = claim(pe, ("fa", g, m))
                    wait_freed(pe, ("f", TT - 1))
                    for k in range(TT):
                        last = pe.matmul(t, f_tok[:, k, g * P:(g + 1) * P], wl[:, m, k, :],
                                         start=(k == 0), stop=(k == TT - 1))
                    fill(("fa", g, m), last)
            pe.wait_ge(S["dist_in"], 48)
            for g in range(FG):
                t = claim(pe, ("z", g))
                wait_freed(pe, ("fa", g, 1))
                pe.matmul(t, dftd[:, 0, :], fa[:, g, 0, :], start=True, stop=False)
                fill(("z", g), pe.matmul(t, dftd[:, 1, :], fa[:, g, 1, :], start=False, stop=True))
            merge("m1")
            out_proj("out1", "m1", 2, "n2")
            norm(2, "n2", L, k0=6)
            for j in range(UPN):
                if j == 0:
                    first_tiles(("up", 0), [("up", 0, n) for n in range(4)], h_parts, "h_ready", 2 * KT)
                else:
                    feature_tiles(("up", j), [("up", j, n) for n in range(4)], h_parts)
                mod_step("mod2", j + 1, 0)
            mod_turn("mod2", 11)
            for n in range(KT):
                claim(pe, ("down", n))
            for j in range(6):
                kt = 4 if j < 5 else 2
                w = parts_of(("down", j), kt)
                for n in range(KT):
                    t = tile(("down", n))
                    for k in range(kt):
                        if n == 0:
                            pe.wait_ge(S["act_low"], 4 * j + k + 1)
                        last = product(t, w, (lambda k, a, b: act_high(k)[:, a:b],
                                                                     lambda k, a, b: act_low_v[:, k, a:b]),
                                       4 * j + k, FT, (n * P, n * P + P), (0, L), True, kw=k)
                    if j == 5:
                        fill(("down", n), last)
                        if n >= 2:
                            norm_step(3, "nf1", L, n - 2)
                if j < 5:
                    last.then_inc(S["chunk_free"], 1)
            def context():
                w = slot(chunk_at["down", 5] % RAW, 4)
                for k in range(KT // 2):
                    turn(("cT2", k), [(j * LC + t * P, w[:, 2 + t, (2 * k + j) * P:(2 * k + j + 1) * P])
                                      for j in range(2) for t in range(CT)])

            norm(3, "nf1", L, context, 6)
            norm(4, "n3", L)
            first_tiles(("in2", 0), [("u", i) for i in range(4)], h_parts, "h_ready", 3 * KT)
            norm(5, "nc2", LC, lambda: feature_tiles(("in2", 1), [("u", 4)], h_parts))
            for i in range(1, 4):
                feature_tiles(("in2", 1), [("u", 4 + i)], h_parts, c0=i * P)
            for hh in range(2):
                token_tiles(("in2", 2 + hh), [("va", hh, t) for t in range(TT)], h_parts)
            pe.wait_ge(S["stage2_in"], 16 * 4)
            for i in range(2):
                turn(("ws", i), [(j * P, ws_raw[:, 4 * i + j, :]) for j in range(4)])
            wait_freed(pe, ("ws", 1))
            for cc in range(TT):
                pe.wait_ge(S["ln_ready"], cc + 1)
                for g in range(NG):
                    t = claim(pe, ("mix", g)) if cc == 0 else tile(("mix", g))
                    last = pe.matmul(t[:, cc * P:(cc + 1) * P], va[:, cc, g * P:(g + 1) * P], ws_t[:, g, :],
                                     start=True, stop=True)
                    if cc == TT - 1:
                        fill(("mix", g), last)
            roped("q2", ("in2", 4), 0, 4, "swap2", raw2)
            roped("q2", ("in2", 5), 4, 4, "swap2", raw2, first=lambda: swap("q2", 3, "swap2", raw2))
            swap("q2", 7, "swap2", raw2)
            roped("k2", ("in2", 6), 0, 2, "swap2", raw2)
            swap("k2", 1, "swap2", raw2)
            token_tiles(("in2", 6), [("vb", t) for t in range(TT)], h_parts, c0=256, width=256)
            pe.wait_ge(S["h_ready"], 5 * KT)
            feature_tiles(("in2", 6), [("kc2", i) for i in range(2)], hc2_parts, width=LC)
            token_tiles(("in2", 6), [("vc2", t) for t in range(CT)], hc2_parts, c0=256, width=256)
            def item(i):
                kv, n, r = i // 16, (i // 4) % 4, i % 4
                return kv, n, r, max(n - 1, 0), min(n + 2, TT)

            def att_scores(i):
                kv, n, r, b0, b1 = item(i)
                h = 4 * kv + r
                o = 64 * (h % 2)
                t = claim(pe, ("as", i))
                lq = q2[o:o + 64, h // 2, n * P:(n + 1) * P]
                pe.matmul(t[:, 512 - (b1 - b0) * P:512], lq, kdup[o:o + 64, kv, b0 * P:b1 * P],
                          start=True, stop=True)
                fill(("as", i), pe.matmul(t[:, 512:512 + LC], lq, kcdup[o:o + 64, kv, :],
                                          start=True, stop=True))

            def att_turn(i):
                _, _, _, b0, b1 = item(i)
                pe.wait_ge(S["p_scaled"], i + 1)
                t = claim(pe, ("at", i))
                nb = b1 - b0 + CT
                o = (3 - (b1 - b0)) * P
                for b in range(nb):
                    last = pe.transpose(t[:, b * P:(b + 1) * P],
                                        prob2[:, i % NPB, o + b * P:o + (b + 1) * P], ident)
                fill(("at", i), last)

            def att_values(g):
                kv, n, _, b0, b1 = item(4 * g)
                wait_freed(pe, ("at", 4 * g + 3))
                t = claim(pe, ("pv", g))
                nb = b1 - b0 + CT
                for b in range(nb):
                    vals = (vb[:, b0 + b, :] if b < b1 - b0 else vcx[:, b - (b1 - b0), :])
                    for par in range(2):
                        last = pe.matmul(t[64 * par:64 * par + 64, 0:256].rearrange("p (a q) -> p a q", a=2),
                                         vals[:, kv * HD:(kv + 1) * HD], prob_ts[g % 2][:, b, par:4:2, :],
                                         start=(b == 0), stop=(b == nb - 1))
                fill(("pv", g), last)

            pe.wait_ge(S["kdup_ready"], 1)
            wait_freed(pe, ("kc2", 1))
            wait_freed(pe, ("vc2", CT - 1))
            for i in range(NH * TT + LAG):
                if i < NH * TT:
                    att_scores(i)
                if i >= LAG:
                    if (i - LAG) % 4 == 1 and i > LAG + 1:
                        att_values((i - LAG) // 4 - 1)
                    att_turn(i - LAG)
            att_values(NH * TT // 4 - 1)
            merge("m2")
            out_proj("out2", "m2", 6, "n4")
            norm(6, "n4", L, k0=6)
            pe.wait_ge(S["router_in"], 16)
            r = claim(pe, "routeT")
            for k in range(KT):
                g = 32 * (k % 4)
                pe.wait_ge(S["h4_ready"], k + 1)
                last = pe.matmul(r[g:g + 32, :], sc_pad[:, k, :], hT[:, k, :], start=(k < 4), stop=(k >= 4),
                                 tile_position=(0, g))
            fill("routeT", last)
            r = claim(pe, "router")
            wait_freed(pe, "routeT")
            for t in range(TT):
                last = pe.matmul(r[:, t * NE:(t + 1) * NE], rt_work[:, t * P:(t + 1) * P], const("routesel"),
                                 start=True, stop=True)
            fill("router", last)
            for t in range(TT):
                for hh in range(2):
                    turn(("ht", t, hh), [(k * P, hT[:, 4 * hh + k, t * P:(t + 1) * P]) for k in range(4)])
            pe.wait_ge(S["aff_ready"], 1)
            a = claim(pe, "affT")
            for t in range(TT):
                last = pe.transpose(a[0:NE, t * P:(t + 1) * P], aff[:, t, :], ident)
            fill("affT", last)
            pe.wait_ge(S["rank_ready"], 1)
            a = claim(pe, "slotT")
            for t in range(TT):
                last = pe.transpose(a[:, t * NE:(t + 1) * NE], rank[0:NE, t * P:(t + 1) * P], ident[0:NE, 0:NE])
            fill("slotT", last)
            pe.wait_ge(S["wsel_ready"], TT - 2)
            pe.wait_ge(S["wsel_half"], 2)
            for q in range(PAIRS):
                turn(("wt", q), [(t * P, wsel[:, t, q * P:(q + 1) * P]) for t in range(TT)])
            def landed_loop(it, m):
                loads = sum(len(chunks[n]) for n in range(m % SLOTS, NCH, RAW)) if m % SLOTS < RAW else 0
                pe.wait_ge(S[f"landed{m % SLOTS}"],
                           it * (16 * PAIR_CHUNKS // SLOTS) + 16 * (loads + m // SLOTS + 1))
                return slot(m, 8 if m < 4 * FQ else 4)

            def bank(b, n=1):
                return ps[:, b * 512:(b + n) * 512]

            wait_freed(pe, ("wt", PAIRS - 1))
            wait_freed(pe, ("wt", PAIRS - 2))
            pe.wait_ge(S["sel_ready"], TT)
            with pe.Fori(0, PAIRS) as it:
                pe.wait_ge(S["y_ready"], it * 2 + 1)
                for d in range(KT):
                    for t in range(TT):
                        last = pe.matmul(bank(6, 2)[:, d * P:(d + 1) * P], h2_tok[:, t, d * P:(d + 1) * P],
                                         sel[:, t, bass.ds(it * P, P)], start=(t == 0), stop=(t == TT - 1))
                    if d % 4 == 3:
                        last.then_inc(S["xe_full"], 1)
                pe.wait_ge(S["xe_ready"], it * 2 + 2)
                pe.wait_ge(S["x_added"], it * KT + 1)

                def turn_hidden(fq):
                    n = it * FQ + fq
                    pe.wait_ge(S["hm_ready"], n + 2)
                    pe.wait_ge(S["hmt_ready"], n + 1)
                    for j in range(4):
                        last = pe.transpose(bank(4)[:, j * P:(j + 1) * P],
                                            hmid[:, fq * 512 + j * P:fq * 512 + (j + 1) * P], ident)
                    last.then_inc(S["hmt_full"], 1)

                for fq in range(FQ):
                    if fq >= 2:
                        pe.wait_ge(S["hm_ready"], it * FQ + fq)
                    for gu in range(2):
                        m = 4 * fq + 2 * gu
                        wa, wb = landed_loop(it, m), landed_loop(it, m + 1)
                        b = bank(2 * (fq % 2) + gu)
                        for k in range(KT):
                            la = pe.matmul(b[0:64, :], xe[:, k, 0:64], wa[:, k, :],
                                           start=(k == 0), stop=(k == KT - 1))
                            lb = pe.matmul(b[64:128, :], xe[:, k, 64:128], wb[:, k, :],
                                           start=(k == 0), stop=(k == KT - 1))
                        la.then_inc(S["chunk_free"], 1)
                        lb.then_inc(S["chunk_free"], 1)
                    if fq:
                        turn_hidden(fq - 1)
                turn_hidden(FQ - 1)
                for kq in range(FQ):
                    pe.wait_ge(S["hmt_ready"], it * FQ + kq + 2)
                    m = 4 * FQ + 2 * kq
                    wa, wb = landed_loop(it, m), landed_loop(it, m + 1)
                    for k in range(4):
                        for hh in range(2):
                            la = pe.matmul(bank(6 + hh)[0:64, :], hmid_t[:, 4 * kq + k, 0:64],
                                           wa[:, k, hh * 512:(hh + 1) * 512],
                                           start=(kq == 0 and k == 0), stop=(kq == FQ - 1 and k == 3))
                            lb = pe.matmul(bank(6 + hh)[64:128, :], hmid_t[:, 4 * kq + k, 64:128],
                                           wb[:, k, hh * 512:(hh + 1) * 512],
                                           start=(kq == 0 and k == 0), stop=(kq == FQ - 1 and k == 3))
                    la.then_inc(S["chunk_free"], 1)
                    lb.then_inc(S["chunk_free"], 1)
                pe.wait_ge(S["y_ready"], it * 2 + 3)
                pe.wait_ge(S["hm_ready"], it * FQ + FQ + 1)
                for d in range(KT):
                    if d >= 4:
                        pe.wait_ge(S["x_added"], it * KT + 1 + d - 3)
                    pe.matmul(bank(d % 4), y_sb[:, d * P:(d + 1) * P], wsel_t[:, bass.ds(it, 1), :].rearrange(
                        "p a b -> p (a b)"), start=True, stop=True).then_inc(S["sc_full"], 1)
            for k in range(KT):
                norm_step(7, "nf2", L, k)
            pe.wait_ge(S["scaled"], 8 * KT)
            for t in range(TT):
                for hh in range(2):
                    turn(("ot", t, hh), [(k * P, hT[:, 4 * hh + k, t * P:(t + 1) * P]) for k in range(4)])

        @block.scalar
        def _(act_e):
            A = act_e.activation

            def copy_out(name, dst, func=ACT.Copy, width=512, **kw_):
                t = wait_full(act_e, name)[:, 0:width]
                free(name, "A", A(dst, t, func, **kw_))

            def norm_squares(m, tag, src, width, written=None, between=None):
                A(small[:, 4:5], eps_col, ACT.Sqrt)
                for k in range(KT):
                    if written:
                        written(k)
                    A(squares(m)[:, k, 0:width], src[:, k, 0:width], ACT.Square).then_inc(S["sq_ready"], 1)
                if m:
                    act_e.wait_ge(S["recip_ready"], m)
                if between:
                    between()
                n = width // P
                copy_out(tag, root[:, 0:n], ACT.Sqrt, width=n, bias=eps_col)

            def norm_affine(m, dst, width, a, shift, high=None, nth=None):
                for k in range(KT + 1):
                    if k < KT:
                        act_e.wait_ge(S["scaled"], KT * m + k + 1)
                        A(dst[:, k, 0:width], dst[:, k, 0:width], ACT.Identity, bias=shift(k), scale=a(k)).then_inc(
                            S["h4_ready"] if m == 6 else S["h_plain"], 1)
                    if k and high:
                        round_h(nth, k - 1, high, dst)

            def round_h(nth, k, high, src):
                act_e.wait_ge(S["h_plain"], KT * nth + k + 1)
                A(high(k, 0, src.shape[2]), src[:, k, :], ACT.Copy).then_inc(S["h_rounded"], 1)

            issued = [0]

            def prepare(name):
                for i in next_splits(issued, name):
                    sl = landed(act_e, order[split[i]])
                    if i >= 2:
                        wait_spent(act_e, split[i - 2])
                    n = split_words(i)
                    A(slots_r[high_slot(i)][:, 0:n], slots[sl][:, 0:n], ACT.Copy).then_inc(S["high_ready"], 1)

            def mod_silu(vi):
                for r in range(2):
                    A(sc_pad[:, :, r], cols[:, vi, 8 * r:8 * r + 8], ACT.Silu).then_inc(S["silu_ready"], 1)

            def mod_rows(tag, c, ahead=True):
                if ahead:
                    prepare((tag, c))
                if c >= 2:
                    wait_full(act_e, (tag, "T", c - 2))
                copy_out((tag, c), m_sb(tag, c))

            def rope_raw(tag, i, g, rawbuf, scale):
                if g >= 2:
                    act_e.wait_ge(S["rope_cos"], g - 1)
                    act_e.wait_ge(S["q_ready"], g - 1)
                copy_out((tag, i), rawbuf[:, i % 2, :], ACT.Copy, scale=scale)

            def branch_highs(tag, p):
                for k in range(branches[tag][p][1]):
                    A((h_high, h_low)[p][:, k, :], branch_views[tag][p][:, k, :], ACT.Copy).then_inc(
                        S["branch_high"], 1)

            def merge_gates(tag, vi):
                for i, (kind, part, nq) in enumerate(MERGE):
                    prepare((tag, kind, part, nq))
                    if kind == "gate":
                        first = 8 if (tag == "m1") == (part == "a") else 0
                        for n in range(4):
                            col = V1["b_gate"] + first + 4 * nq + n
                            copy_out((tag, "gate", part, nq, n), merge_views[tag]["ab".index(part)][:, 4 * nq + n, :],
                                     ACT.Sigmoid, bias=cols[:, vi, col:col + 1])
                    if i == 3:
                        if tag == "m1":
                            wait_freed(act_e, ("z", FG - 1))
                        else:
                            act_e.wait_ge(S["ya_ready"], NG)
                        branch_highs(tag, 0)
                    if i == 4:
                        if tag == "m1":
                            act_e.wait_ge(S["g_ready"], KT)
                        else:
                            wait_freed(act_e, ("pv", NH * TT // 4 - 1))
                        branch_highs(tag, 1)
                    if i == 7:
                        wait_full(act_e, (tag, "proj", "a", 1, 3))
                        for k in range(KT):
                            act_e.wait_ge(S["merged_ready"], (0 if tag == "m1" else KT) + k + 1)
                            A(h_high[:, k, :], merge_views[tag][0][:, k, :], ACT.Copy).then_inc(S["merged_high"], 1)
                    if tag == "m1":
                        mod_rows("mod1", 4 + i)

            act_e.wait_ge(S["ones_ready"], 4)
            wait_freed(act_e, "vecs")
            mod_silu(0)
            for k in range(0, KT, 2):
                copy_out(("xT", k), xT[:, k, :])
            for k in range(0, KT // 2, 2):
                copy_out(("cT", k), hc[:, 2 * k:2 * k + 2, :].rearrange("p a b -> p (a b)"))
            for n in (("xT", 6), ("xT", 7), ("cT", 2), ("cT", 3)):
                wait_freed(act_e, n)
            norm_squares(0, "n1", xT, L, between=lambda: mod_rows("mod1", 0, ahead=False))
            mod_rows("mod1", 1, ahead=False)
            norm_squares(1, "nc", hc, LC)
            mod_rows("mod1", 2, ahead=False)
            prepare(("mod1", 2))
            mod_rows("mod1", 3, ahead=False)
            act_e.wait_ge(S["mods_ready"], 1)
            norm_affine(0, hT, L, lambda k: scale_a[:, 0, k:k + 1], lambda k: mod_cols[:, k, 0:1],
                        h_parts[0], 0)
            norm_affine(1, hc, LC, lambda k: scale_a[:, 1, k:k + 1], lambda k: mod_cols[:, k, 1:2],
                        hc_parts[0], 1)
            act_e.wait_ge(S["bcast_in"], 48)
            A(ea, decay, ACT.Exp).then_inc(S["decay_exp"], 1)
            act_e.wait_ge(S["decay_ready"], 1)
            for d in range(2):
                for t in range(CT):
                    c0 = CONST["age"][0] + 2 * d + t
                    A(ctxw[:, d, t, :], lg[:, 8 * d:8 * d + 8], ACT.Exp, scale=cst[:, c0:c0 + 1]).then_inc(
                        S["decay_exp"], 1)
            prepare(("in1", 0))
            for i in range(4):
                rope_raw("qk1", i, i, raw, DK ** -0.5)
            prepare(("in1", 1))
            for t in range(CT):
                copy_out(("kc", t), kc[:, t, :])
            for i in range(4, 8):
                rope_raw("qk1", i, i, raw, 1.0)
            for i in range(2, 4):
                prepare(("in1", i))
            def decayed_queries(j):
                if j:
                    wait_full(act_e, ("o", 2 * j - 1))
                    act_e.wait_ge(S["qdec_ready"], 2 * j)
                A(qdec[:, 0, :], tpos, ACT.Exp, scale=qcol[:, 0, j:j + 1]).then_inc(S["table_in"], 1)
                A(qdec[:, 1, :], tpos, ACT.Exp, scale=qcol[:, 1, j:j + 1],
                  bias=qcol[:, 2, j:j + 1]).then_inc(S["table_in"], 1)

            def decay_table(h):
                if h >= 2:
                    wait_freed(act_e, ("s", h - 2, TT - 1))
                tb, c0, c1 = table[:, h % 2, :], (TT - 1) * P, TT * P
                A(tb[:, 0:c0], dist_sb[:, 0:c0], ACT.Exp, scale=ea[:, 8 + h:9 + h])
                A(tb[:, c1:], dist_sb[:, c1:], ACT.Exp, scale=lg[:, h:h + 1])
                act_e.wait_ge(S["table_arg"], h + 1)
                A(tb[:, c0:c1], tb[:, c0:c1], ACT.Exp).then_inc(S["table_exp"], 1)

            act_e.wait_ge(S["dist_in"], 32)
            act_e.wait_ge(S["decay_ready"], 2)
            wait_freed(act_e, "S")
            decay_table(0)
            decayed_queries(0)
            decay_table(1)
            for h in range(H1):
                t = wait_full(act_e, ("o", h))
                if h:
                    wait_full(act_e, ("var", h - 1))
                A(osq, t, ACT.Square)
                free(("o", h), "A", A(obuf[:, h, :], t, ACT.Copy))
                if h % 2 and h + 1 < H1:
                    decayed_queries(h // 2 + 1)
                if h + 2 < H1:
                    decay_table(h + 2)
                if h:
                    act_e.wait_ge(S["o_square"], h)
                copy_out(("var", h), rinv, ACT.Sqrt, bias=eps_col)
            wait_full(act_e, ("g", 0))
            for n in range(KT):
                if n % 4 == 0:
                    prepare(("in1", 4 + n // 4))
                copy_out(("g", n), at(10240 + 512 * n, L), ACT.Silu)
            prepare(("in1", 6))
            for t in range(TT):
                copy_out(("f", t), f_tok[:, t, :])
            prepare("dft")
            for g in range(FG):
                for m in range(2):
                    if g == 0 and m == 0:
                        act_e.wait_ge(S["g_ready"], 8)
                    copy_out(("fa", g, m), fa[:, g, m, :])
            merge_gates("m1", 0)
            wait_full(act_e, ("mod1", 11))
            mod_silu(3)
            prepare(("out1", 0))
            mod_rows("mod2", 0)
            prepare(("out1", 1))
            norm_squares(2, "n2", xT, L, lambda k: wait_freed(act_e, ("out1", k)))
            act_e.wait_ge(S["mods_ready"], 2)
            norm_affine(2, hT, L, lambda k: scale_a[:, 2, k:k + 1], lambda k: mod_cols[:, 24 + k, 0:1],
                        h_parts[0], 2)
            def round_act(k):
                act_e.wait_ge(S["act_ready"], k + 1 if k < FT - 2 else FT)
                A(act_high(k), act[:, k, :], ACT.Copy).then_inc(S["act_high"], 1)

            for j in range(UPN):
                prepare(("up", j))
                for n in range(4):
                    f = 2 * j + n % 2 + (FT if n >= 2 else 0)
                    t = wait_full(act_e, ("up", j, n))
                    if j:
                        act_e.wait_ge(S["act_ready"], 2 * (j - 1) + 1 + n % 2)
                    A(conv[:, n, :], t, ACT.Identity, bias=cols[:, 2, 44 + f:45 + f],
                      scale=cols[:, 1, 44 + f:45 + f]).then_inc(S["conv_mid"], 1)
                for n in range(2):
                    wait_freed(act_e, ("up", j, n))
                    A(gelu_a[:, n, :], conv[:, n, :], ACT.Gelu_apprx_tanh).then_inc(S["gelu_ready"], 1)
                mod_rows("mod2", j + 1)
                if j == UPN - 2:
                    for k in range(4):
                        round_act(k)
            wait_full(act_e, ("up", UPN - 1, 3))
            for j in range(6):
                for k in range(4 * j + 4, min(4 * j + 8, FT)):
                    round_act(k)
                prepare(("down", j))
            norm_squares(3, "nf1", xT, L, lambda k: wait_freed(act_e, ("down", k)))
            for k in range(0, KT // 2, 2):
                copy_out(("cT2", k), hc2[:, 2 * k:2 * k + 2, :].rearrange("p a b -> p (a b)"))
            norm_squares(4, "n3", xT, L, lambda k: act_e.wait_ge(S["scaled"], 3 * KT + k + 1))
            act_e.wait_ge(S["mods_ready"], 3)
            norm_affine(4, hT, L, lambda k: scale_a[:, 0, k:k + 1], lambda k: mod_cols2[:, k, 0:1],
                        h_parts[0], 3)
            for n in range(KT):
                if n % 4 == 0:
                    prepare(("in2", n // 4))
                if n == 4:
                    wait_freed(act_e, ("cT2", 2))
                    wait_freed(act_e, ("cT2", 3))
                    wait_full(act_e, "n3")
                    norm_squares(5, "nc2", hc2, LC)
                copy_out(("u", n), ug[:, n, :], ACT.Gelu_apprx_tanh)
            norm_affine(5, hc2, LC, lambda k: scale_a[:, 1, k:k + 1], lambda k: mod_cols2[:, k, 1:2])
            for hh in range(2):
                prepare(("in2", 2 + hh))
                for t in range(TT):
                    copy_out(("va", hh, t), va[:, t, hh * 512:(hh + 1) * 512], ACT.Gelu_apprx_tanh)
                    if hh:
                        act_e.wait_ge(S["ln_stats"], t + 1)
                        A(stats[:, t, 14:15], stats[:, t, 13:14], ACT.Sqrt, bias=eps_col).then_inc(S["ln_root"], 1)
            for i in range(2):
                copy_out(("ws", i), ws_t[:, 4 * i:4 * i + 4, :].rearrange("p a b -> p (a b)"))
            for i in range(8):
                if i % 4 == 0:
                    prepare(("in2", 4 + i // 4))
                rope_raw("q2", i, 8 + i, raw2, HD ** -0.5)
            wait_full(act_e, last_tile["in2", 5])
            for k in range(KT):
                round_h(4, k, hc2_parts[0], hc2)
            for i in range(2):
                rope_raw("k2", i, 16 + i, raw2, 1.0)
            act_e.wait_ge(S["q_ready"], 18)
            for t in range(TT):
                copy_out(("vb", t), vb[:, t, :], width=256)
            act_e.wait_ge(S["kdup_ready"], 1)
            for t in range(CT):
                copy_out(("vc2", t), vcx[:, t, :], width=256)

            def widths(i):
                n = (i // 4) % 4
                return (2 if n in (0, 3) else 3) * P

            def att_exp(i):
                h = 4 * (i // 16) + i % 4
                w = widths(i)
                act_e.wait_ge(S["row_max"], i + 1)
                t = tile(("as", i))
                if i >= NPB:
                    wait_full(act_e, ("at", i - NPB))
                if i >= 4:
                    act_e.wait_ge(S["p_scaled"], i - 3)
                free(("as", i), "A", A(prob2[:, i % NPB, 384 - w:640], t[:, 512 - w:768], ACT.Exp,
                                       bias=neg_m[:, i % 4:i % 4 + 1], accum_out=den[:, i % 4:i % 4 + 1]))
                A(sink_e[:, i % 4:i % 4 + 1], sink[:, h:h + 1], ACT.Exp,
                  bias=neg_m[:, i % 4:i % 4 + 1]).then_inc(S["sink_exp"], 1)

            def att_keep(i):
                nb = widths(i) // P + CT
                if i % 4 == 0 and i >= 8:
                    wait_full(act_e, ("pv", i // 4 - 2))
                t = wait_full(act_e, ("at", i))
                free(("at", i), "A", A(prob_ts[i // 4 % 2][:, 0:nb, i % 4, :],
                                       t[:, 0:nb * P].rearrange("p (b q) -> p b q", b=nb), ACT.Copy))

            def gate_high(q):
                if q == 0:
                    landed(act_e, order[split[gate_split]])
                    wait_spent(act_e, split[gate_split - 2])
                    wait_full(act_e, ("vc2", CT - 1))
                c = slice(q * SLOT // 4, (q + 1) * SLOT // 4)
                last = A(slots_r[high_slot(gate_split)][:, c], slots[split[gate_split] % RAW][:, c], ACT.Copy)
                if q == 3:
                    last.then_inc(S["high_ready"], 1)

            issued[0] = gate_split + 1
            for i in range(NH * TT + LAG):
                if 2 <= i < 6:
                    gate_high(i - 2)
                if i < NH * TT:
                    att_exp(i)
                if i >= LAG:
                    att_keep(i - LAG)
            wait_full(act_e, ("pv", NH * TT // 4 - 1))
            merge_gates("m2", 3)
            for nq in range(2):
                prepare(("out2", nq))
            norm_squares(6, "n4", xT, L, lambda k: wait_freed(act_e, ("out2", k)))
            norm_affine(6, hT, L, lambda k: scale_a[:, 2, k:k + 1], lambda k: mod_cols2[:, 24 + k, 0:1])
            copy_out("routeT", rt_work)
            act_e.wait_ge(S["row_max"], NH * TT + 1)
            A(aff[:, :, :], aff[:, :, :], ACT.Exp).then_inc(S["exp_done"], 1)
            for t in range(TT):
                copy_out(("ht", t, 0), h2_tok[:, t, 0:512])
            for q in range(0, PAIRS, 2):
                copy_out(("wt", q), wsel_t[:, q, :])
            act_e.sem_inc(S["y_ready"], 1)
            act_e.sem_inc(S["hmt_ready"], 1)
            with act_e.Fori(0, PAIRS) as it:
                for hh in range(2):
                    act_e.wait_ge(S["xe_full"], it * 2 + hh + 1)
                    A(xe[:, 4 * hh:4 * hh + 4, :].rearrange("p a b -> p (a b)"),
                      ps[:, (6 + hh) * 512:(7 + hh) * 512], ACT.Copy).then_inc(S["xe_ready"], 1)

                def keep_turned(fq):
                    act_e.wait_ge(S["hmt_full"], it * FQ + fq + 1)
                    A(hmid_t[:, 4 * fq:4 * fq + 4, :].rearrange("p a b -> p (a b)"), ps[:, 4 * 512:5 * 512],
                      ACT.Copy).then_inc(S["hmt_ready"], 1)

                for fq in range(FQ):
                    act_e.wait_ge(S["chunk_free"], it * PAIR_CHUNKS + LOOP_FREE + 4 * fq + 2)
                    if fq >= 2:
                        act_e.wait_ge(S["hm_ready"], it * FQ + fq)
                    A(sg[:, fq % 2, :], ps[:, 2 * (fq % 2) * 512:(2 * (fq % 2) + 1) * 512],
                      ACT.Silu).then_inc(S["silu_done"], 1)
                    if fq:
                        keep_turned(fq - 1)
                keep_turned(FQ - 1)
                act_e.wait_ge(S["chunk_free"], it * PAIR_CHUNKS + LOOP_FREE + PAIR_CHUNKS)
                for hh in range(2):
                    A(y_sb[:, hh * 512:(hh + 1) * 512], ps[:, (6 + hh) * 512:(7 + hh) * 512],
                      ACT.Copy).then_inc(S["y_ready"], 1)
            norm_squares(7, "nf2", xT, L, lambda k: act_e.wait_ge(S["x_added"], 2 + KT * (PAIRS - 1) + k))
            act_e.wait_ge(S["recip_ready"], len(norm_tags))
            for t in range(TT):
                copy_out(("ot", t, 0), out_sb[:, t, 0:512], scale=recip[:, t:t + 1])

        @block.vector
        def _(ve):
            chained = [0]

            def link(ins):
                chained[0] += 1
                ins.then_inc(S["dve_chain"], 1)
                ve.wait_ge(S["dve_chain"], chained[0])

            def wide(v, *shape):
                return v.broadcast_to(list(shape))

            issued = [0]

            def prepare(name):
                for i in next_splits(issued, name):
                    sl, n = split[i] % RAW, split_words(i)
                    ve.wait_ge(S["high_ready"], i + 1)
                    ve.tensor_tensor(slots_r[sl][:, 0:n], slots[sl][:, 0:n],
                                     slots_r[high_slot(i)][:, 0:n].bitcast(F32), ALU.subtract).then_inc(
                        S["low_ready"], 1)

            def low_h(nth, k, high, low, src):
                ve.wait_ge(S["h_rounded"], KT * nth + k + 1)
                ve.tensor_tensor(low(k, 0, src.shape[2]), src[:, k, :], high(k, 0, src.shape[2]).bitcast(F32),
                                 ALU.subtract).then_inc(S["h_ready"], 1)

            def mod_columns(tag, c):
                cc, vi = (mod_cols, 0) if tag == "mod1" else (mod_cols2, 3)
                t = wait_full(ve, (tag, "T", c))
                b = cols[:, vi, V1["b_mod"] + 4 * c:V1["b_mod"] + 4 * c + 4]
                free((tag, "T", c), "D", ve.tensor_tensor(
                    cc[:, 4 * c:4 * c + 4, :], t[:, 0:8].rearrange("p (a b) -> p a b", b=2),
                    wide(b.unsqueeze(2), P, 4, 2), ALU.add))

            def mod_scales(tag, which):
                cc, vi = (mod_cols, 0) if tag == "mod1" else (mod_cols2, 3)
                for i in which:
                    m, r, w = ((8, 0, "norm1"), (8, 1, "norm1"), (32, 0, "norm2"))[i]
                    wait_freed(ve, (tag, "T", m // 4 + 1))
                    last = ve.scalar_tensor_tensor(scale_a[:, i, :], cc[:, m:m + 8, r], 1.0,
                                                   cols[:, vi, V1[w]:V1[w] + 8], ALU.add, ALU.mult)
                last.then_inc(S["mods_ready"], 1)

            def norm_scale(m, tag, src, dst, width, weight=None, between=None, split_h=None):
                n = width // P
                wait_freed(ve, tag)
                if m:
                    wait_full(ve, (norm_tags[m - 1], "wide"))
                ve.reciprocal(recip[:, 0:n], root[:, 0:n]).then_inc(S["recip_ready"], 1)
                if between:
                    between()
                r = wait_full(ve, (tag, "wide"))[:, 0:width]
                for k in range(KT + 2):
                    if split_h and k >= 2:
                        low_h(split_h[0], k - 2, *split_h[1:], dst)
                    if k >= KT:
                        continue
                    if weight is None:
                        last = ve.tensor_tensor(dst[:, k, 0:width], src[:, k, 0:width], r, ALU.mult)
                    else:
                        last = ve.scalar_tensor_tensor(dst[:, k, 0:width], src[:, k, 0:width], weight(k),
                                                       r, ALU.mult, ALU.mult)
                    last.then_inc(S["scaled"], 1)
                ve.wait_ge(S["scaled"], KT * (m + 1))
                free((tag, "wide"), "D", None)

            def rope_sum(tag, i, g, cs, rsinbuf, rcosbuf, dst):
                t = wait_full(ve, (tag, "swap", i))
                if g == (0 if cs is rope_cs else 8):
                    ve.wait_ge(S["rope_in"], 16 if g == 0 else 32)
                free((tag, "swap", i), "D", ve.tensor_tensor(rsinbuf[:, i % 2, :], t, cs[:, 1, :], ALU.mult))
                wait_freed(ve, (tag, "swap", i))
                ve.wait_ge(S["rope_cos"], g + 1)
                ve.tensor_tensor(dst, rsinbuf[:, i % 2, :], rcosbuf[:, i % 2, :], ALU.add).then_inc(S["q_ready"], 1)

            def centred(name, dst):
                t = wait_full(ve, name).rearrange("p (h e) -> p h e", e=DV)
                link(ve.tensor_reduce(negmean[:, 0:4], t, AX.X, ALU.add))
                link(ve.tensor_scalar(negmean[:, 4:8], negmean[:, 0:4], -1.0 / DV, None, ALU.mult))
                free(name, "D", ve.tensor_tensor(dst.rearrange("p (h e) -> p h e", e=DV), t,
                                                 wide(negmean[:, 4:8].unsqueeze(2), P, 4, DV), ALU.add))

            def merged_rest(tag, k):
                ve.wait_ge(S["merged_high"], (0 if tag == "m1" else KT) + k + 1)
                ve.tensor_tensor(merged_low[tag][:, k, :], merge_views[tag][0][:, k, :],
                                 h_high[:, k, :].bitcast(F32), ALU.subtract).then_inc(S["merged_low"], 1)

            def branch_rest(tag, p):
                done = (0 if tag == "m1" else FG + KT) + (branches[tag][0][1] if p else 0)
                for k in range(branches[tag][p][1]):
                    ve.wait_ge(S["branch_high"], done + k + 1)
                    ve.tensor_tensor(branch_lows[tag][p][:, k, :], branch_views[tag][p][:, k, :],
                                     (h_high, h_low)[p][:, k, :].bitcast(F32), ALU.subtract).then_inc(
                                         S["branch_low"], 1)

            def merged_tiles(tag):
                for i, (kind, part, nq) in enumerate(MERGE):
                    p = "ab".index(part)
                    prepare((tag, kind, part, nq))
                    if i == 3:
                        branch_rest(tag, 0)
                    if i == 4:
                        branch_rest(tag, 1)
                    for n in range(4 if kind == "proj" else 0):
                        name = (tag, "proj", part, nq, n)
                        wait_freed(ve, (tag, "gate", part, nq, n))
                        t = wait_full(ve, name)
                        v = merge_views[tag][p][:, 4 * nq + n, :]
                        free(name, "D", ve.tensor_tensor(v, t, v, ALU.mult))
                    if i == 7:
                        for k in range(KT):
                            merged_rest(tag, k)
                    if tag == "m1":
                        prepare(("mod1", 4 + i))
                        if i:
                            mod_columns("mod1", 3 + i)
                if tag == "m1":
                    mod_columns("mod1", 11)
                    mod_scales("mod1", (2,))

            def residual(names, gate, cc, n0=0):
                for n, name in enumerate(names, n0):
                    t = wait_full(ve, name)
                    free(name, "D", ve.scalar_tensor_tensor(xT[:, n, :], t, cc[:, gate + n, 0:1], xT[:, n, :],
                                                            ALU.mult, ALU.add))

            def projected(tag, cc):
                prepare((tag, 0))
                residual([(tag, n) for n in range(4)], 16, cc)
                if tag == "out1":
                    prepare(("mod2", 0))
                residual([(tag, 4)], 16, cc, 4)
                prepare((tag, 1))
                residual([(tag, n) for n in range(5, KT)], 16, cc, 5)

            wait_full(ve, "vecs")
            for i, r in enumerate((104, 88, 88, 104)):
                last = ve.tensor_copy(cols[:, i, 0:r], tile("vecs")[:, i * P:i * P + r])
            free("vecs", "D", last)
            for k in range(1, KT, 2):
                free(("xT", k), "D", ve.tensor_copy(xT[:, k, :], wait_full(ve, ("xT", k))))
            for k in range(1, KT // 2, 2):
                free(("cT", k), "D", ve.tensor_copy(hc[:, 2 * k:2 * k + 2, :].rearrange("p a b -> p (a b)"),
                                                    wait_full(ve, ("cT", k))))
            norm_scale(0, "n1", xT, hT, L, between=lambda: mod_columns("mod1", 0))
            norm_scale(1, "nc", hc, hc, LC, between=lambda: mod_columns("mod1", 1))
            mod_columns("mod1", 2)
            prepare(("mod1", 2))
            mod_columns("mod1", 3)
            mod_scales("mod1", (0, 1))
            for k in range(KT):
                low_h(0, k, *h_parts, hT)
            for k in range(KT):
                low_h(1, k, *hc_parts, hc)
            ve.wait_ge(S["decay_exp"], 1)
            ve.tensor_scalar(lg, ea, -1.0, None, ALU.mult).then_inc(S["decay_ready"], 1)
            ve.wait_ge(S["decay_ready"], 1)
            for o in (0, 64):
                ve.tensor_copy(qcol[o:o + 64, 0, :], lg[o:o + 64, o // 64:8:2])
                last = ve.tensor_copy(qcol[o:o + 64, 1, :], ea[o:o + 64, 8 + o // 64:16:2])
            link(last)
            ve.tensor_scalar(qcol[:, 2, :], qcol[:, 1, :], -float(L + 1), None, ALU.mult).then_inc(
                S["decay_ready"], 1)
            prepare(("in1", 0))
            for i in range(4):
                rope_sum("qk1", i, i, rope_cs, rsin, rcos, obuf[:, 2 + 2 * i, :])
            prepare(("in1", 1))
            wait_freed(ve, ("kc", CT - 1))
            ve.wait_ge(S["decay_exp"], 5)
            for d in range(2):
                for t in range(CT):
                    ve.tensor_tensor(kw[:, d, t, :].rearrange("p (h e) -> p h e", e=DK),
                                     kc[:, t, :].rearrange("p (h e) -> p h e", e=DK),
                                     wide(ctxw[:, d, t, :].unsqueeze(2), P, H1, DK), ALU.mult).then_inc(
                                         S["kw_ready"], 1)
            for i in range(4):
                rope_sum("qk1", 4 + i, 4 + i, rope_cs, rsin, rcos, obuf[:, 3 + 2 * i, :])
            ve.wait_ge(S["q_ready"], 8)
            for hh in range(2):
                prepare(("in1", 2 + hh))
                for t in range(CT):
                    centred(("vc", hh, t), vc[:, t, hh * 512:(hh + 1) * 512])
                for t in range(TT):
                    centred(("v", hh, t), v1[:, t, hh * 512:(hh + 1) * 512])
            t = wait_full(ve, "S")
            free("S", "D", ve.tensor_copy(state[:, :, :, :].rearrange("p d j e -> p (d j e)"), t))
            def finish_head(h):
                wait_freed(ve, ("var", h))
                link(ve.reciprocal(rinv, rinv))
                ve.tensor_tensor(obuf[:, h, :], obuf[:, h, :], rinv, ALU.mult).then_inc(S["o_square"], 1)

            for h in range(H1):
                ve.wait_ge(S["table_ready"], h + 1)
                for i in range(TT):
                    t = wait_full(ve, ("s", h, i))
                    free(("s", h, i), "D", ve.tensor_tensor(
                        probs[:, i, :], t, table[:, h % 2, 384 - i * P:896 - i * P], ALU.mult))
                if h:
                    finish_head(h - 1)
            finish_head(H1 - 1)
            ve.wait_ge(S["o_square"], H1)
            for n in range(KT):
                if n % 4 == 0:
                    prepare(("in1", 4 + n // 4))
                wait_freed(ve, ("g", n))
                ve.tensor_tensor(obuf[:, n, :], at(10240 + 512 * n, L), obuf[:, n, :], ALU.mult).then_inc(
                    S["g_ready"], 1)
            prepare(("in1", 6))
            prepare("dft")
            for g in range(FG):
                free(("z", g), "D", ve.tensor_copy(z[:, g, :], wait_full(ve, ("z", g))))
            merged_tiles("m1")
            projected("out1", mod_cols)
            norm_scale(2, "n2", xT, hT, L, split_h=(2, *h_parts))
            def act_rest(k0):
                for k in range(k0, min(k0 + 4, FT)):
                    ve.wait_ge(S["act_high"], k + 1)
                    ve.tensor_tensor(act_low_v[:, k, :], act[:, k, :], act_high(k).bitcast(F32),
                                     ALU.subtract).then_inc(S["act_low"], 1)

            for j in range(UPN):
                prepare(("up", j))
                for n in range(4):
                    f = 2 * j + n % 2 + (FT if n >= 2 else 0)
                    ve.wait_ge(S["conv_mid"], 4 * j + n + 1)
                    t = wait_full(ve, ("up", j, n))
                    link(ve.scalar_tensor_tensor(conv[:, n, 1:L], t[:, 0:L - 1], cols[:, 1, f:f + 1],
                                                 conv[:, n, 1:L], ALU.mult, ALU.add))
                    free(("up", j, n), "D", ve.scalar_tensor_tensor(
                        conv[:, n, 0:L - 1], t[:, 1:L], cols[:, 2, f:f + 1], conv[:, n, 0:L - 1],
                        ALU.mult, ALU.add))
                wait_freed(ve, ("up", j, 3))
                for n in range(2):
                    ve.wait_ge(S["gelu_ready"], 2 * j + n + 1)
                    ve.tensor_tensor(act[:, 2 * j + n, :], gelu_a[:, n, :], conv[:, 2 + n, :],
                                     ALU.mult).then_inc(S["act_ready"], 1)
                prepare(("mod2", j + 1))
                mod_columns("mod2", j)
            act_rest(0)
            mod_columns("mod2", 11)
            mod_scales("mod2", (0, 1, 2))
            for j in range(6):
                act_rest(4 * j + 4)
                if j < 5:
                    prepare(("down", j))
            residual([("down", 0)], 40, mod_cols)
            prepare(("down", 5))
            residual([("down", n) for n in range(1, KT)], 40, mod_cols, 1)

            def context():
                for k in range(1, KT // 2, 2):
                    free(("cT2", k), "D", ve.tensor_copy(hc2[:, 2 * k:2 * k + 2, :].rearrange("p a b -> p (a b)"),
                                                         wait_full(ve, ("cT2", k))))

            norm_scale(3, "nf1", xT, xT, L, lambda k: cols[:, 0, V1["final"] + k:V1["final"] + k + 1], context)
            ve.wait_ge(S["scaled"], 4 * KT)
            norm_scale(4, "n3", xT, hT, L, split_h=(3, *h_parts))
            prepare(("in2", 0))
            norm_scale(5, "nc2", hc2, hc2, LC)
            for i in range(4):
                prepare(("in2", i))
            ve.wait_ge(S["stage2_in"], 16 * 4)
            for t in range(TT):
                for hh in range(2):
                    wait_freed(ve, ("va", hh, t))
                    last = ve.bn_stats(stats[:, t, 6 * hh:6 * hh + 6], va[:, t, hh * 512:(hh + 1) * 512])
                link(last)
                ve.bn_aggr(stats[:, t, 12:14], stats[:, t, 0:12]).then_inc(S["ln_stats"], 1)
                ve.wait_ge(S["ln_stats"], t + 1)
                link(ve.tensor_scalar(stats[:, t, 15:16], stats[:, t, 12:13], -1.0, None, ALU.mult))
                link(ve.scalar_tensor_tensor(va[:, t, :], va[:, t, :], stats[:, t, 15:16], ln_rows[:, 0, :],
                                             ALU.add, ALU.mult))
                ve.wait_ge(S["ln_root"], t + 1)
                link(ve.reciprocal(stats[:, t, 14:15], stats[:, t, 14:15]))
                ve.scalar_tensor_tensor(va[:, t, :], va[:, t, :], stats[:, t, 14:15], ln_rows[:, 1, :],
                                        ALU.mult, ALU.add).then_inc(S["ln_ready"], 1)
            for g in range(NG):
                t = wait_full(ve, ("mix", g)).rearrange("p (c q) -> p c q", q=P)
                if g >= 2:
                    ve.wait_ge(S["ya_ready"], g - 1)
                free(("mix", g), "D", ve.tensor_tensor(
                    mixed[:, g % 2, :].rearrange("p (c q) -> p c q", q=P), t,
                    wide(bs_rows[:, g, :].unsqueeze(1), P, TT, P), ALU.add))
            ve.wait_ge(S["ya_ready"], NG)
            for i in range(8):
                if i % 4 == 0:
                    prepare(("in2", 4 + i // 4))
                rope_sum("q2", i, 8 + i, rope_cs2, rsin2, rcos2, q2[:, i, :])
            for k in range(KT):
                low_h(4, k, *hc2_parts, hc2)
            for i in range(2):
                rope_sum("k2", i, 16 + i, rope_cs2, rsin2, rcos2, krot[:, i, :])
            ve.wait_ge(S["q_ready"], 18)
            for kv in range(NKV):
                for o in (0, 64):
                    last = ve.tensor_copy(kdup[o:o + 64, kv, :],
                                          krot[64 * (kv % 2):64 * (kv % 2) + 64, kv // 2, :])
            last.then_inc(S["kdup_ready"], 1)
            for i in range(2):
                t = wait_full(ve, ("kc2", i))
                for kv in (2 * i, 2 * i + 1):
                    for o in (0, 64):
                        last = ve.tensor_copy(kcdup[o:o + 64, kv, :],
                                              t[64 * (kv % 2):64 * (kv % 2) + 64, 0:LC])
                free(("kc2", i), "D", last)
            mask_rows = const("mask").rearrange("p (m s) -> p m s", m=2)

            def att_max(i):
                n, h = (i // 4) % 4, 4 * (i // 16) + i % 4
                w = (2 if n in (0, 3) else 3) * P
                t = wait_full(ve, ("as", i))
                if n == 0:
                    v, m = t[:, 384:512], mask_rows[:, 1, :]
                elif n == 3:
                    v, m = t[:, 256:384], mask_rows[:, 0, :]
                else:
                    v, m = t[:, 128:512].rearrange("p (b s) -> p b s", s=P)[:, 0:3:2, :], mask_rows
                link(ve.tensor_tensor(v, v, m, ALU.add))
                link(ve.tensor_reduce(row_top[:, 0:1], t[:, 512 - w:768], AX.X, ALU.max))
                if i >= 4:
                    ve.wait_ge(S["sink_exp"], i - 3)
                ve.tensor_scalar(neg_m[:, i % 4:i % 4 + 1], row_top[:, 0:1], sink[:, h:h + 1], -1.0,
                                 ALU.max, ALU.mult).then_inc(S["row_max"], 1)

            def att_scale(i):
                n = (i // 4) % 4
                w = (2 if n in (0, 3) else 3) * P
                c0 = i % 4
                ve.wait_ge(S["sink_exp"], i + 1)
                link(ve.tensor_tensor(row_top[:, 1:2], den[:, c0:c0 + 1], sink_e[:, c0:c0 + 1], ALU.add))
                link(ve.reciprocal(row_top[:, 2:3], row_top[:, 1:2]))
                p = prob2[:, i % NPB, 384 - w:640]
                ve.tensor_scalar(p, p, row_top[:, 2:3], None, ALU.mult).then_inc(S["p_scaled"], 1)

            def att_out(g):
                kv, n = g // 4, g % 4
                t = wait_full(ve, ("pv", g))
                free(("pv", g), "D", ve.tensor_copy(q2[:, 2 * kv:2 * kv + 2, n * P:(n + 1) * P],
                                                    t[:, 0:256].rearrange("p (a q) -> p a q", a=2)))

            def gate_low(q):
                sl = split[gate_split] % RAW
                ve.wait_ge(S["high_ready"], gate_split + 1)
                c = slice(q * SLOT // 4, (q + 1) * SLOT // 4)
                last = ve.tensor_tensor(slots_r[sl][:, c], slots[sl][:, c],
                                        slots_r[high_slot(gate_split)][:, c].bitcast(F32), ALU.subtract)
                if q == 3:
                    last.then_inc(S["low_ready"], 1)

            issued[0] = gate_split + 1
            for i in range(NH * TT + LAG):
                if 7 <= i < 11:
                    gate_low(i - 7)
                if i < NH * TT:
                    att_max(i)
                if 0 < i <= NH * TT:
                    att_scale(i - 1)
                if (i - LAG) % 4 == 2 and i > LAG + 2:
                    att_out((i - LAG) // 4 - 1)
            att_out(NH * TT // 4 - 1)
            merged_tiles("m2")
            projected("out2", mod_cols2)
            norm_scale(6, "n4", xT, hT, L)
            r = wait_full(ve, "router")[:, 0:TT * NE].rearrange("p (t e) -> p t e", e=NE)
            top = rt_small[:, 0:TT]
            link(ve.tensor_reduce(top, r, AX.X, ALU.max))
            free("router", "D", ve.tensor_tensor(aff, r, wide(top.unsqueeze(2), P, TT, NE), ALU.subtract))
            wait_freed(ve, "router")
            ve.sem_inc(S["row_max"], 1)
            for t in range(TT):
                free(("ht", t, 1), "D", ve.tensor_copy(h2_tok[:, t, 512:1024], wait_full(ve, ("ht", t, 1))))
            ve.wait_ge(S["exp_done"], 1)
            link(ve.tensor_reduce(rt_small[:, 4:8], aff, AX.X, ALU.add))
            link(ve.reciprocal(rt_small[:, 4:8], rt_small[:, 4:8]))
            ve.tensor_tensor(aff, aff, wide(rt_small[:, 4:8].unsqueeze(2), P, TT, NE), ALU.mult).then_inc(
                S["aff_ready"], 1)
            free("affT", "D", ve.tensor_copy(aff_t[0:NE, :], wait_full(ve, "affT")[0:NE, :]))
            wait_freed(ve, "affT")
            src = aff_t[0:NE, :]
            for i in range(CAP // 8):
                link(ve.max(top8[0:NE, :], src))
                link(ve.match_replace(out=rt_work[0:NE, :], in_to_replace=top8[0:NE, :], in_values=src,
                                      imm_value=-1.0))
                src = rt_work[0:NE, :]
            link(ve.tensor_tensor(chosen[0:NE, :], rt_work[0:NE, :], aff_t[0:NE, :], ALU.not_equal))
            link(ve.tensor_tensor_scan(rank[0:NE, :], chosen[0:NE, :], chosen[0:NE, :], 0.0, ALU.add, ALU.bypass))
            link(ve.tensor_tensor(rank[0:NE, :], rank[0:NE, :], chosen[0:NE, :], ALU.mult))
            ve.tensor_scalar(rank[0:NE, :], rank[0:NE, :], -1.0, None, ALU.add).then_inc(S["rank_ready"], 1)
            free("slotT", "D", ve.tensor_copy(slot_of[:, :, :].rearrange("p a b -> p (a b)"),
                                              wait_full(ve, "slotT")[:, 0:TT * NE]))
            wait_freed(ve, "slotT")
            for t in range(TT):
                s3 = sel[:, t, :].rearrange("p (e j) -> p e j", e=NE)
                ve.tensor_tensor(s3, wide(const("iota").unsqueeze(1), P, NE, CAP),
                                 wide(slot_of[:, t, :].unsqueeze(2), P, NE, CAP), ALU.is_equal).then_inc(
                                     S["sel_ready"], 1)
            ve.wait_ge(S["sel_ready"], TT)
            for t in range(2, TT):
                ve.tensor_tensor(wsel[:, t, :].rearrange("p (e j) -> p e j", e=NE),
                                 sel[:, t, :].rearrange("p (e j) -> p e j", e=NE),
                                 wide(aff[:, t, :].unsqueeze(2), P, NE, CAP), ALU.mult).then_inc(
                                     S["wsel_ready"], 1)
            for q in range(1, PAIRS, 2):
                free(("wt", q), "D", ve.tensor_copy(wsel_t[:, q, :], wait_full(ve, ("wt", q))))
            ve.sem_inc(S["hm_ready"], 1)
            ve.sem_inc(S["x_added"], 1)
            with ve.Fori(0, PAIRS) as it:
                for fq in range(FQ):
                    ve.wait_ge(S["chunk_free"], it * PAIR_CHUNKS + LOOP_FREE + 4 * fq + 4)
                    ve.wait_ge(S["silu_done"], it * FQ + fq + 1)
                    b = 2 * (fq % 2) + 1
                    ve.tensor_tensor(hmid[:, fq * 512:(fq + 1) * 512], sg[:, fq % 2, :],
                                     ps[:, b * 512:(b + 1) * 512], ALU.mult).then_inc(S["hm_ready"], 1)
                for d in range(KT):
                    ve.wait_ge(S["sc_full"], it * KT + d + 1)
                    b = d % 4
                    ve.scalar_tensor_tensor(xT[:, d, :], ps[:, b * 512:(b + 1) * 512],
                                            mod_cols2[:, 40 + d, 0:1], xT[:, d, :],
                                            ALU.mult, ALU.add).then_inc(S["x_added"], 1)
            ve.wait_ge(S["hm_ready"], 1 + FQ * PAIRS)
            for k in range(KT):
                w = cols[:, 3, V1["final"] + k:V1["final"] + k + 1]
                ve.wait_ge(S["x_added"], 2 + KT * (PAIRS - 1) + k)
                ve.tensor_scalar(hT[:, k, :], xT[:, k, :], w, None, ALU.mult).then_inc(S["scaled"], 1)
            wait_freed(ve, "nf2")
            wait_full(ve, ("n4", "wide"))
            ve.reciprocal(recip[:, 0:TT], root[:, 0:TT]).then_inc(S["recip_ready"], 1)
            ve.wait_ge(S["recip_ready"], len(norm_tags))
            for t in range(TT):
                free(("ot", t, 1), "D", ve.tensor_scalar(out_sb[:, t, 512:1024], wait_full(ve, ("ot", t, 1)),
                                                         recip[:, t:t + 1], None, ALU.mult))

        @block.gpsimd
        def _(po):
            po.memset(mean_ones[:, 0, :], 1.0 / D).then_inc(S["ones_ready"], 1)
            po.memset(mean_ones[:, 1, :], 1.0 / DV).then_inc(S["ones_ready"], 1)
            po.memset(eps_col, EPS).then_inc(S["ones_ready"], 1)
            po.memset(sc_pad[:, :, :], 0.0).then_inc(S["ones_ready"], 1)

            def rope_cosines(tag, i, g, cs, rawbuf, rcosbuf):
                wait_freed(po, (tag, i))
                if g >= 2:
                    po.wait_ge(S["q_ready"], g - 1)
                po.tensor_tensor(rcosbuf[:, i % 2, :], rawbuf[:, i % 2, :], cs[:, 0, :], ALU.mult).then_inc(
                    S["rope_cos"], 1)

            wait_full(po, ("mod1", "T", 3))
            po.dma_start(rope_cs[:, :, :], rope1).then_inc(S["rope_in"], 16)
            po.wait_ge(S["rope_in"], 16)
            for i in range(8):
                rope_cosines("qk1", i, i, rope_cs, raw, rcos)
            wait_full(po, "S")
            po.dma_start(dist_sb, dist[:, 0:896]).then_inc(S["dist_in"], 16)
            po.dma_start(tpos, dist[:, 896:896 + L]).then_inc(S["dist_in"], 16)
            po.wait_ge(S["dist_in"], 32)
            po.wait_ge(S["decay_ready"], 2)

            def table_argument(h):
                if h >= 2:
                    wait_freed(po, ("s", h - 2, TT - 1))
                c0, c1 = (TT - 1) * P, TT * P
                tb, d = table[:, h % 2, c0:c1], dist_sb[:, c0:c1]
                po.tensor_scalar(tb, d, 0.0, ea[:, 8 + h:9 + h], ALU.min, ALU.mult).then_inc(S["pool_chain"], 1)
                if h:
                    po.wait_ge(S["table_arg"], h)
                po.tensor_scalar(band, d, 0.0, lg[:, h:h + 1], ALU.max, ALU.mult).then_inc(S["pool_chain"], 1)
                po.wait_ge(S["pool_chain"], 2 * h + 2)
                po.tensor_tensor(tb, tb, band, ALU.add).then_inc(S["table_arg"], 1)

            def table_diagonal(h):
                po.wait_ge(S["table_exp"], h + 1)
                tb = table[:, h % 2, 384:512]
                po.tensor_tensor(tb, tb, ident, ALU.add).then_inc(S["table_ready"], 1)

            def decay_queries(j):
                for d in range(2):
                    po.wait_ge(S["table_in"], 2 * j + d + 1)
                    po.tensor_tensor(qdec[:, d, :], qdec[:, d, :], obuf[:, 2 + 2 * j, :], ALU.mult).then_inc(
                        S["qdec_ready"], 1)

            table_argument(0)
            table_argument(1)
            table_diagonal(0)
            decay_queries(0)
            table_diagonal(1)
            for h in range(H1):
                if h + 2 < H1:
                    table_argument(h + 2)
                if h % 2 and h + 1 < H1:
                    decay_queries(h // 2 + 1)
                if h + 2 < H1:
                    table_diagonal(h + 2)
            po.wait_ge(S["g_ready"], KT)
            po.dma_start(dftd[:, :, :], dft_dim).then_inc(S["dist_in"], 16)

            def add_parts(tag):
                a, b = merge_views[tag]
                for nq in range(2):
                    for n in range(4):
                        wait_freed(po, (tag, "proj", "b", nq, n))
                        k = 4 * nq + n
                        po.tensor_tensor(a[:, k, :], a[:, k, :], b[:, k, :], ALU.add).then_inc(S["merged_ready"], 1)

            add_parts("m1")
            wait_full(po, ("mod2", 11))
            po.dma_start(sc_pad[:, :, 0:NE], w_router_2[0].rearrange("(k p) e -> p k e", p=P)).then_inc(
                S["router_in"], 16)
            wait_full(po, ("down", KT - 1))
            po.dma_start(ln_rows[:, 0, :], gmlp_ln_g_2[0].partition_broadcast(P)).then_inc(S["stage2_in"], 16)
            po.dma_start(ln_rows[:, 1, :], gmlp_ln_b_2[0].partition_broadcast(P)).then_inc(S["stage2_in"], 16)
            po.dma_start(bs_rows[:, :, :], b_spatial_2[0].partition_broadcast(P)).then_inc(S["stage2_in"], 16)
            po.dma_start(ws_raw[:, :, :], w_spatial_2[0].rearrange("g p q -> p g q")).then_inc(
                S["stage2_in"], 16)
            for g in range(NG):
                wait_freed(po, ("mix", g))
                wait_freed(po, ("u", g))
                po.tensor_tensor(ug[:, g, :], ug[:, g, :], mixed[:, g % 2, :], ALU.mult).then_inc(
                    S["ya_ready"], 1)
            wait_full(po, ("mix", NG - 1))
            po.dma_start(rope_cs2[:, :, :], rope2).then_inc(S["rope_in"], 16)
            po.wait_ge(S["rope_in"], 32)
            po.wait_ge(S["ya_ready"], NG)
            for i in range(8):
                rope_cosines("q2", i, 8 + i, rope_cs2, raw2, rcos2)
            for i in range(2):
                rope_cosines("k2", i, 16 + i, rope_cs2, raw2, rcos2)
            add_parts("m2")
            wait_full(po, ("ht", TT - 1, 1))
            po.wait_ge(S["aff_ready"], 1)
            for t in range(2):
                po.wait_ge(S["sel_ready"], t + 1)
                po.tensor_tensor(wsel[:, t, :].rearrange("p (e j) -> p e j", e=NE),
                                 sel[:, t, :].rearrange("p (e j) -> p e j", e=NE),
                                 aff[:, t, :].unsqueeze(2).broadcast_to([P, NE, CAP]), ALU.mult).then_inc(
                                     S["wsel_half"], 1)


def rope_table(angles, sign_rows):
    return np.stack([np.cos(angles), np.sin(angles)], 1)


def shape_constants():
    f = np.float32
    c = np.zeros((P, NCONST), f)

    def put(name, v):
        a, b = CONST[name]
        c[:, a:b] = v

    p, n = np.arange(P)[:, None], np.arange(P)[None, :]
    put("ident", p == n)

    def swap(half):
        m = np.zeros((P, P), f)
        for i in range(P):
            if i % (2 * half) < half:
                m[i + half, i] = -1.0
            else:
                m[i - half, i] = 1.0
        return m

    put("swap1", swap(32))
    put("swap2", swap(16))
    mask = np.zeros((P, 2, P), f)
    mask[:, 0] = np.where(n >= p, 0.0, -1e30)
    mask[:, 1] = np.where(n <= p, 0.0, -1e30)
    put("mask", mask.reshape(P, 2 * P))
    put("iota", np.arange(CAP)[None, :])
    put("age", np.concatenate([LC - 1 - p, LC - 1 - P - p, p, P + p], 1))
    sel = np.zeros((P, 2), f)
    for g in range(4):
        sel[32 * g, 0] = sel[32 * g + 1, 1] = 1.0
    put("modsel", sel)
    put("routesel", np.tile(np.eye(32, NE, dtype=f), (4, 1)))

    t = np.arange(L)
    row, col = (t // 64).astype(f), (t % 64).astype(f)
    inv = (f(10000.0) ** (-np.arange(16, dtype=f) / f(16))).astype(f)
    a1 = np.concatenate([row[None] * inv[:, None], col[None] * inv[:, None]], 0)
    a1 = np.tile(a1, (4, 1)).astype(np.float64)
    a2 = np.concatenate([np.tile(row[None] * inv[:, None], (2, 1)), np.tile(col[None] * inv[:, None], (2, 1))], 0)
    a2 = np.tile(a2, (2, 1)).astype(np.float64)
    r1, r2 = rope_table(a1, 32).astype(f), rope_table(a2, 16).astype(f)

    k = np.arange(L)
    w = 2 * np.pi * ((k[:, None] * k[None, :]) % L) / L
    s = 1.0 / np.sqrt(L * 128.0)
    dl = np.stack([np.cos(w), np.sin(w)], 0) * s
    dl = dl.reshape(2, TT, P, L).transpose(2, 0, 1, 3)
    wd = 2 * np.pi * ((p * n) % P) / P
    dd = np.stack([np.cos(wd), -np.sin(wd)], 1)
    dist = np.concatenate([np.arange(896)[None, :] - 384 - p, np.tile(np.arange(1, L + 1), (P, 1))], 1)
    return dict(consts=c, rope1=r1, rope2=r2,
                dft_len=np.ascontiguousarray(dl.reshape(P, 4, 1024)).astype(f),
                dft_dim=dd.astype(f), dist=dist.astype(f))


_INS = ["x", "c", "ctx", "c_ctx", "w_mod", "b_mod", "norm1_w", "w_in", "ret_decay_f", "ret_decay_b",
        "w_ret_out", "w_four_out", "w_branch_gate", "b_branch_gate", "w_out", "norm2_w", "w_up",
        "conv_w", "conv_b", "w_down", "final_norm_w", "c_2", "ctx_2", "c_ctx_2", "w_ada_2", "b_ada_2",
        "norm1_g_2", "w_in_2", "b_merge_gate_2", "gmlp_ln_g_2", "gmlp_ln_b_2", "w_spatial_2",
        "b_spatial_2", "attn_sink_2", "w_proj_a_2", "w_proj_b_2", "w_out_2", "norm2_g_2", "w_router_2",
        "w_exp_gate_2", "w_exp_up_2", "w_exp_down_2", "final_g_2"]


def kernel(**inputs):
    import concourse.bacc as bacc
    from concourse.bass_utils import run_bass_kernel_spmd

    nc = bacc.Bacc("TRN2", target_bir_lowering=False, num_devices=1)
    arrays, args = {}, []
    tensors = {n: np.ascontiguousarray(inputs[n]) for n in _INS} | shape_constants()
    for name, a in tensors.items():
        arrays[f"in_{name}"] = a
        args.append(nc.dram_tensor(f"in_{name}", a.shape, mybir.dt.from_np(a.dtype), kind="ExternalInput").ap())
    out = nc.dram_tensor("out_0", (1, L, D), F32, kind="ExternalOutput").ap()
    build_two_blocks(nc, *args, out)
    r = run_bass_kernel_spmd(nc, [arrays], core_ids=[0])
    return r.results[0]["out_0"]
```
